# Optimizing a Trainium2 kernel written in Bass

```python
import jax, jax.numpy as jnp
from jax import lax
import numpy as np
import math

D_MODEL = 1024
BATCH = 1
SEQ = 512
DEPTH = 2

DN_HEADS = 8
DN_DK = 128
DN_DV = 128
DN_CONV = 4
DN_CHUNK = 64
SW_Q_HEADS = 16
SW_KV_HEADS = 2
SW_HEAD_DIM = 64
SW_WINDOW = 128
SW_BLOCK = 128
ROPE_THETA = 500000.0
ROT_DIM = SW_HEAD_DIM // 4
D_FF = 4 * D_MODEL
EPS = 1e-6

DN_QK_W = DN_HEADS * DN_DK
DN_V_W = DN_HEADS * DN_DV
SW_Q_W = SW_Q_HEADS * SW_HEAD_DIM
SW_KV_W = SW_KV_HEADS * SW_HEAD_DIM
IN_SPLITS = [DN_QK_W, DN_QK_W, DN_V_W, DN_V_W, DN_HEADS, DN_HEADS,
             SW_Q_W, SW_KV_W, SW_KV_W, D_MODEL, D_MODEL]
D_IN = sum(IN_SPLITS)
IN_OFFSETS = np.cumsum(IN_SPLITS)[:-1].tolist()


def rmsnorm(x, g):
    xf = x.astype(jnp.float32)
    y = xf * lax.rsqrt(jnp.mean(xf * xf, axis=-1, keepdims=True) + EPS)
    return (y * g.astype(jnp.float32)).astype(x.dtype)

def l2norm(t):
    tf = t.astype(jnp.float32)
    return tf * lax.rsqrt(jnp.sum(tf * tf, axis=-1, keepdims=True) + EPS)

def causal_conv_silu(x, w):
    S = x.shape[1]
    K = w.shape[0]
    xp = jnp.pad(x, ((0, 0), (K - 1, 0), (0, 0)))
    y = sum(xp[:, j:j + S] * w[j] for j in range(K))
    return jax.nn.silu(y)

def gated_delta_rule(q, k, v, g, beta):
    B, S, H, dk = q.shape
    dv = v.shape[-1]
    C = DN_CHUNK
    N = S // C

    def chunks(t):
        return t.reshape(B, N, C, H, -1).transpose(0, 3, 1, 2, 4)

    q, k, v = chunks(q), chunks(k), chunks(v)
    g = g.reshape(B, N, C, H).transpose(0, 3, 1, 2)
    beta = beta.reshape(B, N, C, H).transpose(0, 3, 1, 2)
    g = jnp.cumsum(g, axis=-1)

    idx = jnp.arange(C)
    causal = idx[:, None] >= idx[None, :]
    strict = idx[:, None] > idx[None, :]
    diff = g[..., :, None] - g[..., None, :]
    decay = jnp.where(causal, jnp.exp(jnp.where(causal, diff, 0.0)), 0.0)

    kb = k * beta[..., None]
    L = jnp.where(strict, jnp.einsum('bhnid,bhnjd->bhnij', kb, k) * decay, 0.0)
    u = lax.linalg.triangular_solve(L, v * beta[..., None], left_side=True,
                                    lower=True, unit_diagonal=True)
    w = lax.linalg.triangular_solve(L, kb * jnp.exp(g)[..., None], left_side=True,
                                    lower=True, unit_diagonal=True)
    a_intra = jnp.einsum('bhnid,bhnjd->bhnij', q, k) * decay
    q_dec = q * jnp.exp(g)[..., None]
    g_last = g[..., -1]
    k_dec = k * jnp.exp(g_last[..., None] - g)[..., None]

    def to_front(t):
        return jnp.moveaxis(t, 2, 0)

    xs = (to_front(q_dec), to_front(k_dec), to_front(u), to_front(w),
          to_front(a_intra), jnp.moveaxis(g_last, 2, 0))

    def step(state, inp):
        qd, kd, u_c, w_c, a_c, gl = inp
        v_new = u_c - jnp.einsum('bhcd,bhde->bhce', w_c, state)
        o = (jnp.einsum('bhcd,bhde->bhce', qd, state)
             + jnp.einsum('bhij,bhje->bhie', a_c, v_new))
        state = state * jnp.exp(gl)[..., None, None] + jnp.einsum('bhcd,bhce->bhde', kd, v_new)
        return state, o

    state0 = jnp.zeros((B, H, dk, dv), jnp.float32)
    _, o = lax.scan(step, state0, xs)
    return o.transpose(1, 0, 3, 2, 4).reshape(B, S, H, dv)

def deltanet_branch(q_in, k_in, v_in, z, b_in, a_in, conv_w, a_log, dt_bias, norm_g):
    B, S, _ = q_in.shape
    qkv = causal_conv_silu(jnp.concatenate([q_in, k_in, v_in], axis=-1), conv_w)
    q, k, v = jnp.split(qkv, [DN_QK_W, 2 * DN_QK_W], axis=-1)
    q = l2norm(q.reshape(B, S, DN_HEADS, DN_DK)) * (DN_DK ** -0.5)
    k = l2norm(k.reshape(B, S, DN_HEADS, DN_DK))
    v = v.reshape(B, S, DN_HEADS, DN_DV).astype(jnp.float32)
    beta = jax.nn.sigmoid(b_in.astype(jnp.float32))
    g = -jnp.exp(a_log.astype(jnp.float32)) * jax.nn.softplus(
        a_in.astype(jnp.float32) + dt_bias.astype(jnp.float32))
    o = gated_delta_rule(q, k, v, g, beta)
    o = rmsnorm(o, norm_g) * jax.nn.silu(z.reshape(B, S, DN_HEADS, DN_DV).astype(jnp.float32))
    return o.reshape(B, S, DN_V_W).astype(q_in.dtype)

def partial_rope(x, positions):
    half = ROT_DIM // 2
    inv_freq = ROPE_THETA ** (-jnp.arange(half, dtype=jnp.float32) * (2.0 / ROT_DIM))
    ang = positions.astype(jnp.float32)[..., None] * inv_freq
    cos = jnp.cos(ang)[:, :, None, :]
    sin = jnp.sin(ang)[:, :, None, :]
    xr = x[..., :ROT_DIM].astype(jnp.float32)
    x1, x2 = xr[..., :half], xr[..., half:]
    rot = jnp.concatenate([x1 * cos - x2 * sin, x2 * cos + x1 * sin], axis=-1)
    return jnp.concatenate([rot.astype(x.dtype), x[..., ROT_DIM:]], axis=-1)

def swa_sink_branch(q_in, k_in, v_in, positions, sinks):
    B, S, _ = q_in.shape
    G = SW_Q_HEADS // SW_KV_HEADS
    nb = S // SW_BLOCK
    q = partial_rope(q_in.reshape(B, S, SW_Q_HEADS, SW_HEAD_DIM), positions)
    k = partial_rope(k_in.reshape(B, S, SW_KV_HEADS, SW_HEAD_DIM), positions)
    v = v_in.reshape(B, S, SW_KV_HEADS, SW_HEAD_DIM)

    qb = q.reshape(B, nb, SW_BLOCK, SW_KV_HEADS, G, SW_HEAD_DIM).astype(jnp.float32)

    def band(t):
        tp = jnp.pad(t, ((0, 0), (SW_BLOCK, 0), (0, 0), (0, 0)))
        tb = tp.reshape(B, nb + 1, SW_BLOCK, SW_KV_HEADS, SW_HEAD_DIM)
        return jnp.concatenate([tb[:, :-1], tb[:, 1:]], axis=2)

    kw = band(k).astype(jnp.float32)
    vw = band(v)
    scores = jnp.einsum('bnqhgd,bnkhd->bnhgqk', qb, kw) * (SW_HEAD_DIM ** -0.5)

    qi = jnp.arange(SW_BLOCK)[:, None] + SW_BLOCK
    ki = jnp.arange(2 * SW_BLOCK)[None, :]
    off = qi - ki
    in_band = (off >= 0) & (off < SW_WINDOW)
    blk = jnp.arange(nb)[:, None, None]
    valid = (blk * SW_BLOCK + ki[None] - SW_BLOCK) >= 0
    mask = (in_band[None] & valid)[None, :, None, None]
    scores = jnp.where(mask, scores, -jnp.inf)

    sink = sinks.astype(jnp.float32).reshape(SW_KV_HEADS, G)[None, None, :, :, None, None]
    m = jnp.maximum(jnp.max(scores, axis=-1, keepdims=True), sink)
    p = jnp.exp(scores - m)
    probs = p / (jnp.sum(p, axis=-1, keepdims=True) + jnp.exp(sink - m))
    o = jnp.einsum('bnhgqk,bnkhd->bnqhgd', probs.astype(vw.dtype), vw)
    return o.reshape(B, S, SW_Q_W)

def hybrid_layer(x, positions, pre_mix_g, w_in, dn_conv_w, dn_a_log, dn_dt_bias, dn_norm_g,
                 sw_sinks, w_up_dn, w_up_sw, w_o, post_mix_g, pre_mlp_g, w_ff1, w_ff2,
                 post_mlp_g):
    h = rmsnorm(x, pre_mix_g)
    proj = h @ w_in
    (dn_q, dn_k, dn_v, dn_z, dn_b, dn_a, sw_q, sw_k, sw_v,
     gate_a, gate_b) = jnp.split(proj, IN_OFFSETS, axis=-1)
    y_a = deltanet_branch(dn_q, dn_k, dn_v, dn_z, dn_b, dn_a, dn_conv_w, dn_a_log,
                          dn_dt_bias, dn_norm_g) @ w_up_dn
    y_b = swa_sink_branch(sw_q, sw_k, sw_v, positions, sw_sinks) @ w_up_sw
    mix = (jax.nn.sigmoid(gate_a) * y_a + jax.nn.sigmoid(gate_b) * y_b) @ w_o
    x = x + rmsnorm(mix, post_mix_g)

    h2 = rmsnorm(x, pre_mlp_g)
    ff = jnp.square(jax.nn.relu(h2 @ w_ff1)) @ w_ff2
    return x + rmsnorm(ff, post_mlp_g)

def first_inputs(seed: int = 0) -> dict:
    key = jax.random.key(seed)
    ks = jax.random.split(key, 20)
    f32 = jnp.float32

    def nrm(k, shape, scale):
        return jax.random.normal(k, shape, f32) * scale

    def gain(k, shape):
        return 1.0 + 0.02 * jax.random.normal(k, shape, f32)

    x = jax.random.normal(ks[0], (BATCH, SEQ, D_MODEL), f32)
    positions = jnp.broadcast_to(jnp.arange(SEQ, dtype=jnp.int32), (BATCH, SEQ))
    dt = jnp.exp(jax.random.uniform(ks[5], (DEPTH, DN_HEADS), f32,
                                    np.log(1e-3), np.log(1e-1)))
    return {
        'x': x,
        'positions': positions,
        'pre_mix_g': gain(ks[1], (DEPTH, D_MODEL)),
        'w_in': nrm(ks[2], (DEPTH, D_MODEL, D_IN), D_MODEL ** -0.5),
        'dn_conv_w': nrm(ks[3], (DEPTH, DN_CONV, 2 * DN_QK_W + DN_V_W), DN_CONV ** -0.5),
        'dn_a_log': jnp.log(jax.random.uniform(ks[4], (DEPTH, DN_HEADS), f32, 1.0, 16.0)),
        'dn_dt_bias': dt + jnp.log(-jnp.expm1(-dt)),
        'dn_norm_g': gain(ks[6], (DEPTH, DN_DV)),
        'sw_sinks': nrm(ks[7], (DEPTH, SW_Q_HEADS), 0.5),
        'w_up_dn': nrm(ks[8], (DEPTH, DN_V_W, D_MODEL), DN_V_W ** -0.5),
        'w_up_sw': nrm(ks[9], (DEPTH, SW_Q_W, D_MODEL), SW_Q_W ** -0.5),
        'w_o': nrm(ks[10], (DEPTH, D_MODEL, D_MODEL), D_MODEL ** -0.5),
        'post_mix_g': gain(ks[11], (DEPTH, D_MODEL)),
        'pre_mlp_g': gain(ks[12], (DEPTH, D_MODEL)),
        'w_ff1': nrm(ks[13], (DEPTH, D_MODEL, D_FF), D_MODEL ** -0.5),
        'w_ff2': nrm(ks[14], (DEPTH, D_FF, D_MODEL), D_FF ** -0.5),
        'post_mlp_g': gain(ks[15], (DEPTH, D_MODEL)),
    }

def first_block(x, positions, pre_mix_g, w_in, dn_conv_w, dn_a_log, dn_dt_bias, dn_norm_g,
              sw_sinks, w_up_dn, w_up_sw, w_o, post_mix_g, pre_mlp_g, w_ff1, w_ff2,
              post_mlp_g):
    for l in range(DEPTH):
        x = hybrid_layer(x, positions, pre_mix_g[l], w_in[l], dn_conv_w[l], dn_a_log[l],
                         dn_dt_bias[l], dn_norm_g[l], sw_sinks[l], w_up_dn[l], w_up_sw[l],
                         w_o[l], post_mix_g[l], pre_mlp_g[l], w_ff1[l], w_ff2[l],
                         post_mlp_g[l])
    return x


DEPTH_2 = 1

SSM_WIDTH = D_MODEL // 2
SSM_GROUP_SIZE = 16
SSM_GROUPS = SSM_WIDTH // SSM_GROUP_SIZE
SSM_STATE = 64
DT_MIN = 1e-3
DT_MAX = 1e-1
POOL_WIDTH = D_MODEL // 2
POOL_WINDOWS = (2, 4, 8, 16)
POOL_GROUPS = len(POOL_WINDOWS)
POOL_GROUP = POOL_WIDTH // POOL_GROUPS
N_IN = 2 * SSM_WIDTH + 2 * POOL_WIDTH + 2 * D_MODEL
SPLITS = (SSM_WIDTH, 2 * SSM_WIDTH, 2 * SSM_WIDTH + POOL_WIDTH,
          2 * SSM_WIDTH + 2 * POOL_WIDTH, 2 * SSM_WIDTH + 2 * POOL_WIDTH + D_MODEL)


def _rmsnorm(x, g):
    x32 = x.astype(jnp.float32)
    y = x32 * lax.rsqrt(jnp.mean(x32 * x32, axis=-1, keepdims=True) + EPS)
    return y.astype(x.dtype) * g

def _complex_linear_combine(left, right):
    a1r, a1i, b1r, b1i = left
    a2r, a2i, b2r, b2i = right
    ar = a2r * a1r - a2i * a1i
    ai = a2r * a1i + a2i * a1r
    br = a2r * b1r - a2i * b1i + b2r
    bi = a2r * b1i + a2i * b1r + b2i
    return ar, ai, br, bi

def _s5_branch(u, log_dt, lam_re, lam_im, b_re, b_im, c_re, c_im, d_skip, w_glu, b_glu):
    bsz, seq, _ = u.shape
    ug = u.reshape(bsz, seq, SSM_GROUPS, SSM_GROUP_SIZE)
    dt = jnp.exp(log_dt)[:, None]
    mag = jnp.exp(lam_re * dt)
    ang = lam_im * dt
    abar_re = mag * jnp.cos(ang)
    abar_im = mag * jnp.sin(ang)
    num_re = abar_re - 1.0
    num_im = abar_im
    den = lam_re * lam_re + lam_im * lam_im
    coef_re = (num_re * lam_re + num_im * lam_im) / den
    coef_im = (num_im * lam_re - num_re * lam_im) / den
    bbar_re = coef_re[..., None] * b_re - coef_im[..., None] * b_im
    bbar_im = coef_re[..., None] * b_im + coef_im[..., None] * b_re
    bu_re = jnp.einsum('blgc,gpc->blgp', ug, bbar_re)
    bu_im = jnp.einsum('blgc,gpc->blgp', ug, bbar_im)
    a_re = jnp.broadcast_to(abar_re, bu_re.shape)
    a_im = jnp.broadcast_to(abar_im, bu_im.shape)
    _, _, s_re, s_im = lax.associative_scan(_complex_linear_combine,
                                            (a_re, a_im, bu_re, bu_im), axis=1)
    y = (jnp.einsum('blgp,gcp->blgc', s_re, c_re)
         - jnp.einsum('blgp,gcp->blgc', s_im, c_im))
    y = y.reshape(bsz, seq, SSM_WIDTH) + d_skip * u
    y = jax.nn.gelu(y)
    return y * jax.nn.sigmoid(y @ w_glu + b_glu)

def _pool_branch(u, w_group, scale):
    bsz, seq, _ = u.shape
    u32 = u.astype(jnp.float32)
    cs = jnp.cumsum(u32, axis=1)
    pos = jnp.arange(seq)
    outs = []
    for gi, win in enumerate(POOL_WINDOWS):
        csg = cs[:, :, gi * POOL_GROUP:(gi + 1) * POOL_GROUP]
        shifted = jnp.pad(csg, ((0, 0), (win, 0), (0, 0)))[:, :seq]
        count = jnp.minimum(pos + 1, win).astype(jnp.float32)[None, :, None]
        mean = (csg - shifted) / count
        outs.append(mean - u32[:, :, gi * POOL_GROUP:(gi + 1) * POOL_GROUP])
    pooled = jnp.stack(outs, axis=2).astype(u.dtype)
    mixed = jnp.einsum('blgc,gcd->blgd', pooled, w_group).reshape(bsz, seq, POOL_WIDTH)
    return mixed * scale

def second_inputs(seed: int = 0) -> dict:
    key = jax.random.key(seed)
    ks = jax.random.split(key, 24)
    f32 = jnp.float32
    nrm = lambda k, shape, std: (jax.random.normal(k, shape, f32) * std)
    x = jax.random.normal(ks[0], (BATCH, SEQ, D_MODEL), f32)
    norm_g = 1.0 + nrm(ks[1], (DEPTH_2, D_MODEL), 0.05)
    w_in = nrm(ks[2], (DEPTH_2, D_MODEL, N_IN), D_MODEL ** -0.5)
    b_in = nrm(ks[3], (DEPTH_2, N_IN), 0.02)
    ssm_log_dt = jax.random.uniform(ks[4], (DEPTH_2, SSM_GROUPS), f32,
                                    math.log(DT_MIN), math.log(DT_MAX))
    n_idx = jnp.arange(SSM_STATE, dtype=f32)
    ssm_lam_re = -0.5 + nrm(ks[5], (DEPTH_2, SSM_GROUPS, SSM_STATE), 0.01)
    ssm_lam_im = math.pi * n_idx[None, None, :] + nrm(ks[6], (DEPTH_2, SSM_GROUPS, SSM_STATE), 0.01)
    b_std = (2.0 * SSM_GROUP_SIZE) ** -0.5
    ssm_b_re = nrm(ks[7], (DEPTH_2, SSM_GROUPS, SSM_STATE, SSM_GROUP_SIZE), b_std)
    ssm_b_im = nrm(ks[8], (DEPTH_2, SSM_GROUPS, SSM_STATE, SSM_GROUP_SIZE), b_std)
    c_std = SSM_STATE ** -0.5
    ssm_c_re = nrm(ks[9], (DEPTH_2, SSM_GROUPS, SSM_GROUP_SIZE, SSM_STATE), c_std)
    ssm_c_im = nrm(ks[10], (DEPTH_2, SSM_GROUPS, SSM_GROUP_SIZE, SSM_STATE), c_std)
    ssm_d = nrm(ks[11], (DEPTH_2, SSM_WIDTH), 1.0)
    ssm_w_glu = nrm(ks[12], (DEPTH_2, SSM_WIDTH, SSM_WIDTH), SSM_WIDTH ** -0.5)
    ssm_b_glu = nrm(ks[13], (DEPTH_2, SSM_WIDTH), 0.02)
    pool_w = nrm(ks[14], (DEPTH_2, POOL_GROUPS, POOL_GROUP, POOL_GROUP), POOL_GROUP ** -0.5)
    pool_scale = 1.0 + nrm(ks[15], (DEPTH_2, POOL_WIDTH), 0.1)
    w_branch_a = nrm(ks[16], (DEPTH_2, SSM_WIDTH, D_MODEL), SSM_WIDTH ** -0.5)
    w_branch_b = nrm(ks[17], (DEPTH_2, POOL_WIDTH, D_MODEL), POOL_WIDTH ** -0.5)
    w_out = nrm(ks[18], (DEPTH_2, D_MODEL, D_MODEL), D_MODEL ** -0.5)
    final_norm_g = 1.0 + nrm(ks[19], (D_MODEL,), 0.05)
    return {"x": x, "norm_g": norm_g, "w_in": w_in, "b_in": b_in,
            "ssm_log_dt": ssm_log_dt, "ssm_lam_re": ssm_lam_re, "ssm_lam_im": ssm_lam_im,
            "ssm_b_re": ssm_b_re, "ssm_b_im": ssm_b_im, "ssm_c_re": ssm_c_re, "ssm_c_im": ssm_c_im,
            "ssm_d": ssm_d, "ssm_w_glu": ssm_w_glu, "ssm_b_glu": ssm_b_glu,
            "pool_w": pool_w, "pool_scale": pool_scale,
            "w_branch_a": w_branch_a, "w_branch_b": w_branch_b, "w_out": w_out,
            "final_norm_g": final_norm_g}

def second_block(x, norm_g, w_in, b_in, ssm_log_dt, ssm_lam_re, ssm_lam_im, ssm_b_re, ssm_b_im,
              ssm_c_re, ssm_c_im, ssm_d, ssm_w_glu, ssm_b_glu, pool_w, pool_scale,
              w_branch_a, w_branch_b, w_out, final_norm_g):
    for l in range(DEPTH_2):
        h = _rmsnorm(x, norm_g[l])
        proj = h @ w_in[l] + b_in[l]
        ua, za, ub, zb, ga, gb = jnp.split(proj, SPLITS, axis=-1)
        ya = _s5_branch(ua, ssm_log_dt[l], ssm_lam_re[l], ssm_lam_im[l], ssm_b_re[l], ssm_b_im[l],
                        ssm_c_re[l], ssm_c_im[l], ssm_d[l], ssm_w_glu[l], ssm_b_glu[l])
        ya = ya * jax.nn.silu(za)
        yb = _pool_branch(ub, pool_w[l], pool_scale[l]) * jax.nn.silu(zb)
        merged = (jax.nn.sigmoid(ga) * (ya @ w_branch_a[l])
                  + jax.nn.sigmoid(gb) * (yb @ w_branch_b[l]))
        x = x + merged @ w_out[l]
    return _rmsnorm(x, final_norm_g)


def setup_inputs(seed=0):
    out = dict(first_inputs(seed))
    for name, value in second_inputs(seed + 1).items():
        if name != "x":
            out[name + "_2"] = value
    return out


def reference(
    x, positions, pre_mix_g, w_in, dn_conv_w, dn_a_log, dn_dt_bias, dn_norm_g, sw_sinks,
    w_up_dn, w_up_sw, w_o, post_mix_g, pre_mlp_g, w_ff1, w_ff2, post_mlp_g, norm_g_2, w_in_2,
    b_in_2, ssm_log_dt_2, ssm_lam_re_2, ssm_lam_im_2, ssm_b_re_2, ssm_b_im_2, ssm_c_re_2,
    ssm_c_im_2, ssm_d_2, ssm_w_glu_2, ssm_b_glu_2, pool_w_2, pool_scale_2, w_branch_a_2,
    w_branch_b_2, w_out_2, final_norm_g_2,
):
    x = first_block(
        x, positions, pre_mix_g, w_in, dn_conv_w, dn_a_log, dn_dt_bias, dn_norm_g, sw_sinks,
        w_up_dn, w_up_sw, w_o, post_mix_g, pre_mlp_g, w_ff1, w_ff2, post_mlp_g,
    )
    return second_block(
        x, norm_g_2, w_in_2, b_in_2, ssm_log_dt_2, ssm_lam_re_2, ssm_lam_im_2, ssm_b_re_2,
        ssm_b_im_2, ssm_c_re_2, ssm_c_im_2, ssm_d_2, ssm_w_glu_2, ssm_b_glu_2, pool_w_2,
        pool_scale_2, w_branch_a_2, w_branch_b_2, w_out_2, final_norm_g_2,
    )


_drawn_inputs = setup_inputs


def setup_inputs(seed=0):
    import zlib

    import numpy as np

    out = dict(_drawn_inputs(seed))
    spreads = {}
    factors = {'sw_sinks': 4.644,
     'post_mix_g': 2.685,
     'pre_mlp_g': 2.931,
     'post_mlp_g': 3.112,
     'norm_g_2': 5.675,
     'b_in_2': 8.0,
     'ssm_log_dt_2': 64.0,
     'ssm_lam_re_2': 64.0,
     'ssm_lam_im_2': 64.0,
     'ssm_b_re_2': 64.0,
     'ssm_b_im_2': 64.0,
     'ssm_c_re_2': 64.0,
     'ssm_c_im_2': 64.0,
     'ssm_w_glu_2': 3.122,
     'ssm_b_glu_2': 188.505,
     'pool_scale_2': 4.667}
    for name, (base, spread) in spreads.items():
        noise = np.random.default_rng([zlib.crc32(name.encode()), seed]).standard_normal(out[name].shape)
        drawn = base * np.exp(spread * noise) if base else spread * noise
        out[name] = __import__('jax').numpy.asarray(drawn.astype(out[name].dtype))
    for name, factor in factors.items():
        out[name] = (out[name] * factor).astype(out[name].dtype)
    return out
```

```python
from contextlib import ExitStack

import numpy as np
import concourse.bass as bass
from concourse import mybir

F32 = mybir.dt.float32
F32R = mybir.dt.float32r
I32 = mybir.dt.int32
ALU = mybir.AluOpType
ACT = mybir.ActivationFunctionType
AX = mybir.AxisListType

P = 128
SEQ, D_MODEL, DEPTH, D_FF = 512, 1024, 2, 4096
KT = D_MODEL // P
HEADS, CONV = 8, 4
CH = SEQ // P
SWQ = 8
HD = 64
FFC = D_FF // D_MODEL
EPS = 1e-6
NEG = -1e30
LEVELS = (2, 4, 8, 16, 32, 64)
SG = 4
ST = 16
TBL = 32
TBH = SEQ // TBL
PARTS = 8

def layer_tiles():
    out = [("ab", 0)]
    for h in range(HEADS):
        out += [("q", h), ("k", h), ("v", h), ("z", h)]
    out += [("swk", 0), ("swv", 0)] + [("swq", t) for t in range(SWQ)]
    for f in range(KT):
        out += [("ga", f), ("ya", f)]
    for f in range(KT):
        out += [("gb", f), ("yb", f)]
    out += [("wo", f) for f in range(KT)]
    up = lambda c: [("f1", 8 * c + j) for j in range(8)]
    down = lambda c: [("f2", 8 * c + j) for j in range(8)]
    out += up(0)
    for c in range(1, FFC):
        out += up(c) + down(c - 1)
    return out + down(FFC - 1)


def second_tiles():
    out = [("ua", i) for i in range(SG)] + [("za", i) for i in range(SG)]
    out += [("ub", i) for i in range(SG)] + [("zb", i) for i in range(SG)] + [("pw", 0)]
    out += [("gb", f) for f in range(KT)] + [("bb", i) for i in range(KT // 2)]
    out += [("ga", f) for f in range(KT - 1)] + [("glu", i) for i in range(SG // 2)] + [("ga", KT - 1)]
    return out + [("ba", i) for i in range(KT // 2)] + [("wo", f) for f in range(KT)]


OUTS = {"pw": SG, "bb": 2, "glu": 2, "ba": 2}
S_DEPTH = {"pw": 1, "bb": SG, "glu": SG, "ba": SG}


def outputs_of(tile):
    kind, i = tile
    n = OUTS.get(kind, 1)
    return [(kind, n * i + o) for o in range(n)]


LT_TILES = layer_tiles()
L_AT = {t: i for i, t in enumerate(LT_TILES)}
S_TILES = second_tiles()
S_AT = {t: i for i, t in enumerate(S_TILES)}

CONST = {}
_at = 0
for _name, _n in [("ident", P), ("ones", P), ("upper", P), ("first", P), ("levels", P * len(LEVELS)), ("rot", P),
                  ("dup0", P), ("dup1", P), ("window", 2 * P), ("invfreq", 1), ("isrot", 1), ("notrot", 1),
                  ("eps", 1), ("eps4", 1), ("halfpi", 1), ("invcount", 16)]:
    CONST[_name] = (_at, _at + _n)
    _at += _n
NCONST = _at

PARAM = {}
_at = 0
for _name, _n in [("pre_mix", KT), ("post_mix", KT), ("pre_mlp", KT), ("post_mlp", KT), ("conv", CONV * 3 * HEADS),
                  ("norm", 1), ("a_log", HEADS), ("dt_bias", HEADS), ("sinks", 2 * SWQ)]:
    PARAM[_name] = (_at, _at + _n)
    _at += _n
NPARAM = _at


PARAM2 = {}
_at = 0
for _name, _n in [("norm", KT), ("final", KT), ("b_in", D_MODEL * 4 // P), ("d", SG), ("b_glu", SG), ("pool_scale", SG),
                  ("lam_re", ST), ("lam_im", ST), ("log_dt", ST)]:
    PARAM2[_name] = (_at, _at + _n)
    _at += _n
NPARAM2 = _at
IN2 = {"ua": 0, "za": SG, "ub": 2 * SG, "zb": 3 * SG, "ga": 4 * SG, "gb": 4 * SG + KT}


def constants():
    c = np.zeros((P, NCONST), np.float32)
    i, j = np.arange(P)[:, None], np.arange(P)[None, :]

    def put(name, v):
        c[:, CONST[name][0]:CONST[name][1]] = v

    put("ident", i == j)
    put("ones", 1.0)
    put("upper", i <= j)
    put("first", (i % 2 == 0) & (j == i + 1))
    put("levels", np.concatenate([(i // (2 * s) == j // (2 * s)) & (i % (2 * s) >= s) & (j % (2 * s) < s)
                                  for s in LEVELS], axis=1))
    r = i % HD
    half = HD // 8
    rj = j % HD
    put("rot", -1.0 * ((rj < half) & (i == j + half)) + 1.0 * ((rj >= half) & (rj < 2 * half) & (i == j - half)))
    put("dup0", i == j % HD)
    put("dup1", i == j % HD + HD)
    q, k = np.arange(P)[:, None] + P, np.arange(2 * P)[None, :]
    put("window", np.where((q - k >= 0) & (q - k < P), 0.0, NEG))
    p = np.arange(P)[:, None]
    inv = np.float32(500000.0) ** (-(p % half).astype(np.float32) * np.float32(2.0 / (2 * half)))
    put("invfreq", np.where(p % HD < 2 * half, inv, 0.0))
    put("isrot", p % HD < 2 * half)
    put("notrot", p % HD >= 2 * half)
    put("eps", EPS)
    put("eps4", 4 * EPS)
    put("halfpi", np.pi / 2)
    put("invcount", 1.0 / np.arange(1, 17)[None, :])
    return c


class Count:

    def __init__(self, rounds):
        self.value = {}
        n = 0
        for key, stages in rounds:
            for s in stages:
                self.value[key, s] = n
                n += 1
            self.value[key, "end"] = n

    def before(self, key, stage):
        return self.value[key, stage]

    def end(self, key):
        return self.value[key, "end"]


E_STAGES = {
    "ab": ["scale"],
    "q": ["scale", "tap3", "tap2", "tap1", "tap0", "tanh", "silu"],
    "z": ["scale", "tanh", "silu"],
    "swk": ["scale", "cosk", "rotk", "sink", "addk", "dupk", "copyk"],
    "swv": ["scale", "turnv", "copyv"],
    "swq": ["scale"],
    "ga": ["scale", "tanh"],
    "ya": ["gate"],
    "yb": ["gate", "add", "high", "low"],
    "wo": ["copy", "square", "sum"],
    "f1": ["scale", "relu2", "high", "low"],
}
E_STAGES["k"] = E_STAGES["v"] = E_STAGES["q"]
E_STAGES["gb"] = E_STAGES["ga"]


def e_stages(tile):
    kind, i = tile
    if kind == "f2":
        return (["copy"] if i < 8 else ["add"]) + (["square", "sum"] if i >= 8 * (FFC - 1) else [])
    return E_STAGES[kind]


G_STAGES = ["turn", "copy", "tanh", "beta", "hbeta", "addb", "max", "abs", "expn", "plus1", "ln", "sp", "expa", "g",
            "cumsum", "copyc", "diff", "exps", "nbeg"]
A_STAGES = (["sqk", "sumk", "rootk", "recipk", "normk", "sqq", "sumq", "rootq", "recipq", "normq",
             "rows", "kbeta", "diff", "exps", "qdec", "gram", "mask", "masked", "first", "minus", "turni", "copyi"]
            + [f"{s}{v}" for v in range(len(LEVELS))
               for s in (["p", "pmask", "q", "update"] + (["turn", "copy"] if v < len(LEVELS) - 1 else []))]
            + ["turnkv", "copykv"])
B_STAGES = (["v0", "copyv0", "o0", "state0"]
            + [f"{s}{c}" for c in range(1, CH)
               for s in (["r", "rr", "v", "copyv", "o"] + (["state"] if c < CH - 1 else []))]
            + ["square", "sum", "root", "recip", "norm", "gate", "high", "low"])
C_STAGES = (["rot", "cos", "sin", "addq"]
            + [f"{s}{e}" for e in range(2)
               for s in ("score", "mask", "max", "maxs", "neg", "exp", "den", "recip", "prob", "turn", "copy", "pv")]
            + ["high", "low"])

E = Count([(t, e_stages(t)) for t in LT_TILES])
G = Count([(0, G_STAGES)])
A = Count([(h, A_STAGES) for h in range(HEADS)])
B = Count([(h, B_STAGES) for h in range(HEADS)])
C = Count([(t, C_STAGES) for t in range(SWQ)])


def layer_order():
    out = []

    def tile(j, beside=(), reads_last=False):
        t = LT_TILES[j]
        behind = [("E", LT_TILES[j - 1], s) for s in e_stages(LT_TILES[j - 1])] if j else []
        if j and t in (("wo", 0), ("f2", 8 * (FFC - 1))):
            out.extend(behind)
            behind = []
        if j + 1 < len(LT_TILES):
            out.append(("split", j + 1, None))
        for p in range(PARTS):
            out.append(("mm", j, p))
            half = PARTS // 2
            if p < half:
                out.extend(behind[len(behind) * p // half:len(behind) * (p + 1) // half])
            a = half - 1 if reads_last else 0
            if p >= a:
                out.extend(beside[len(beside) * (p - a) // (PARTS - a):len(beside) * (p + 1 - a) // (PARTS - a)])

    out.append(("split", 0, None))
    tile(0)
    j = 1
    for slot in range(HEADS + 2):
        a = [("A", slot - 1, s) for s in A_STAGES] if 1 <= slot <= HEADS else []
        b = [("B", slot - 2, s) for s in B_STAGES] if slot >= 2 else []
        if slot == 0:
            a = [("G", 0, s) for s in G_STAGES]
        n = 4 if slot < HEADS else 0
        if not n:
            n = 2 if slot == HEADS else 1
        for i in range(n):
            beside = []
            m = max(len(a), len(b))
            for k in range(PARTS * 4):
                for c in (a, b):
                    lo, hi = i / n, (i + 1) / n
                    part = c[int(len(c) * lo):int(len(c) * hi)]
                    beside += part[len(part) * k // (PARTS * 4):len(part) * (k + 1) // (PARTS * 4)]
            if slot == 0 and i == 0:
                beside, late = [], beside
            elif slot == 0 and i == 1:
                beside = late + beside
            tile(j, beside, reads_last=(i == 0))
            j += 1
    c = [("C", t, s) for t in range(SWQ) for s in C_STAGES]
    first = L_AT["swq", 1]
    assert j == first
    n = L_AT["gb", 0] - first
    while j < len(LT_TILES):
        i = j - first
        tile(j, c[len(c) * i // n:len(c) * (i + 1) // n] if i < n else (), reads_last=(i == 0))
        j += 1
    out.extend([("E", LT_TILES[-1], s) for s in e_stages(LT_TILES[-1])])
    return out


L_ORDER = layer_order()

def e2_stages(out):
    kind, i = out
    if kind == "ub":
        return (["scale", "bias"] + [f"sum{m}" for m in range(i + 1)] + ["mean", "early", "high", "low"])
    return {"ua": ["scale", "bias"], "za": ["scale", "bias", "tanh", "silu"], "zb": ["scale", "bias", "tanh", "silu"],
            "pw": ["scale", "high", "low"], "gb": ["scale", "bias", "tanh"], "ga": ["scale", "bias", "tanh"],
            "bb": ["gate"], "glu": ["tanh", "gate", "silu", "high", "low"], "ba": ["gate", "add", "high", "low"],
            "wo": ["add", "square", "sum"]}[kind]


T_STAGES = ["coscos", "sinsin", "cos", "cossin", "sincos", "sin"]
SS_BASE = ["input", "turn", "turned", "scan", "back", "state", "output"]


def s_stages(st):
    return (SS_BASE + (["skip", "gelu"] if st % 4 == 3 else []) + (["highs", "lows"] if st == ST - 1 else []))


E2 = Count([(o, e2_stages(o)) for t in S_TILES for o in outputs_of(t)])
T = Count([(st, T_STAGES) for st in range(ST)])
SS = Count([(st, s_stages(st)) for st in range(ST)])
S_OUT = [o for t in S_TILES for o in outputs_of(t)]
S_OUT_AT = {o: n for n, o in enumerate(S_OUT)}


def second_order():
    out = [("split", 0, None)]
    first, last = S_AT["za", 0], S_AT["glu", 0]
    s = [("T", 0, t) for t in T_STAGES]
    for st in range(ST):
        tables = [("T", st + 1, t) for t in T_STAGES] if st + 1 < ST else []
        mine = [("S", st, t) for t in s_stages(st)]
        for i, m in enumerate(mine):
            s.append(m)
            s += tables[len(tables) * i // len(mine):len(tables) * (i + 1) // len(mine)]
    behind = []
    for j, t in enumerate(S_TILES):
        if j + 1 < len(S_TILES):
            out.append(("split", j + 1, None))
        if t in (("ba", 0), ("wo", 0), ("pw", 0), ("bb", 0)):
            out.extend(behind)
            behind = []
        outs = outputs_of(t)
        each = PARTS // len(outs)
        i = j - first
        beside = s[len(s) * i // (last - first):len(s) * (i + 1) // (last - first)] if first <= j < last else []
        for p in range(PARTS):
            out.append(("mm", j, p))
            half = each // 2 if each > 1 else 1
            q = p % each
            if q < half:
                out.extend(behind[len(behind) * q // half:len(behind) * (q + 1) // half])
            if q == each - 1:
                behind = [("E", outs[p // each], e) for e in e2_stages(outs[p // each])]
            a = PARTS // 2 - 1 if j == first else 0
            if p >= a:
                out.extend(beside[len(beside) * (p - a) // (PARTS - a):len(beside) * (p + 1 - a) // (PARTS - a)])
    out.extend(behind)
    return out


S_ORDER = second_order()
RAW, SPLIT = 3, 2


def build(nc, xT, pos, consts, params, w1, w2, params2, smallb, smallc, outT):
    with ExitStack() as ctx:
        def sb(name, shape, dt=F32):
            return ctx.enter_context(nc.sbuf_tensor(name, shape, dt))

        def sem(name):
            return ctx.enter_context(nc.semaphore(name))

        def at(base, off, name, shape, dt=F32):
            return nc.alloc_sbuf_tensor_at(name, shape, dt, offset=base + off)

        TILE = SEQ * 4
        x = sb("x", [P, KT, SEQ])
        hH, hL = sb("hH", [P, KT, SEQ], F32R), sb("hL", [P, KT, SEQ], F32R)
        cst = sb("cst", [P, NCONST])
        par_at = (nc.sbuf_base + 31) // 32 * 32
        par = sb("par", [P, NPARAM])
        rope_at = (nc.sbuf_base + 31) // 32 * 32
        ropeC, ropeS = sb("ropeC", [P, SEQ]), sb("ropeS", [P, SEQ])
        raw = sb("raw", [P, RAW, KT, P])
        wH, wL = sb("wH", [P, SPLIT, KT, P], F32R), sb("wL", [P, SPLIT, KT, P], F32R)
        rstd, rstdp = sb("rstd", [P, SEQ]), sb("rstdp", [P, SEQ])
        sq = sb("sq", [P, 2, SEQ])
        tmp = sb("tmp", [P, SEQ])
        small = sb("small", [P, 512])
        turn_small = sb("turn_small", [P, 2, ST, TBL])
        base_o = (nc.sbuf_base + 31) // 32 * 32
        OH, OL = sb("OH", [P, KT, SEQ], F32R), sb("OL", [P, KT, SEQ], F32R)
        base_s = (nc.sbuf_base + 31) // 32 * 32
        SH, SL = sb("SH", [P, KT, SEQ], F32R), sb("SL", [P, KT, SEQ], F32R)
        base_a = (nc.sbuf_base + 31) // 32 * 32
        acc = sb("acc", [P, KT, SEQ])
        base_r = (nc.sbuf_base + 31) // 32 * 32
        room = sb("room", [P, 11, SEQ])

        hd = at(base_s, 0, "hd", [P, 3, 4, SEQ])
        kbeta = at(base_s, 12 * TILE, "kbeta", [P, SEQ])
        Xi = at(base_s, 13 * TILE, "Xi", [P, CH, P])
        LTm = at(base_s, 14 * TILE, "LTm", [P, CH, P])
        Pm = at(base_s, 15 * TILE, "Pm", [P, CH, P])
        XT = at(base_a, 0, "XT", [P, 2, CH, P])
        AT = at(base_a, 2 * TILE, "AT", [P, 2, CH, P])
        qd = at(base_a, 4 * TILE, "qd", [P, 2, CH, P])
        kd = at(base_a, 6 * TILE, "kd", [P, 2, CH, P])
        vb = at(base_r, 0, "vb", [P, 2, CH, P])
        DT = at(base_r, 2 * TILE, "DT", [P, CH, P])
        sqa = at(base_r, 3 * TILE, "sqa", [P, SEQ])
        rna = at(base_r, 4 * TILE, "rna", [P, SEQ])
        osq = at(base_r, 5 * TILE, "osq", [P, SEQ])
        orn = at(base_r, 6 * TILE, "orn", [P, SEQ])
        S = at(base_r, 7 * TILE, "S", [P, P])
        rr = at(base_r, 7 * TILE + 512, "rr", [P, P])
        vn = at(base_r, 7 * TILE + 1024, "vn", [P, P])
        ab = at(base_r, 8 * TILE, "ab", [P, SEQ])
        qraw = at(base_s, 8 * TILE, "qraw", [P, SWQ, SEQ])
        kc, kr = hd[:, 2, 0, :], hd[:, 2, 1, :]
        kk = at(base_r, 8 * TILE, "kk", [P, 2, SEQ])
        vtok = at(base_r, 10 * TILE, "vtok", [P, CH, P])
        qr = at(base_r, 0, "qr", [P, SEQ])
        qc = at(base_r, 1 * TILE, "qc", [P, SEQ])
        prob = at(base_r, 2 * TILE, "prob", [P, CH, 2 * P])
        probT = at(base_r, 4 * TILE, "probT", [P, 2 * CH, P])
        gate = at(base_r, 6 * TILE, "gate", [P, SEQ])
        gated = at(base_r, 7 * TILE, "gated", [P, SEQ])
        def col(i, n=CH * HEADS):
            return small[:, i:i + n]
        abt, th, beta, hbeta = col(0, 64), col(64), col(96), col(128)
        at_, mx, ea, gg, gcl = col(160), col(192), col(224, 8), col(232), col(264, 64)
        kdec, egl, eg, nbeg = col(328), col(360), col(392), col(424)
        m4, nm4, den, es = col(456, 4), col(460, 4), col(464, 4), col(468, 4)

        ps = ctx.enter_context(nc.psum_tensor("ps", [P, 8, 512], F32))
        psA, psB = ps[:, 2:4, :], ps[:, 4:6, :]

        def k_(name):
            return cst[:, CONST[name][0]:CONST[name][1]]

        def p_(name, i=None, n=1):
            a, b = PARAM[name]
            return par[:, a:b] if i is None else par[:, a + i:a + i + n]

        def conv(kind, head, tap):
            return p_("conv", ("qkv".index(kind) * HEADS + head) * CONV + tap)

        def over_chunks(m):
            return m.unsqueeze(1).to_broadcast([P, CH, P])

        names = ("loaded0", "loaded1", "loaded2", "high_done", "low_done", "tile_done", "tile_stage",
                 "gate_stage", "inverse_stage", "scan_stage", "window_stage", "x_ready", "sq_done", "h_high", "h_low",
                 "ssq_done", "root_done", "rstd_ready", "params_in", "x_part", "sum_in", "sum_done", "post_root",
                 "post_ready", "input_in", "out_done", "setup", "out_ready", "table_stage", "state_stage")
        sems = {n: sem(n) for n in names}
        nums = [s.num for s in sems.values()]
        assert nums == list(range(nums[0], nums[0] + len(nums)))
        loaded = [sems[f"loaded{i}"] for i in range(RAW)]
        (high_done, low_done, tile_done, tile_stage, gate_stage, inverse_stage, scan_stage, window_stage, x_ready,
         sq_done, h_high, h_low, ssq_done, root_done, rstd_ready, params_in, x_part, sum_in, sum_done, post_root,
         post_ready, input_in, out_done, setup, out_ready, table_stage, state_stage) = [sems[n] for n in names[RAW:]]

        def clear_all():
            with nc.Block() as block:
                @block.sync
                def _(sp):
                    sp.sem_clear(range(nums[0], nums[0] + len(nums)))

        with nc.Block() as block:
            @block.sync
            def _(sp):
                sp.dma_start(x[:, :, :], xT).then_inc(input_in, 16)
                sp.dma_start(cst[:, :], consts).then_inc(input_in, 16)
                sp.dma_start(sq[:, 0, :].bitcast(I32), pos.to_broadcast([P, SEQ])).then_inc(input_in, 16)

            @block.vector
            def _(v):
                step = [0]

                def link(ins):
                    step[0] += 1
                    ins.then_inc(setup, 1)
                    v.wait_ge(setup, step[0])

                v.wait_ge(input_in, 48)
                link(v.tensor_copy(tmp[:, :], sq[:, 0, :].bitcast(I32)))
                link(v.tensor_scalar(tmp[:, :], tmp[:, :], k_("invfreq"), None, ALU.mult))
                range_reduce(v, link, rstd[:, :], tmp[:, :], sq[:, 0, :], 0.0)
                range_reduce(v, link, rstdp[:, :], tmp[:, :], sq[:, 0, :], 0.25)
                v.wait_ge(x_part, 2)
                link(v.tensor_scalar(ropeS[:, :], ropeS[:, :], k_("isrot"), None, ALU.mult))
                link(v.tensor_scalar(ropeC[:, :], ropeC[:, :], k_("isrot"), k_("notrot"), ALU.mult, ALU.add))

            @block.scalar
            def _(act):
                act.wait_ge(setup, 2 + 2 * RANGE_STEPS)
                act.activation(ropeS[:, :], rstd[:, :], ACT.Sin).then_inc(x_part, 1)
                act.activation(ropeC[:, :], rstdp[:, :], ACT.Sin, bias=k_("halfpi")).then_inc(x_part, 1)
        clear_all()

        def splitting(block, tiles, weights, params_of):
            @block.sync
            def _(sp):
                if params_of is not None:
                    sp.dma_start(par[:, :], params_of).then_inc(params_in, 16)
                for j in range(len(tiles)):
                    if j >= RAW:
                        sp.wait_ge(low_done, j - RAW + 1)
                    sp.dma_start(raw[:, j % RAW, :, :].rearrange("p t n -> p (t n)"), weights(j)).then_inc(loaded[j % RAW], 16)

        def split_high(act, j):
            act.wait_ge(loaded[j % RAW], 16 * (j // RAW + 1))
            if j >= SPLIT:
                act.wait_ge(tile_done, j - SPLIT + 1)
            act.activation(wH[:, j % SPLIT, :, :], raw[:, j % RAW, :, :], ACT.Copy).then_inc(high_done, 1)

        def split_low(pool, j):
            pool.wait_ge(high_done, j + 1)
            pool.tensor_tensor(wL[:, j % SPLIT, :, :], raw[:, j % RAW, :, :], wH[:, j % SPLIT, :, :].bitcast(F32),
                               ALU.subtract).then_inc(low_done, 1)

        def products(pe, j, p, out, rH, rL, depth, col0=0, width=P, kt0=0, parts=PARTS, before=None):
            s = j % SPLIT
            t = -1
            for t in range(depth * p // parts, depth * (p + 1) // parts):
                if before is not None:
                    before(t)
                wh = wH[:, s, kt0 + t, col0:col0 + width]
                wl = wL[:, s, kt0 + t, col0:col0 + width]
                pe.matmul(out, wh, rH[:, t, :], start=(t == 0), stop=False)
                pe.matmul(out, wh, rL[:, t, :], start=False, stop=False)
                mm = pe.matmul(out, wl, rH[:, t, :], start=False, stop=(t == depth - 1))
            if (t + 1) == depth:
                mm.then_inc(tile_done, 1)

        tmp2 = [room[:, 9, :], room[:, 10, :]]

        def x_add(v, t, gain, n):
            v.scalar_tensor_tensor(out=tmp2[t % 2], in0=acc[:, t, :], scalar=gain(t), in1=rstdp[:, :],
                                   op0=ALU.mult, op1=ALU.mult).then_inc(x_part, 1)
            v.wait_ge(x_part, n + t + 1)
            v.tensor_tensor(x[:, t, :], x[:, t, :], tmp2[t % 2], ALU.add).then_inc(x_ready, 1)

        def x_low(v, t, gain, n):
            v.wait_ge(h_high, n + t + 1)
            v.scalar_tensor_tensor(out=hL[:, t, :], in0=x[:, t, :], scalar=gain(t), in1=hH[:, t, :].bitcast(F32),
                                   op0=ALU.mult, op1=ALU.subtract).then_inc(h_low, 1)

        def x_high(act, gain, n, ready):
            for t in range(KT):
                if ready is not None:
                    act.wait_ge(x_ready, ready + t + 1)
                act.activation(hH[:, t, :], x[:, t, :], ACT.Copy, scale=gain(t)).then_inc(h_high, 1)
                if t >= 2:
                    act.wait_ge(ssq_done, n + t - 1)
                act.activation(sq[:, t % 2, :], x[:, t, :], ACT.Square).then_inc(sq_done, 1)

        def x_sum(pe, base, t):
            pe.wait_ge(sq_done, base + t + 1)
            pe.matmul(ps[:, 7, :], k_("ones"), sq[:, t % 2, :], start=(t == 0), stop=(t == KT - 1)).then_inc(ssq_done, 1)

        def root_scalar(act, done, n, out, src, scale, eps, ready):
            act.wait_ge(done, n)
            act.activation(out, src, ACT.Sqrt, bias=k_(eps), scale=scale).then_inc(ready, 1)

        with nc.Fori(0, DEPTH) as layer:
            with nc.Block() as block:
                splitting(block, LT_TILES, lambda j: w1[layer, j], params[layer])

                @block.gpsimd
                def _(pool):
                    for kind, j, s in L_ORDER:
                        if kind == "split":
                            split_low(pool, j)
                        elif kind == "A":
                            if s not in ("normk", "qdec", "mask"):
                                continue
                            pool.wait_ge(inverse_stage, A.before(j, s))
                            q, k = hd[:, j % 3, 0, :], hd[:, j % 3, 1, :]
                            if s == "normk":
                                pool.tensor_tensor(k, k, rna[:, :], ALU.mult).then_inc(inverse_stage, 1)
                            if s == "qdec":
                                if j >= 2:
                                    pool.wait_ge(scan_stage, B.end(j - 2))
                                pool.tensor_tensor(qd[:, j % 2, :, :], q.rearrange("p (c n) -> p c n", c=CH),
                                                   rna[:, :].rearrange("p (c n) -> p c n", c=CH),
                                                   ALU.mult).then_inc(inverse_stage, 1)
                            if s == "mask":
                                pool.tensor_tensor(DT[:, :, :], DT[:, :, :], over_chunks(k_("upper")),
                                                   ALU.mult).then_inc(inverse_stage, 1)
                        elif kind == "B" and s in ("gate", "low"):
                            pool.wait_ge(scan_stage, B.before(j, s))
                            if s == "gate":
                                pool.tensor_tensor(osq[:, :], osq[:, :], hd[:, j % 3, 3, :], ALU.mult).then_inc(scan_stage, 1)
                            else:
                                pool.tensor_tensor(OL[:, j, :], osq[:, :], OH[:, j, :].bitcast(F32),
                                                   ALU.subtract).then_inc(scan_stage, 1)
                        elif kind == "E" and s == "low":
                            pool.wait_ge(tile_stage, E.before(j, s))
                            if j[0] == "f1":
                                c, t = j[1] // 8, j[1] % 8
                                pool.tensor_tensor((OL, SL)[c % 2][:, t, :], tmp[:, :],
                                                   (OH, SH)[c % 2][:, t, :].bitcast(F32),
                                                   ALU.subtract).then_inc(tile_stage, 1)
                            else:
                                pool.tensor_tensor(OL[:, j[1], :], gated[:, :], OH[:, j[1], :].bitcast(F32),
                                                   ALU.subtract).then_inc(tile_stage, 1)

                @block.scalar
                def _(act):
                    act.wait_ge(params_in, 16)
                    split_high(act, 0)
                    x_high(act, lambda t: p_("pre_mix", t), 0, None)
                    root_scalar(act, ssq_done, KT, rstd[:, :], ps[:, 7, :], 1.0 / D_MODEL, "eps", root_done)
                    for kind, j, s in L_ORDER[1:]:
                        if kind == "split":
                            split_high(act, j)
                        elif kind == "G" and s in ("tanh", "abs", "expn", "ln", "expa", "exps"):
                            act.wait_ge(gate_stage, G.before(0, s))
                            a3 = abt.rearrange("p (c n) -> p c n", c=CH)
                            if s == "tanh":
                                act.activation(th.rearrange("p (c n) -> p c n", c=CH), a3[:, :, 0:HEADS], ACT.Tanh, scale=0.5).then_inc(gate_stage, 1)
                            if s == "abs":
                                act.activation(at_, at_, ACT.Abs).then_inc(gate_stage, 1)
                            if s == "expn":
                                act.activation(at_, at_, ACT.Exp, scale=-1.0).then_inc(gate_stage, 1)
                            if s == "ln":
                                act.activation(at_, at_, ACT.Ln).then_inc(gate_stage, 1)
                            if s == "expa":
                                act.activation(ea, p_("a_log"), ACT.Exp).then_inc(gate_stage, 1)
                            if s == "exps":
                                act.activation(kdec, kdec, ACT.Exp)
                                act.activation(egl, gcl[:, 32:64], ACT.Exp)
                                act.activation(eg, gcl[:, 0:32], ACT.Exp).then_inc(gate_stage, 1)
                        elif kind == "A":
                            q, k, vv = (hd[:, j % 3, i, :] for i in range(3))
                            mine = ("sqk", "rootk", "sqq", "rootq", "exps", "copykv")
                            if not (s in mine or s.startswith("copy")):
                                continue
                            act.wait_ge(inverse_stage, A.before(j, s))
                            if s in ("sqk", "sqq"):
                                if s == "sqk":
                                    act.wait_ge(tile_stage, E.end(("z", j)))
                                act.activation(sqa[:, :], k if s == "sqk" else q, ACT.Square).then_inc(inverse_stage, 1)
                            elif s in ("rootk", "rootq"):
                                act.activation(rna[:, :], psA[:, 0, :], ACT.Sqrt, bias=k_("eps4")).then_inc(inverse_stage, 1)
                            elif s == "exps":
                                act.activation(rna[:, :], psA[:, 0, :], ACT.Exp)
                                act.activation(DT[:, :, :], DT[:, :, :], ACT.Exp).then_inc(inverse_stage, 1)
                            elif s == "copykv":
                                for c in range(CH):
                                    i = c * HEADS + j
                                    act.activation(kd[:, j % 2, c, :], psA[:, 0, c * P:(c + 1) * P], ACT.Copy, scale=kdec[:, i:i + 1])
                                    ins = act.activation(vb[:, j % 2, c, :], psA[:, 1, c * P:(c + 1) * P], ACT.Copy, scale=hbeta[:, i:i + 1])
                                ins.then_inc(inverse_stage, 1)
                            else:
                                act.activation(Xi[:, :, :], psA[:, 0, :].rearrange("p (c n) -> p c n", c=CH), ACT.Copy).then_inc(inverse_stage, 1)
                        elif kind == "B" and (s.startswith("copyv") or s in ("square", "root", "high")):
                            act.wait_ge(scan_stage, B.before(j, s))
                            if s == "square":
                                act.activation(osq[:, :], psB[:, 1, :], ACT.Square).then_inc(scan_stage, 1)
                            elif s == "root":
                                act.activation(orn[:, :], psB[:, 0, :], ACT.Sqrt, bias=k_("eps4"), scale=4.0 / P).then_inc(scan_stage, 1)
                            elif s == "high":
                                act.activation(OH[:, j, :], osq[:, :], ACT.Copy).then_inc(scan_stage, 1)
                            else:
                                act.activation(vn[:, :], psB[:, 0, 0:P], ACT.Copy).then_inc(scan_stage, 1)
                        elif kind == "C" and (s[:-1] in ("exp", "copy") or s == "high"):
                            act.wait_ge(window_stage, C.before(j, s))
                            if s[:-1] == "exp":
                                e = int(s[-1])
                                for n in range(CH):
                                    a = P if n == 0 else 0
                                    act.activation(prob[:, n, a:], prob[:, n, a:], ACT.Exp, bias=nm4[:, n:n + 1],
                                                   accum_out=den[:, n:n + 1])
                                act.activation(es, nm4, ACT.Exp, bias=p_("sinks", 2 * j + e)).then_inc(window_stage, 1)
                            elif s[:-1] == "copy":
                                act.activation(probT[:, 0:2 * CH - 1, :], psB.rearrange("p b (c n) -> p (b c) n", n=P)[:, 0:2 * CH - 1, :],
                                               ACT.Copy).then_inc(window_stage, 1)
                            else:
                                act.activation(SH[:, j, :], ps[:, 7, :], ACT.Copy).then_inc(window_stage, 1)
                        elif kind == "E" and s in ("tap3", "tanh", "copyk", "copyv", "high", "square"):
                            act.wait_ge(tile_stage, E.before(j, s))
                            kd_, i = j
                            dst = hd[:, i % 3, "qkvz".index(kd_), :] if kd_ in "qkvz" else None
                            if s == "tap3":
                                if kd_ == "q" and i >= 3:
                                    act.wait_ge(scan_stage, B.end(i - 3))
                                act.activation(dst, tmp[:, :], ACT.Copy, scale=conv(kd_, i, 3)).then_inc(tile_stage, 1)
                            elif s == "tanh" and kd_ in "qkv":
                                act.activation(tmp[:, :], dst, ACT.Tanh, scale=0.5).then_inc(tile_stage, 1)
                            elif s == "tanh" and kd_ == "z":
                                act.activation(dst, tmp[:, :], ACT.Tanh, scale=0.5).then_inc(tile_stage, 1)
                            elif s == "tanh":
                                act.activation(gate[:, :], gate[:, :], ACT.Tanh, scale=0.5).then_inc(tile_stage, 1)
                            elif s == "copyk":
                                act.activation(kk[:, 0, :], ps[:, 6, :], ACT.Copy)
                                act.activation(kk[:, 1, :], ps[:, 7, :], ACT.Copy).then_inc(tile_stage, 1)
                            elif s == "copyv":
                                act.activation(vtok[:, :, :], ps[:, 6, :].rearrange("p (c n) -> p c n", c=CH), ACT.Copy).then_inc(tile_stage, 1)
                            elif s == "high" and kd_ == "f1":
                                act.activation((OH, SH)[i // 8 % 2][:, i % 8, :], tmp[:, :], ACT.Copy).then_inc(tile_stage, 1)
                            elif s == "high":
                                act.activation(OH[:, i, :], gated[:, :], ACT.Copy).then_inc(tile_stage, 1)
                            else:
                                act.activation(sq[:, 0, :], acc[:, i % 8, :], ACT.Square).then_inc(tile_stage, 1)
                            if j == ("wo", KT - 1) and s == "square":
                                root_scalar(act, sum_done, 1, rstdp[:, :], ps[:, 7, :], 1.0 / D_MODEL, "eps", post_root)
                                x_high(act, lambda t: p_("pre_mlp", t), KT, 0)
                                root_scalar(act, ssq_done, 2 * KT, rstd[:, :], ps[:, 7, :], 1.0 / D_MODEL, "eps", root_done)
                    root_scalar(act, sum_done, 2, rstdp[:, :], ps[:, 7, :], 1.0 / D_MODEL, "eps", post_root)

                @block.vector
                def _(v):
                    def rstd_vector(n):
                        v.wait_ge(root_done, n)
                        v.reciprocal(rstd[:, :], rstd[:, :]).then_inc(rstd_ready, 1)
                        v.wait_ge(rstd_ready, n)

                    def post_vector(n):
                        v.wait_ge(post_root, n)
                        v.reciprocal(rstdp[:, :], rstdp[:, :]).then_inc(post_ready, 1)

                    v.wait_ge(params_in, 16)
                    for t in range(KT):
                        x_low(v, t, lambda t: p_("pre_mix", t), 0)
                    rstd_vector(1)
                    for kind, j, s in L_ORDER[1:]:
                        if kind == "G":
                            if s not in ("copy", "beta", "hbeta", "addb", "max", "plus1", "sp", "g", "copyc", "diff", "nbeg"):
                                continue
                            v.wait_ge(gate_stage, G.before(0, s))
                            c8 = lambda ap: ap.rearrange("p (c n) -> p c n", c=CH)
                            if s == "copy":
                                ins = v.tensor_copy(abt, psA[:, 0, 0:64])
                            elif s == "beta":
                                ins = v.tensor_scalar(beta, th, 0.5, 0.5, ALU.mult, ALU.add)
                            elif s == "hbeta":
                                ins = v.tensor_scalar(hbeta, beta, 0.5, None, ALU.mult)
                            elif s == "addb":
                                ins = v.tensor_tensor(c8(at_), c8(abt)[:, :, HEADS:2 * HEADS],
                                                      p_("dt_bias").unsqueeze(1).to_broadcast([P, CH, HEADS]), ALU.add)
                            elif s == "max":
                                ins = v.tensor_scalar(mx, at_, 0.0, None, ALU.max)
                            elif s == "plus1":
                                ins = v.tensor_scalar(at_, at_, 1.0, None, ALU.add)
                            elif s == "sp":
                                ins = v.tensor_tensor(at_, at_, mx, ALU.add)
                            elif s == "g":
                                ins = v.scalar_tensor_tensor(out=c8(gg), in0=c8(at_), scalar=-1.0,
                                                             in1=ea.unsqueeze(1).to_broadcast([P, CH, HEADS]),
                                                             op0=ALU.mult, op1=ALU.mult)
                            elif s == "copyc":
                                ins = v.tensor_copy(gcl, psA[:, 0, 0:64])
                            elif s == "diff":
                                ins = v.tensor_tensor(kdec, gcl[:, 32:64], gcl[:, 0:32], ALU.subtract)
                            else:
                                ins = v.scalar_tensor_tensor(out=nbeg, in0=beta, scalar=-1.0, in1=eg,
                                                             op0=ALU.mult, op1=ALU.mult)
                            ins.then_inc(gate_stage, 1)
                        elif kind == "A":
                            h = j
                            q, k = hd[:, h % 3, 0, :], hd[:, h % 3, 1, :]
                            a0, a1 = (psA[:, i, :].rearrange("p (c n) -> p c n", c=CH) for i in range(2))
                            lev = int(s[-1]) if s[-1].isdigit() else None
                            if not (s in ("recipk", "recipq", "normq", "kbeta", "diff", "masked", "first", "minus")
                                    or s.startswith("pmask") or s.startswith("update")):
                                continue
                            v.wait_ge(inverse_stage, A.before(h, s))
                            if s in ("recipk", "recipq"):
                                ins = v.reciprocal(rna[:, :], rna[:, :])
                            elif s == "normq":
                                ins = v.scalar_tensor_tensor(out=q, in0=q, scalar=float(P) ** -0.5, in1=rna[:, :],
                                                             op0=ALU.mult, op1=ALU.mult)
                            elif s == "kbeta":
                                ins = v.tensor_tensor(kbeta[:, :], k, psA[:, 1, :], ALU.mult)
                            elif s == "diff":
                                for c in range(CH):
                                    i = c * HEADS + h
                                    ins = v.tensor_scalar(DT[:, c, :], a0[:, c, :], gcl[:, i:i + 1], 0.0,
                                                          ALU.subtract, ALU.min)
                            elif s == "masked":
                                if h >= 2:
                                    v.wait_ge(scan_stage, B.end(h - 2))
                                v.tensor_tensor(AT[:, h % 2, :, :], a1, DT[:, :, :], ALU.mult)
                                ins = v.tensor_tensor(LTm[:, :, :], a0, DT[:, :, :], ALU.mult)
                            elif s == "first":
                                ins = v.tensor_tensor(XT[:, h % 2, :, :], LTm[:, :, :], over_chunks(k_("first")), ALU.mult)
                            elif s == "minus":
                                ins = v.tensor_tensor(XT[:, h % 2, :, :], over_chunks(k_("ident")), XT[:, h % 2, :, :], ALU.subtract)
                            elif s.startswith("pmask"):
                                m = k_("levels")[:, lev * P:(lev + 1) * P]
                                ins = v.tensor_tensor(Pm[:, :, :], a0, over_chunks(m), ALU.mult)
                            else:
                                ins = v.tensor_tensor(XT[:, h % 2, :, :], XT[:, h % 2, :, :], a1, ALU.subtract)
                            ins.then_inc(inverse_stage, 1)
                        elif kind == "B":
                            h = j
                            if not (s[:-1] in ("rr", "state") or s in ("recip", "norm")):
                                continue
                            v.wait_ge(scan_stage, B.before(h, s))
                            if s == "state0":
                                ins = v.tensor_copy(S[:, :], psB[:, 0, P:2 * P])
                            elif s.startswith("state"):
                                i = int(s[-1]) * HEADS + h
                                ins = v.scalar_tensor_tensor(out=S[:, :], in0=S[:, :], scalar=egl[:, i:i + 1],
                                                             in1=psB[:, 0, P:2 * P], op0=ALU.mult, op1=ALU.add)
                            elif s.startswith("rr"):
                                c = int(s[-1])
                                i = c * HEADS + h
                                ins = v.scalar_tensor_tensor(out=rr[:, :], in0=psB[:, 0, 2 * P:3 * P],
                                                             scalar=nbeg[:, i:i + 1], in1=vb[:, h % 2, c, :],
                                                             op0=ALU.mult, op1=ALU.add)
                            elif s == "recip":
                                ins = v.reciprocal(orn[:, :], orn[:, :])
                            else:
                                ins = v.scalar_tensor_tensor(out=osq[:, :], in0=psB[:, 1, :], scalar=p_("norm"),
                                                             in1=orn[:, :], op0=ALU.mult, op1=ALU.mult)
                            ins.then_inc(scan_stage, 1)
                        elif kind == "C":
                            t = j
                            e = int(s[-1]) if s[-1].isdigit() else 0
                            w = s.rstrip("01")
                            if w not in ("cos", "sin", "addq", "mask", "max", "maxs", "neg", "den", "recip", "prob", "low"):
                                continue
                            v.wait_ge(window_stage, C.before(t, s))
                            if w == "cos":
                                ins = v.tensor_tensor(qc[:, :], qraw[:, t, :], ropeC[:, :], ALU.mult)
                            elif w == "sin":
                                if t == 0:
                                    v.memset(prob[:, 0, 0:P], NEG)
                                ins = v.tensor_tensor(qr[:, :], ps[:, 6, :], ropeS[:, :], ALU.mult)
                            elif w == "addq":
                                ins = v.tensor_tensor(qr[:, :], qr[:, :], qc[:, :], ALU.add)
                            elif w == "mask":
                                sc = psA.rearrange("p b (n k) -> p (b n) k", k=2 * P)
                                v.scalar_tensor_tensor(out=prob[:, 0, P:], in0=sc[:, 0, P:], scalar=float(HD) ** -0.5,
                                                       in1=k_("window")[:, P:], op0=ALU.mult, op1=ALU.add)
                                ins = v.scalar_tensor_tensor(out=prob[:, 1:, :], in0=sc[:, 1:, :], scalar=float(HD) ** -0.5,
                                                             in1=k_("window").unsqueeze(1).to_broadcast([P, CH - 1, 2 * P]),
                                                             op0=ALU.mult, op1=ALU.add)
                            elif w == "max":
                                ins = v.tensor_reduce(m4, prob[:, :, :], AX.X, ALU.max)
                            elif w == "maxs":
                                ins = v.tensor_scalar(m4, m4, p_("sinks", 2 * t + e), None, ALU.max)
                            elif w == "neg":
                                ins = v.tensor_scalar(nm4, m4, -1.0, None, ALU.mult)
                            elif w == "den":
                                ins = v.tensor_tensor(den, den, es, ALU.add)
                            elif w == "recip":
                                ins = v.reciprocal(den, den)
                            elif w == "prob":
                                v.tensor_scalar(prob[:, 0, P:], prob[:, 0, P:], den[:, 0:1], None, ALU.mult)
                                ins = v.tensor_tensor(prob[:, 1:, :], prob[:, 1:, :],
                                                      den[:, 1:].unsqueeze(2).to_broadcast([P, CH - 1, 2 * P]), ALU.mult)
                            else:
                                ins = v.tensor_tensor(SL[:, t, :], ps[:, 7, :], SH[:, t, :].bitcast(F32), ALU.subtract)
                            ins.then_inc(window_stage, 1)
                        elif kind == "E":
                            kd_, i = j
                            n = L_AT[j]
                            b = ps[:, n % 2, :]
                            if s in ("tanh", "tap3", "rotk", "dupk", "copyk", "turnv", "copyv", "high", "low", "square"):
                                continue
                            v.wait_ge(tile_stage, E.before(j, s))
                            if s == e_stages(j)[0]:
                                v.wait_ge(tile_done, n + 1)
                                if j == ("f1", 0):
                                    rstd_vector(2)
                            dst = hd[:, i % 3, "qkvz".index(kd_), :] if kd_ in "qkvz" else None
                            if s == "scale":
                                out = {"ab": ab[0:16, :], "ga": gate[:, :], "gb": gate[:, :], "swq": None}.get(kd_, tmp[:, :])
                                if kd_ == "swq":
                                    out = qraw[:, i, :]
                                m = 16 if kd_ == "ab" else P
                                if j == ("swq", 0):
                                    v.wait_ge(scan_stage, B.end(HEADS - 1))
                                ins = v.tensor_tensor(out, b[0:m, :], rstd[0:m, :], ALU.mult)
                            elif s in ("tap2", "tap1", "tap0"):
                                d = 3 - int(s[-1])
                                ins = v.scalar_tensor_tensor(out=dst[:, d:], in0=tmp[:, 0:SEQ - d], scalar=conv(kd_, i, 3 - d),
                                                             in1=dst[:, d:], op0=ALU.mult, op1=ALU.add)
                            elif s == "silu" and kd_ != "z":
                                ins = v.scalar_tensor_tensor(out=dst, in0=tmp[:, :], scalar=1.0, in1=dst, op0=ALU.add, op1=ALU.mult)
                            elif s == "silu":
                                ins = v.scalar_tensor_tensor(out=dst, in0=dst, scalar=1.0, in1=tmp[:, :], op0=ALU.add, op1=ALU.mult)
                            elif s == "cosk":
                                v.wait_ge(scan_stage, B.end(HEADS - 3))
                                ins = v.tensor_tensor(kc, tmp[:, :], ropeC[:, :], ALU.mult)
                            elif s == "sink":
                                ins = v.tensor_tensor(kr, ps[:, 6, :], ropeS[:, :], ALU.mult)
                            elif s == "addk":
                                ins = v.tensor_tensor(kr, kr, kc, ALU.add)
                            elif s == "gate" and kd_ == "ya":
                                ins = v.scalar_tensor_tensor(out=acc[:, i, :], in0=gate[:, :], scalar=1.0, in1=b, op0=ALU.add, op1=ALU.mult)
                            elif s == "gate":
                                ins = v.scalar_tensor_tensor(out=gated[:, :], in0=gate[:, :], scalar=1.0, in1=b, op0=ALU.add, op1=ALU.mult)
                            elif s == "add" and kd_ == "yb":
                                ins = v.tensor_tensor(gated[:, :], gated[:, :], acc[:, i, :], ALU.add)
                            elif s == "relu2":
                                ins = v.scalar_tensor_tensor(out=tmp[:, :], in0=tmp[:, :], scalar=0.0, in1=tmp[:, :], op0=ALU.max, op1=ALU.mult)
                            elif s == "copy" and kd_ == "wo":
                                ins = v.tensor_scalar(acc[:, i, :], b, 0.5, None, ALU.mult)
                            elif s == "copy":
                                ins = v.tensor_copy(acc[:, i % 8, :], b)
                            elif s == "add":
                                ins = v.tensor_tensor(acc[:, i % 8, :], acc[:, i % 8, :], b, ALU.add)
                            elif s == "sum":
                                if i % 8 == 0:
                                    ins = v.tensor_copy(sq[:, 1, :], sq[:, 0, :])
                                else:
                                    ins = v.tensor_tensor(sq[:, 1, :], sq[:, 1, :], sq[:, 0, :], ALU.add)
                            ins.then_inc(tile_stage, 1)
                            if j == ("wo", KT - 1) and s == "sum":
                                post_vector(1)
                                v.wait_ge(post_ready, 1)
                                for t in range(KT + 1):
                                    if t < KT:
                                        x_add(v, t, lambda t: p_("post_mix", t), 0)
                                    if t:
                                        x_low(v, t - 1, lambda t: p_("pre_mlp", t), KT)
                    post_vector(2)
                    v.wait_ge(post_ready, 2)
                    for t in range(KT):
                        x_add(v, t, lambda t: p_("post_mlp", t), KT)

                @block.tensor
                def _(pe):
                    ident = k_("ident")
                    for kind, j, s in L_ORDER:
                        if kind == "mm":
                            tile = LT_TILES[j]
                            kd_, i = tile
                            rH, rL = hH, hL
                            before = None
                            if s == 0:
                                pe.wait_ge(low_done, j + 1)
                                if j >= 2:
                                    pe.wait_ge(tile_stage, E.before(LT_TILES[j - 2], e_stages(LT_TILES[j - 2])[0]) + 1)
                                if tile == ("ya", 0):
                                    pe.wait_ge(scan_stage, B.end(HEADS - 1))
                                if tile == ("yb", 0):
                                    pe.wait_ge(window_stage, C.end(SWQ - 1))
                                if tile == ("wo", 0):
                                    pe.wait_ge(tile_stage, E.end(("yb", KT - 1)))
                                if kd_ == "f2" and i % 8 == 0:
                                    pe.wait_ge(tile_stage, E.end(("f1", i + 7)))
                                if tile == ("f1", 0):
                                    pe.wait_ge(tile_stage, E.end(("wo", KT - 1)))
                                    pe.matmul(ps[:, 7, :], k_("ones"), sq[:, 1, :], start=True, stop=True).then_inc(sum_done, 1)
                            if kd_ in ("ya", "wo"):
                                rH, rL = OH, OL
                            elif kd_ == "yb":
                                rH, rL = SH, SL
                            elif kd_ == "f2":
                                rH, rL = (OH, OL) if i // 8 % 2 == 0 else (SH, SL)
                            if tile in (("ab", 0), ("f1", 0)):
                                base = 0 if kd_ == "ab" else KT

                                def before(t, base=base):
                                    if t == 0 and base:
                                        pe.wait_ge(post_root, 1)
                                    pe.wait_ge(h_low, base + t + 1)
                                    x_sum(pe, base, t)
                            m = 16 if kd_ == "ab" else P
                            products(pe, j, s, ps[0:m, j % 2, :], rH, rL, KT, width=m, before=before)
                        elif kind == "G" and s in ("turn", "cumsum"):
                            pe.wait_ge(gate_stage, G.before(0, s))
                            if s == "turn":
                                pe.wait_ge(tile_stage, E.end(("ab", 0)))
                                for c in range(CH):
                                    ins = pe.transpose(psA[:, 0, c * 16:(c + 1) * 16], ab[0:16, c * P:(c + 1) * P], ident[0:16, 0:16])
                            else:
                                pe.matmul(psA[:, 0, 0:32], k_("upper"), gg, start=True, stop=True)
                                ins = pe.matmul(psA[:, 0, 32:64], k_("ones"), gg, start=True, stop=True)
                            ins.then_inc(gate_stage, 1)
                        elif kind == "A":
                            h = j
                            mine = ("sumk", "sumq", "rows", "gram", "turnkv")
                            if not (s in mine or s[:-1] in ("p", "q", "turn")):
                                continue
                            pe.wait_ge(inverse_stage, A.before(h, s))
                            q, k, vv = (hd[:, h % 3, i, :] for i in range(3))
                            cs = [slice(c * P, (c + 1) * P) for c in range(CH)]
                            for c in range(CH):
                                i = c * HEADS + h
                                if s in ("sumk", "sumq"):
                                    if c == 0:
                                        ins = pe.matmul(psA[:, 0, :], k_("ones"), sqa[:, :], start=True, stop=True)
                                elif s == "rows":
                                    if h == 0 and c == 0:
                                        pe.wait_ge(gate_stage, G.end(0))
                                    pe.matmul(psA[:, 0, cs[c]], gg[:, i:i + 1].to_broadcast([P, P]), k_("upper"), start=True, stop=True)
                                    ins = pe.matmul(psA[:, 1, cs[c]], beta[:, i:i + 1].to_broadcast([P, P]), ident, start=True, stop=True)
                                elif s == "gram":
                                    pe.matmul(psA[:, 0, cs[c]], k[:, cs[c]], kbeta[:, cs[c]], start=True, stop=True)
                                    ins = pe.matmul(psA[:, 1, cs[c]], k[:, cs[c]], q[:, cs[c]], start=True, stop=True)
                                elif s.startswith("turnkv"):
                                    pe.transpose(psA[:, 0, cs[c]], k[:, cs[c]], ident)
                                    ins = pe.transpose(psA[:, 1, cs[c]], vv[:, cs[c]], ident)
                                elif s.startswith("turn"):
                                    ins = pe.transpose(psA[:, 0, cs[c]], XT[:, h % 2, c, :], ident)
                                elif s.startswith("p"):
                                    ins = pe.matmul(psA[:, 0, cs[c]], LTm[:, c, :], Xi[:, c, :], start=True, stop=True)
                                else:
                                    ins = pe.matmul(psA[:, 1, cs[c]], Pm[:, c, :], XT[:, h % 2, c, :], start=True, stop=True)
                            ins.then_inc(inverse_stage, 1)
                        elif kind == "B" and (s[:-1] in ("v", "o", "r") or s == "sum"):
                            h = j
                            pe.wait_ge(scan_stage, B.before(h, s))
                            k = hd[:, h % 3, 1, :]
                            c = int(s[-1]) if s != "sum" else 0
                            cc = slice(c * P, (c + 1) * P)
                            if s == "v0":
                                pe.wait_ge(inverse_stage, A.end(h))
                            if s == "sum":
                                ins = pe.matmul(psB[:, 0, :], k_("ones"), osq[:, :], start=True, stop=True)
                            elif s[0] == "r":
                                ins = pe.matmul(psB[:, 0, 2 * P:3 * P], k[:, cc], S[:, :], start=True, stop=True)
                            elif s[0] == "v":
                                ins = pe.matmul(psB[:, 0, 0:P], XT[:, h % 2, c, :], vb[:, h % 2, 0, :] if c == 0 else rr[:, :],
                                                start=True, stop=True)
                            else:
                                if c:
                                    pe.matmul(psB[:, 1, cc], S[:, :], qd[:, h % 2, c, :], start=True, stop=False)
                                ins = pe.matmul(psB[:, 1, cc], vn[:, :], AT[:, h % 2, c, :], start=(c == 0), stop=True)
                                if c < CH - 1:
                                    ins = pe.matmul(psB[:, 0, P:2 * P], kd[:, h % 2, c, :], vn[:, :], start=True, stop=True)
                            ins.then_inc(scan_stage, 1)
                        elif kind == "C":
                            t = j
                            e = int(s[-1]) if s[-1].isdigit() else 0
                            rows = slice(HD * e, HD * (e + 1))
                            kv = t // (SWQ // 2)
                            w = s.rstrip("01")
                            if w not in ("rot", "score", "turn", "pv"):
                                continue
                            pe.wait_ge(window_stage, C.before(t, s))
                            if w == "rot":
                                pe.wait_ge(tile_stage, E.end(("swq", t)))
                                ins = pe.matmul(ps[:, 6, :], k_("rot"), qraw[:, t, :], start=True, stop=True)
                            elif w == "score":
                                for n in range(CH):
                                    qn = qr[rows, n * P:(n + 1) * P]
                                    bank, o = n // 2, (n % 2) * 2 * P
                                    if n == 0:
                                        ins = pe.matmul(psA[:, 0, P:2 * P], qn, kk[rows, kv, 0:P], start=True, stop=True)
                                    else:
                                        ins = pe.matmul(psA[:, bank, o:o + 2 * P], qn, kk[rows, kv, (n - 1) * P:(n + 1) * P],
                                                        start=True, stop=True)
                            elif w == "turn":
                                pT = psB.rearrange("p b (c n) -> p (b c) n", n=P)
                                for i in range(2 * CH - 1):
                                    n, half = (i + 1) // 2, (i + 1) % 2
                                    ins = pe.transpose(pT[:, i, :], prob[:, n, half * P:(half + 1) * P], ident)
                            else:
                                for n in range(CH):
                                    o = ps[rows, 7, n * P:(n + 1) * P]
                                    for half in ((0, 1) if n else (1,)):
                                        i = 2 * n + half - 1
                                        ins = pe.matmul(o, vtok[:, n - 1 + half, HD * kv:HD * (kv + 1)], probT[:, i, :],
                                                        start=(half == 0 or n == 0), stop=(half == 1))
                            ins.then_inc(window_stage, 1)
                        elif kind == "E" and s in ("rotk", "dupk", "turnv"):
                            pe.wait_ge(tile_stage, E.before(j, s))
                            if s == "rotk":
                                ins = pe.matmul(ps[:, 6, :], k_("rot"), tmp[:, :], start=True, stop=True)
                            elif s == "dupk":
                                pe.matmul(ps[:, 6, :], k_("dup0"), kr, start=True, stop=True)
                                ins = pe.matmul(ps[:, 7, :], k_("dup1"), kr, start=True, stop=True)
                            else:
                                for c in range(CH):
                                    ins = pe.transpose(ps[:, 6, c * P:(c + 1) * P], tmp[:, c * P:(c + 1) * P], ident)
                            ins.then_inc(tile_stage, 1)
                    pe.wait_ge(tile_stage, E.end(LT_TILES[-1]))
                    pe.matmul(ps[:, 7, :], k_("ones"), sq[:, 1, :], start=True, stop=True).then_inc(sum_done, 1)
            clear_all()

        par2 = at(par_at, 0, "par2", [P, NPARAM2])
        bmat = at(rope_at, 0, "bmat", [P, 2, SG, P])
        u = at(base_o, 0, "u", [P, SG, SEQ])
        za = at(base_o, 4 * TILE, "za", [P, SG, SEQ])
        turn_c = at(base_o, 8 * TILE, "turn_c", [P, 2, SEQ])
        turn_s = at(base_o, 10 * TILE, "turn_s", [P, 2, SEQ])
        turn_t = at(base_o, 12 * TILE, "turn_t", [P, SEQ])
        cmat = at(base_o, 13 * TILE, "cmat", [P, 2, ST, 32])
        big = at(base_o, 15 * TILE, "big", [P, 2, ST, TBH])
        craw = at(base_a, 0, "craw", [P, 2, ST, 32])
        ctmp = at(base_a, 2 * TILE, "ctmp", [P, 4, ST, 32])
        cols = at(base_a, 6 * TILE, "cols", [P, 20, ST])
        zb = at(base_r, 0, "zb", [P, SG, SEQ])
        t1, t2, zr, zi, sr, si = (at(base_r, (4 + i) * TILE, n, [P, SEQ]) for i, n in
                                  enumerate(("t1", "t2", "zr", "zi", "sr", "si")))
        mixed = at(base_r, 10 * TILE, "mixed", [P, SEQ])
        yaH, yaL = at(base_r, 0, "yaH", [P, SG, SEQ], F32R), at(base_r, 4 * TILE, "yaL", [P, SG, SEQ], F32R)
        sga_a, sga_b = at(base_s, 4 * TILE, "sga_a", [P, SG, SEQ]), at(base_s, 12 * TILE, "sga_b", [P, SG, SEQ])

        def sga(f):
            return (sga_a if f < SG else sga_b)[:, f % SG, :]

        def p2(name, i=None, n=1):
            a, b = PARAM2[name]
            return par2[:, a:b] if i is None else par2[:, a + i:a + i + n]

        mag = small[:, 0:ST]
        half_glu = small[:, ST:ST + SG]

        with nc.Block() as block:
            @block.sync
            def _(sp):
                sp.dma_start(par2[:, :], params2).then_inc(input_in, 16)
                sp.dma_start(bmat[:, :, :, :].rearrange("p a b c -> p (a b c)"), smallb).then_inc(input_in, 16)
                sp.dma_start(craw[:, :, :, :].rearrange("p a b c -> p (a b c)"), smallc).then_inc(input_in, 16)

            dt, ang, lr, ws, wc, k0, cr, ci, nr, ni, den2, q1, q2, q3, q4, cfr, cfi = (cols[:, i, :] for i in range(17))

            @block.scalar
            def _(act):
                act.wait_ge(input_in, 48)
                act.activation(dt, p2("log_dt"), ACT.Exp).then_inc(x_part, 1)
                act.wait_ge(setup, 2)
                act.activation(mag, lr, ACT.Exp).then_inc(x_part, 1)
                act.wait_ge(setup, 2 + 2 * RANGE_STEPS)
                act.activation(ci, ws, ACT.Sin).then_inc(x_part, 1)
                act.activation(cr, wc, ACT.Sin, bias=k_("halfpi")).then_inc(x_part, 1)

            @block.vector
            def _(v):
                step = [0]

                def link(ins):
                    step[0] += 1
                    ins.then_inc(setup, 1)
                    v.wait_ge(setup, step[0])

                def mul(o, a, b):
                    link(v.tensor_tensor(o, a, b, ALU.mult))

                v.wait_ge(x_part, 1)
                link(v.tensor_tensor(ang, p2("lam_im"), dt, ALU.mult))
                link(v.tensor_tensor(lr, p2("lam_re"), dt, ALU.mult))
                range_reduce(v, link, ws, ang, k0, 0.0)
                range_reduce(v, link, wc, ang, k0, 0.25)
                v.wait_ge(x_part, 4)
                link(v.tensor_scalar(half_glu, p2("b_glu"), 0.5, None, ALU.mult))
                mul(nr, mag, cr)
                link(v.tensor_scalar(nr, nr, 1.0, None, ALU.subtract))
                mul(ni, mag, ci)
                mul(q1, p2("lam_re"), p2("lam_re"))
                mul(q2, p2("lam_im"), p2("lam_im"))
                link(v.tensor_tensor(den2, q1, q2, ALU.add))
                link(v.reciprocal(den2, den2))
                mul(q1, nr, p2("lam_re"))
                mul(q2, ni, p2("lam_im"))
                link(v.tensor_tensor(cfr, q1, q2, ALU.add))
                mul(cfr, cfr, den2)
                mul(q1, ni, p2("lam_re"))
                mul(q2, nr, p2("lam_im"))
                link(v.tensor_tensor(cfi, q1, q2, ALU.subtract))
                mul(cfi, cfi, den2)
                wide = lambda a: a.unsqueeze(2).to_broadcast([P, ST, 32])
                mul(ctmp[:, 0], craw[:, 0], wide(cfr))
                mul(ctmp[:, 1], craw[:, 1], wide(cfi))
                mul(ctmp[:, 2], craw[:, 1], wide(cfr))
                mul(ctmp[:, 3], craw[:, 0], wide(cfi))
                link(v.tensor_tensor(cmat[:, 0], ctmp[:, 0], ctmp[:, 1], ALU.subtract))
                link(v.scalar_tensor_tensor(out=cmat[:, 1], in0=ctmp[:, 2], scalar=-1.0, in1=ctmp[:, 3],
                                            op0=ALU.mult, op1=ALU.subtract))
                for table, n in ((turn_small, TBL), (big, TBH)):
                    link(v.memset(table[:, 0, :, 0:1], 1.0))
                    link(v.memset(table[:, 1, :, 0:1], 0.0))
                    k = 1
                    while k < n:
                        a, b = table[:, 0, :, 0:k], table[:, 1, :, 0:k]
                        c = cr.unsqueeze(2).to_broadcast([P, ST, k])
                        d = ci.unsqueeze(2).to_broadcast([P, ST, k])
                        w = [ctmp[:, i, :, 0:k] for i in range(4)]
                        mul(w[0], a, c)
                        mul(w[1], b, d)
                        mul(w[2], a, d)
                        mul(w[3], b, c)
                        link(v.tensor_tensor(table[:, 0, :, k:2 * k], w[0], w[1], ALU.subtract))
                        link(v.tensor_tensor(table[:, 1, :, k:2 * k], w[2], w[3], ALU.add))
                        mul(q1, cr, cr)
                        mul(q2, ci, ci)
                        mul(q3, cr, ci)
                        link(v.tensor_tensor(cr, q1, q2, ALU.subtract))
                        link(v.tensor_scalar(ci, q3, 2.0, None, ALU.mult))
                        k *= 2
        clear_all()

        with nc.Block() as block:
            @block.sync
            def _(sp):
                for j in range(len(S_TILES)):
                    if j >= RAW:
                        sp.wait_ge(low_done, j - RAW + 1)
                    sp.dma_start(raw[:, j % RAW, :, :].rearrange("p t n -> p (t n)"), w2[j]).then_inc(loaded[j % RAW], 16)

            @block.gpsimd
            def _(pool):
                for kind, j, s in S_ORDER:
                    if kind == "split":
                        split_low(pool, j)
                    elif kind == "T":
                        pool.wait_ge(table_stage, T.before(j, s))
                        if s == "coscos" and j >= 2:
                            pool.wait_ge(state_stage, SS.before(j - 2, "state") + 1)
                        cc, ss, tt = turn_c[:, j % 2, :], turn_s[:, j % 2, :], turn_t[:, :]
                        grid = lambda ap: ap.rearrange("p (a b) -> p a b", b=TBL)
                        hi = lambda i: big[:, i, j, :].unsqueeze(2).to_broadcast([P, TBH, TBL])
                        lo = lambda i: turn_small[:, i, j, :].unsqueeze(1).to_broadcast([P, TBH, TBL])
                        if s == "coscos":
                            ins = pool.tensor_tensor(grid(cc), hi(0), lo(0), ALU.mult)
                        elif s == "sinsin":
                            ins = pool.tensor_tensor(grid(tt), hi(1), lo(1), ALU.mult)
                        elif s == "cos":
                            ins = pool.tensor_tensor(cc, cc, tt, ALU.subtract)
                        elif s == "cossin":
                            ins = pool.tensor_tensor(grid(ss), hi(0), lo(1), ALU.mult)
                        elif s == "sincos":
                            ins = pool.tensor_tensor(grid(tt), hi(1), lo(0), ALU.mult)
                        else:
                            ins = pool.tensor_tensor(ss, ss, tt, ALU.add)
                        ins.then_inc(table_stage, 1)
                    elif kind == "E" and j[0] == "ub" and s == "low":
                        pool.wait_ge(tile_stage, E2.before(j, s))
                        i = j[1]
                        pool.tensor_tensor(SL[:, SG + i, :], mixed[:, :], SH[:, SG + i, :].bitcast(F32),
                                           ALU.subtract).then_inc(tile_stage, 1)

            @block.scalar
            def _(act):
                def high(j):
                    act.wait_ge(loaded[j % RAW], 16 * (j // RAW + 1))
                    if j >= SPLIT:
                        act.wait_ge(tile_done, S_OUT_AT[outputs_of(S_TILES[j - SPLIT])[-1]] + 1)
                    act.activation(wH[:, j % SPLIT, :, :], raw[:, j % RAW, :, :], ACT.Copy).then_inc(high_done, 1)

                high(0)
                x_high(act, lambda t: p2("norm", t), 0, None)
                root_scalar(act, ssq_done, KT, rstd[:, :], ps[:, 7, :], 1.0 / D_MODEL, "eps", root_done)
                for kind, j, s in S_ORDER[1:]:
                    if kind == "split":
                        high(j)
                    elif kind == "S" and s in ("gelu", "highs"):
                        act.wait_ge(state_stage, SS.before(j, s))
                        if s == "gelu":
                            act.activation(u[:, j // 4, :], u[:, j // 4, :], ACT.Gelu_apprx_tanh).then_inc(state_stage, 1)
                        else:
                            act.wait_ge(tile_stage, E2.end(("bb", KT - 1)))
                            act.activation(SH[:, 0:SG, :], u[:, :, :], ACT.Copy).then_inc(state_stage, 1)
                    elif kind == "E" and s in ("tanh", "high", "square"):
                        kd_, i = j
                        act.wait_ge(tile_stage, E2.before(j, s))
                        if kd_ == "glu" and s == "tanh":
                            n = S_OUT_AT[j]
                            act.wait_ge(tile_done, n + 1)
                            ins = act.activation(tmp[:, :], ps[:, n % 2, :], ACT.Tanh, scale=0.5, bias=half_glu[:, i:i + 1])
                        elif s == "tanh" and kd_ in ("za", "zb"):
                            ins = act.activation(tmp[:, :], (za if kd_ == "za" else zb)[:, i, :], ACT.Tanh, scale=0.5)
                        elif s == "tanh":
                            g = acc[:, i, :] if kd_ == "gb" else sga(i)
                            ins = act.activation(g, g, ACT.Tanh, scale=0.5)
                        elif s == "high":
                            dst, f = {"ub": (SH[:, (SG + i) % KT, :], 1.0), "pw": (SH[:, i, :], 0.5),
                                      "glu": (yaH[:, i % SG, :], 0.25), "ba": (OH[:, i, :], 0.5)}[kd_]
                            ins = act.activation(dst, mixed[:, :], ACT.Copy, scale=f)
                        else:
                            ins = act.activation(sq[:, 0, :], x[:, i, :], ACT.Square)
                        ins.then_inc(tile_stage, 1)
                root_scalar(act, sum_done, 1, rstdp[:, :], ps[:, 7, :], 1.0 / D_MODEL, "eps", post_root)

            @block.vector
            def _(v):
                for t in range(KT):
                    x_low(v, t, lambda t: p2("norm", t), 0)
                v.wait_ge(root_done, 1)
                v.reciprocal(rstd[:, :], rstd[:, :]).then_inc(rstd_ready, 1)
                v.wait_ge(rstd_ready, 1)
                for kind, j, s in S_ORDER[1:]:
                    if kind == "S" and s not in ("input", "output", "gelu", "highs"):
                        v.wait_ge(state_stage, SS.before(j, s))
                        cc, ss = turn_c[:, j % 2, :], turn_s[:, j % 2, :]
                        mul = lambda o, a, b: v.tensor_tensor(o[:, :], a, b, ALU.mult)
                        if s == "turn":
                            v.wait_ge(table_stage, T.end(j))
                            mul(t1, cc, psA[:, 0, :])
                            mul(t2, ss, psA[:, 1, :])
                            mul(sr, cc, psA[:, 1, :])
                            ins = mul(si, ss, psA[:, 0, :])
                        elif s == "turned":
                            v.tensor_tensor(zr[:, :], t1[:, :], t2[:, :], ALU.add)
                            ins = v.tensor_tensor(zi[:, :], sr[:, :], si[:, :], ALU.subtract)
                        elif s == "scan":
                            decay = mag[:, j:j + 1].to_broadcast([P, SEQ])
                            v.tensor_tensor_scan(t1[:, :], decay, zr[:, :], 0.0, ALU.mult, ALU.add)
                            ins = v.tensor_tensor_scan(t2[:, :], decay, zi[:, :], 0.0, ALU.mult, ALU.add)
                        elif s == "back":
                            mul(zr, cc, t1[:, :])
                            mul(zi, ss, t2[:, :])
                            mul(sr, cc, t2[:, :])
                            ins = mul(si, ss, t1[:, :])
                        elif s == "state":
                            v.tensor_tensor(zr[:, :], zr[:, :], zi[:, :], ALU.subtract)
                            ins = v.tensor_tensor(sr[:, :], sr[:, :], si[:, :], ALU.add)
                        elif s == "skip":
                            c = j // 4
                            ins = v.scalar_tensor_tensor(out=u[:, c, :], in0=u[:, c, :], scalar=p2("d", c),
                                                         in1=ps[:, 4, :], op0=ALU.mult, op1=ALU.add)
                        else:
                            ins = v.tensor_tensor(SL[:, 0:SG, :], u[:, :, :], SH[:, 0:SG, :].bitcast(F32), ALU.subtract)
                        ins.then_inc(state_stage, 1)
                    elif kind == "E":
                        kd_, i = j
                        n = S_OUT_AT[j]
                        b = ps[:, n % 2, :]
                        if s in ("tanh", "high", "square") or (kd_ == "ub" and s == "low"):
                            continue
                        v.wait_ge(tile_stage, E2.before(j, s))
                        if s == e2_stages(j)[0]:
                            v.wait_ge(tile_done, n + 1)
                        if s in ("scale", "bias") and kd_ != "pw":
                            dst = {"ua": lambda: u[:, i, :], "za": lambda: za[:, i, :], "ub": lambda: tmp[:, :],
                                   "zb": lambda: zb[:, i, :], "gb": lambda: acc[:, i, :], "ga": lambda: sga(i)}[kd_]()
                            if s == "scale":
                                ins = v.tensor_tensor(dst, b, rstd[:, :], ALU.mult)
                            else:
                                ins = v.tensor_scalar(dst, dst, p2("b_in", IN2[kd_] + i), None, ALU.add)
                        elif s == "silu" and kd_ != "glu":
                            z = (za if kd_ == "za" else zb)[:, i, :]
                            ins = v.scalar_tensor_tensor(out=z, in0=tmp[:, :], scalar=1.0, in1=z, op0=ALU.add, op1=ALU.mult)
                        elif s.startswith("sum") and kd_ == "ub":
                            m = int(s[-1])
                            d = 2 ** m
                            src = tmp if m == 0 else sq[:, (m - 1) % 2, :]
                            dst = sq[:, m % 2, :]
                            v.tensor_copy(dst[:, 0:d], src[:, 0:d])
                            ins = v.tensor_tensor(dst[:, d:], src[:, d:SEQ], src[:, 0:SEQ - d], ALU.add)
                        elif s == "mean":
                            win = 2 ** (i + 1)
                            src = sq[:, i % 2, :]
                            v.scalar_tensor_tensor(out=mixed[:, :], in0=src, scalar=1.0 / win, in1=tmp[:, :],
                                                   op0=ALU.mult, op1=ALU.subtract)
                            ins = v.tensor_tensor(small[:, 32:32 + win], src[:, 0:win], k_("invcount")[:, 0:win], ALU.mult)
                        elif s == "early":
                            win = 2 ** (i + 1)
                            ins = v.tensor_tensor(mixed[:, 0:win], small[:, 32:32 + win], tmp[:, 0:win], ALU.subtract)
                        elif kd_ == "pw" and s == "scale":
                            ins = v.scalar_tensor_tensor(out=mixed[:, :], in0=b, scalar=p2("pool_scale", i), in1=zb[:, i, :],
                                                         op0=ALU.mult, op1=ALU.mult)
                        elif s == "low":
                            f, hi_, dst = {"pw": (0.5, SH[:, i, :], SL[:, i, :]), "glu": (0.25, yaH[:, i % SG, :], yaL[:, i % SG, :]),
                                           "ba": (0.5, OH[:, i, :], OL[:, i, :])}[kd_]
                            ins = v.scalar_tensor_tensor(out=dst, in0=mixed[:, :], scalar=f, in1=hi_.bitcast(F32),
                                                         op0=ALU.mult, op1=ALU.subtract)
                        elif s == "gate" and kd_ == "bb":
                            ins = v.scalar_tensor_tensor(out=acc[:, i, :], in0=acc[:, i, :], scalar=1.0, in1=b, op0=ALU.add, op1=ALU.mult)
                        elif s == "gate" and kd_ == "glu":
                            ins = v.scalar_tensor_tensor(out=tmp[:, :], in0=tmp[:, :], scalar=1.0, in1=u[:, i, :], op0=ALU.add, op1=ALU.mult)
                        elif s == "silu":
                            ins = v.tensor_tensor(mixed[:, :], tmp[:, :], za[:, i, :], ALU.mult)
                        elif s == "gate":
                            ins = v.scalar_tensor_tensor(out=mixed[:, :], in0=sga(i), scalar=1.0, in1=b, op0=ALU.add, op1=ALU.mult)
                        elif s == "add" and kd_ == "ba":
                            ins = v.tensor_tensor(mixed[:, :], mixed[:, :], acc[:, i, :], ALU.add)
                        elif s == "add":
                            ins = v.tensor_tensor(x[:, i, :], x[:, i, :], b, ALU.add)
                        elif s == "sum" and i == 0:
                            ins = v.tensor_copy(sq[:, 1, :], sq[:, 0, :])
                        else:
                            ins = v.tensor_tensor(sq[:, 1, :], sq[:, 1, :], sq[:, 0, :], ALU.add)
                        ins.then_inc(tile_stage, 1)
                v.wait_ge(post_root, 1)
                v.reciprocal(rstdp[:, :], rstdp[:, :]).then_inc(post_ready, 1)
                v.wait_ge(post_ready, 1)
                for t in range(KT):
                    v.scalar_tensor_tensor(out=acc[:, t, :], in0=x[:, t, :], scalar=p2("final", t), in1=rstdp[:, :],
                                           op0=ALU.mult, op1=ALU.mult).then_inc(x_ready, 1)

            @block.tensor
            def _(pe):
                for kind, j, s in S_ORDER:
                    if kind == "mm":
                        tile = S_TILES[j]
                        kd_, i = tile
                        outs = outputs_of(tile)
                        each = PARTS // len(outs)
                        o, part = outs[s // each], s % each
                        n = S_OUT_AT[o]
                        depth = S_DEPTH.get(kd_, KT)
                        if s == 0:
                            pe.wait_ge(low_done, j + 1)
                        if part == 0 and n >= 2:
                            pe.wait_ge(tile_stage, E2.before(S_OUT[n - 2], e2_stages(S_OUT[n - 2])[0]) + 1)
                        if s == 0:
                            if kd_ == "pw":
                                pe.wait_ge(tile_stage, E2.end(("ub", SG - 1)))
                            if tile == ("bb", 0):
                                pe.wait_ge(tile_stage, E2.end(("pw", SG - 1)))
                            if tile == ("glu", 0):
                                pe.wait_ge(state_stage, SS.end(ST - 1))
                            if tile == ("ba", 0):
                                pe.wait_ge(tile_stage, E2.end(("glu", SG - 1)))
                            if tile == ("wo", 0):
                                pe.wait_ge(tile_stage, E2.end(("ba", KT - 1)))
                        rH, rL = {"pw": lambda: (SH[:, SG + o[1]:, :], SL[:, SG + o[1]:, :]), "bb": lambda: (SH, SL),
                                  "glu": lambda: (SH, SL), "ba": lambda: (yaH, yaL),
                                  "wo": lambda: (OH, OL)}.get(kd_, lambda: (hH, hL))()
                        before = None
                        if tile == ("ua", 0):
                            def before(t):
                                pe.wait_ge(h_low, t + 1)
                                x_sum(pe, 0, t)
                        products(pe, j, part, ps[:, n % 2, :], rH, rL, depth, kt0=(s // each) * depth, parts=each,
                                 before=before)
                    elif kind == "S" and s in ("input", "output"):
                        pe.wait_ge(state_stage, SS.before(j, s))
                        c, r = j // 4, slice(32 * (j % 4), 32 * (j % 4 + 1))
                        if s == "input":
                            if j % 4 == 0:
                                pe.wait_ge(tile_stage, E2.end(("ua", c)))
                            pe.matmul(psA[:, 0, :], bmat[r, 0, c, :], u[r, c, :], start=True, stop=True)
                            ins = pe.matmul(psA[:, 1, :], bmat[r, 1, c, :], u[r, c, :], start=True, stop=True)
                        else:
                            pe.matmul(ps[r, 4, :], cmat[:, 0, j, :], zr[:, :], start=True, stop=False)
                            ins = pe.matmul(ps[r, 4, :], cmat[:, 1, j, :], sr[:, :], start=False, stop=True)
                        ins.then_inc(state_stage, 1)
                pe.wait_ge(tile_stage, E2.end(("wo", KT - 1)))
                pe.matmul(ps[:, 7, :], k_("ones"), sq[:, 1, :], start=True, stop=True).then_inc(sum_done, 1)
        with nc.Block() as block:
            @block.sync
            def _(sp):
                sp.dma_start(outT, acc[:, :, :]).then_inc(out_done, 16)
                sp.wait_ge(out_done, 16)


RANGE_STEPS = 6


def range_reduce(v, link, out, ang, k, quarter):
    two_pi = 2 * np.pi
    p1 = 6.28125
    p2 = float(np.float32(0.00193500518798828125))
    p3 = float(np.float32(two_pi - p1 - p2))
    magic = 1.5 * 2.0 ** 23
    link(v.tensor_scalar(k, ang, 1.0 / two_pi, quarter, ALU.mult, ALU.add))
    link(v.tensor_scalar(k, k, magic, None, ALU.add))
    link(v.tensor_scalar(k, k, magic, None, ALU.subtract))
    link(v.scalar_tensor_tensor(out=out, in0=k, scalar=-p1, in1=ang, op0=ALU.mult, op1=ALU.add))
    link(v.scalar_tensor_tensor(out=out, in0=k, scalar=-p2, in1=out, op0=ALU.mult, op1=ALU.add))
    link(v.scalar_tensor_tensor(out=out, in0=k, scalar=-p3, in1=out, op0=ALU.mult, op1=ALU.add))


def kernel(**inputs):
    import concourse.bacc as bacc
    from concourse.bass_utils import run_bass_kernel_spmd

    a = {n: np.asarray(v) for n, v in inputs.items()}

    def tiles(w, depth=KT):
        n = w.shape[-1] // P
        return w.reshape(depth, P, n, P).transpose(2, 1, 0, 3).reshape(n, P, depth * P)

    def columns(g):
        return g.reshape(-1, P).T

    def every(g):
        return np.broadcast_to(g[None, :], (P, g.size))

    w1, params = [], []
    for l in range(DEPTH):
        wi = a["w_in"][l]
        o = np.cumsum([0, 1024, 1024, 1024, 1024, 16, 1024, 128, 128, 1024, 1024])
        t = {n: tiles(wi[:, o[i]:o[i + 1]]) for i, n in enumerate(("q", "k", "v", "z", None, "swq", "swk", "swv", "ga", "gb")) if n}
        ab = np.zeros((P, KT, P), np.float32)
        ab[:, :, 0:16] = wi[:, o[4]:o[5]].reshape(KT, P, 16).transpose(1, 0, 2)
        t["ab"] = ab.reshape(1, P, D_MODEL)
        t["ya"], t["yb"], t["wo"] = (tiles(a[n][l]) for n in ("w_up_dn", "w_up_sw", "w_o"))
        t["f1"] = tiles(a["w_ff1"][l])
        t["f2"] = np.concatenate([tiles(a["w_ff2"][l][c * D_MODEL:(c + 1) * D_MODEL]) for c in range(FFC)])
        w1.append(np.stack([t[k][i] for k, i in LT_TILES]))
        conv = a["dn_conv_w"][l].reshape(CONV, 3 * HEADS, P).transpose(2, 1, 0).reshape(P, -1)
        params.append(np.concatenate([columns(a[n][l]) for n in ("pre_mix_g", "post_mix_g", "pre_mlp_g", "post_mlp_g")]
                                     + [conv, a["dn_norm_g"][l][:, None], every(a["dn_a_log"][l]),
                                        every(a["dn_dt_bias"][l]), every(a["sw_sinks"][l])], axis=1))
    w = a["w_in_2"][0]
    t = {k: tiles(w[:, P * i:P * (i + n)]) for k, i, n in (("ua", IN2["ua"], SG), ("za", IN2["za"], SG), ("ub", IN2["ub"], SG),
                                                           ("zb", IN2["zb"], SG), ("ga", IN2["ga"], KT), ("gb", IN2["gb"], KT))}

    def pairs(w):
        h = tiles(w, SG)
        return h.reshape(-1, 2, P, SG * P).transpose(0, 2, 1, 3).reshape(-1, P, 2 * SG * P)

    t["bb"], t["ba"], t["glu"] = pairs(a["w_branch_b_2"][0]), pairs(a["w_branch_a_2"][0]), pairs(a["ssm_w_glu_2"][0])
    t["pw"] = np.zeros((1, P, D_MODEL), np.float32)
    t["pw"][0, :, 0:SG * P] = a["pool_w_2"][0].transpose(1, 0, 2).reshape(P, SG * P)
    t["wo"] = tiles(a["w_out_2"][0])
    states = lambda v: v.reshape(ST, P).T
    log_dt = np.broadcast_to(a["ssm_log_dt_2"][0][:, None], (2 * ST, P // 2))
    params2 = np.concatenate([columns(a[n][0]) for n in ("norm_g_2",)] + [columns(a["final_norm_g_2"])]
                             + [columns(a[n][0]) for n in ("b_in_2", "ssm_d_2", "ssm_b_glu_2", "pool_scale_2")]
                             + [states(a["ssm_lam_re_2"][0]), states(a["ssm_lam_im_2"][0]), states(log_dt)], axis=1)
    smallb = np.zeros((2, P, SG, P), np.float32)
    smallc = np.zeros((2, P, ST, 32), np.float32)
    for i, (nb, ncm) in enumerate((("ssm_b_re_2", "ssm_c_re_2"), ("ssm_b_im_2", "ssm_c_im_2"))):
        for g in range(2 * ST):
            st, e = g // 2, g % 2
            row, col = 32 * (st % 4) + 16 * e, 64 * e
            smallb[i, row:row + 16, st // 4, col:col + 64] = a[nb][0, g].T
            smallc[i, col:col + 64, st, 16 * e:16 * e + 16] = a[ncm][0, g].T
    data = {
        "w2": np.stack([t[k][i] for k, i in S_TILES]),
        "params2": params2,
        "smallb": smallb.transpose(1, 0, 2, 3).reshape(P, -1),
        "smallc": smallc.transpose(1, 0, 2, 3).reshape(P, -1),
        "xT": a["x"][0].T.reshape(KT, P, SEQ).transpose(1, 0, 2),
        "pos": a["positions"].reshape(1, SEQ),
        "consts": constants(),
        "params": np.stack(params),
        "w1": np.stack(w1),
    }
    nc = bacc.Bacc("TRN2", target_bir_lowering=False, num_devices=1)
    data = {n: np.ascontiguousarray(v) for n, v in data.items()}
    aps = {n: nc.dram_tensor(n, v.shape, mybir.dt.from_np(v.dtype), kind="ExternalInput").ap() for n, v in data.items()}
    outT = nc.dram_tensor("outT", (P, KT, SEQ), F32, kind="ExternalOutput").ap()
    build(nc, aps["xT"], aps["pos"], aps["consts"], aps["params"], aps["w1"], aps["w2"], aps["params2"],
          aps["smallb"], aps["smallc"], outT)
    r = run_bass_kernel_spmd(nc, [data], core_ids=[0])
    got = r.results[0]["outT"]
    return got.transpose(1, 0, 2).reshape(1, D_MODEL, SEQ).transpose(0, 2, 1)
```

```python
from contextlib import ExitStack

import numpy as np
import concourse.bass as bass
from concourse import mybir

F32 = mybir.dt.float32
F32R = mybir.dt.float32r
I32 = mybir.dt.int32
ALU = mybir.AluOpType
ACT = mybir.ActivationFunctionType
AX = mybir.AxisListType

P = 128
SEQ, D_MODEL, DEPTH, D_FF = 512, 1024, 2, 4096
KT = D_MODEL // P
HEADS, CONV = 8, 4
CH = SEQ // P
SWQ = 8
HD = 64
FFC = D_FF // D_MODEL
EPS = 1e-6
NEG = -1e30
LEVELS = (2, 4, 8, 16, 32, 64)
SG = 4
ST = 16
TBL = 32
TBH = SEQ // TBL
PARTS = 8

def layer_tiles():
    out = [("ab", 0)]
    for h in range(HEADS):
        out += [("q", h), ("k", h), ("v", h), ("z", h)]
    out += [("swk", 0), ("swv", 0)] + [("swq", t) for t in range(SWQ)]
    for f in range(KT):
        out += [("ga", f), ("ya", f)]
    for f in range(KT):
        out += [("gb", f), ("yb", f)]
    out += [("wo", f) for f in range(KT)]
    up = lambda c: [("f1", 8 * c + j) for j in range(8)]
    down = lambda c: [("f2", 8 * c + j) for j in range(8)]
    out += up(0)
    for c in range(1, FFC):
        out += up(c) + down(c - 1)
    return out + down(FFC - 1)


def second_tiles():
    out = [("ua", i) for i in range(SG)] + [("za", i) for i in range(SG)]
    out += [("ub", i) for i in range(SG)] + [("zb", i) for i in range(SG)] + [("pw", 0)]
    out += [("gb", f) for f in range(KT)] + [("bb", i) for i in range(KT // 2)]
    out += [("ga", f) for f in range(KT - 1)] + [("glu", i) for i in range(SG // 2)] + [("ga", KT - 1)]
    return out + [("ba", i) for i in range(KT // 2)] + [("wo", f) for f in range(KT)]


OUTS = {"pw": SG, "bb": 2, "glu": 2, "ba": 2}
S_DEPTH = {"pw": 1, "bb": SG, "glu": SG, "ba": SG}


def outputs_of(tile):
    kind, i = tile
    n = OUTS.get(kind, 1)
    return [(kind, n * i + o) for o in range(n)]


LT_TILES = layer_tiles()
L_AT = {t: i for i, t in enumerate(LT_TILES)}
S_TILES = second_tiles()
S_AT = {t: i for i, t in enumerate(S_TILES)}

CONST = {}
_at = 0
for _name, _n in [("ident", P), ("ones", P), ("upper", P), ("first", P), ("levels", P * len(LEVELS)), ("rot", P),
                  ("dup0", P), ("dup1", P), ("window", 2 * P), ("invfreq", 1), ("isrot", 1), ("notrot", 1),
                  ("eps", 1), ("eps4", 1), ("halfpi", 1), ("invcount", 16)]:
    CONST[_name] = (_at, _at + _n)
    _at += _n
NCONST = _at

PARAM = {}
_at = 0
for _name, _n in [("pre_mix", KT), ("post_mix", KT), ("pre_mlp", KT), ("post_mlp", KT), ("conv", CONV * 3 * HEADS),
                  ("norm", 1), ("a_log", HEADS), ("dt_bias", HEADS), ("sinks", 2 * SWQ)]:
    PARAM[_name] = (_at, _at + _n)
    _at += _n
NPARAM = _at


PARAM2 = {}
_at = 0
for _name, _n in [("norm", KT), ("final", KT), ("b_in", D_MODEL * 4 // P), ("d", SG), ("b_glu", SG), ("pool_scale", SG),
                  ("lam_re", ST), ("lam_im", ST), ("log_dt", ST)]:
    PARAM2[_name] = (_at, _at + _n)
    _at += _n
NPARAM2 = _at
IN2 = {"ua": 0, "za": SG, "ub": 2 * SG, "zb": 3 * SG, "ga": 4 * SG, "gb": 4 * SG + KT}


def constants():
    c = np.zeros((P, NCONST), np.float32)
    i, j = np.arange(P)[:, None], np.arange(P)[None, :]

    def put(name, v):
        c[:, CONST[name][0]:CONST[name][1]] = v

    put("ident", i == j)
    put("ones", 1.0)
    put("upper", i <= j)
    put("first", (i % 2 == 0) & (j == i + 1))
    put("levels", np.concatenate([(i // (2 * s) == j // (2 * s)) & (i % (2 * s) >= s) & (j % (2 * s) < s)
                                  for s in LEVELS], axis=1))
    r = i % HD
    half = HD // 8
    rj = j % HD
    put("rot", -1.0 * ((rj < half) & (i == j + half)) + 1.0 * ((rj >= half) & (rj < 2 * half) & (i == j - half)))
    put("dup0", i == j % HD)
    put("dup1", i == j % HD + HD)
    q, k = np.arange(P)[:, None] + P, np.arange(2 * P)[None, :]
    put("window", np.where((q - k >= 0) & (q - k < P), 0.0, NEG))
    p = np.arange(P)[:, None]
    inv = np.float32(500000.0) ** (-(p % half).astype(np.float32) * np.float32(2.0 / (2 * half)))
    put("invfreq", np.where(p % HD < 2 * half, inv, 0.0))
    put("isrot", p % HD < 2 * half)
    put("notrot", p % HD >= 2 * half)
    put("eps", EPS)
    put("eps4", 4 * EPS)
    put("halfpi", np.pi / 2)
    put("invcount", 1.0 / np.arange(1, 17)[None, :])
    return c


class Count:

    def __init__(self, rounds):
        self.value = {}
        n = 0
        for key, stages in rounds:
            for s in stages:
                self.value[key, s] = n
                n += 1
            self.value[key, "end"] = n

    def before(self, key, stage):
        return self.value[key, stage]

    def end(self, key):
        return self.value[key, "end"]


E_STAGES = {
    "ab": ["scale"],
    "q": ["scale", "tap3", "tap2", "tap1", "tap0", "tanh", "silu"],
    "z": ["scale", "tanh", "silu"],
    "swk": ["scale", "cosk", "rotk", "sink", "addk", "dupk", "copyk"],
    "swv": ["scale", "turnv", "copyv"],
    "swq": ["scale"],
    "ga": ["scale", "tanh"],
    "ya": ["gate"],
    "yb": ["gate", "add", "high", "low"],
    "wo": ["copy", "square", "sum"],
    "f1": ["scale", "relu2", "high", "low"],
}
E_STAGES["k"] = E_STAGES["v"] = E_STAGES["q"]
E_STAGES["gb"] = E_STAGES["ga"]


def e_stages(tile):
    kind, i = tile
    if kind == "f2":
        return (["copy"] if i < 8 else ["add"]) + (["square", "sum"] if i >= 8 * (FFC - 1) else [])
    return E_STAGES[kind]


G_STAGES = ["turn", "copy", "tanh", "beta", "hbeta", "addb", "max", "abs", "expn", "plus1", "ln", "sp", "expa", "g",
            "cumsum", "copyc", "diff", "exps", "nbeg"]
D_STAGES = ["square", "sums", "root", "recip", "scales", "rows", "kbeta", "diff", "exps", "qdec", "mask", "gram",
            "masked", "first", "minus", "turnkv", "copykv"]
A_STAGES = ["turni", "copyi"] + [f"{s}{v}" for v in range(len(LEVELS))
                                 for s in (["p", "pmask", "q", "update"] + (["turn", "copy"] if v < len(LEVELS) - 1 else []))]
B_STAGES = (["v0", "copyv0", "o0", "state0"]
            + [f"{s}{c}" for c in range(1, CH)
               for s in (["r", "rr", "v", "copyv", "o"] + (["state"] if c < CH - 1 else []))]
            + ["square", "sums", "mean", "root", "recip", "factor", "row", "norm", "high", "low"])
C_STAGES = (["rot", "cos", "sin", "addq"]
            + [f"{s}{e}" for e in range(2)
               for s in ("score", "mask", "max", "maxs", "neg", "exp", "den", "recip", "prob", "turn", "copy", "pv")]
            + ["high", "low"])

E = Count([(t, e_stages(t)) for t in LT_TILES])
G = Count([(0, G_STAGES)])
A = Count([(h, A_STAGES) for h in range(HEADS)])
B = Count([(h, B_STAGES) for h in range(HEADS)])
D = Count([(h, D_STAGES) for h in range(HEADS)])
C = [Count([(t, C_STAGES) for t in range(e, SWQ, 2)]) for e in range(2)]


def layer_order():
    out = []

    def tile(j, beside=(), reads_last=False):
        t = LT_TILES[j]
        behind = [("E", LT_TILES[j - 1], s) for s in e_stages(LT_TILES[j - 1])] if j else []
        if j and t in (("wo", 0), ("f2", 8 * (FFC - 1))):
            out.extend(behind)
            behind = []
        if j + 1 < len(LT_TILES):
            out.append(("split", j + 1, None))
        for p in range(PARTS):
            out.append(("mm", j, p))
            half = PARTS // 2
            if p < half:
                out.extend(behind[len(behind) * p // half:len(behind) * (p + 1) // half])
            a = half - 1 if reads_last else 0
            if p >= a:
                out.extend(beside[len(beside) * (p - a) // (PARTS - a):len(beside) * (p + 1 - a) // (PARTS - a)])

    out.append(("split", 0, None))
    tile(0)
    j = 1
    merged = lambda chains, k, n: [s for c in chains for s in c[len(c) * k // n:len(c) * (k + 1) // n]]
    for slot in range(HEADS + 3):
        chains = [[(name, slot - lag, s) for s in stages] for name, stages, lag in
                  (("B", B_STAGES, 3), ("A", A_STAGES, 2), ("D", D_STAGES, 1)) if 0 <= slot - lag < HEADS]
        if slot == 0:
            chains = [[("G", 0, s) for s in G_STAGES]]
        n = {HEADS: 1, HEADS + 1: 5, HEADS + 2: 4}.get(slot, 4)
        steps = [merged(chains, k, 48) for k in range(48)]
        for i in range(n):
            if slot == 0:
                a, b = (0, 0) if i == 0 else (48 * (i - 1) // (n - 1), 48 * i // (n - 1))
            else:
                a, b = 48 * i // n, 48 * (i + 1) // n
            tile(j, [x for k in range(a, b) for x in steps[k]], reads_last=(i == 0))
            j += 1
    first = L_AT["ga", 0]
    assert j == first
    even, odd = ([("C", t, s) for t in range(e, SWQ, 2) for s in C_STAGES] for e in range(2))
    lag = len(C_STAGES) // 2
    c = []
    for k in range(len(even) + lag):
        c += even[k:k + 1] + (odd[k - lag:k - lag + 1] if k >= lag else [])
    n = L_AT["gb", 0] - first
    while j < len(LT_TILES):
        i = j - first
        tile(j, c[len(c) * i // n:len(c) * (i + 1) // n] if i < n else (), reads_last=(i == 0))
        j += 1
    out.extend([("E", LT_TILES[-1], s) for s in e_stages(LT_TILES[-1])])
    return out


L_ORDER = layer_order()

def e2_stages(out):
    kind, i = out
    if kind == "ub":
        return (["scale", "bias"] + [f"sum{m}" for m in range(i + 1)] + ["mean", "early", "high", "low"])
    return {"ua": ["scale", "bias"], "za": ["scale", "bias", "tanh", "silu"], "zb": ["scale", "bias", "tanh", "silu"],
            "pw": ["scale", "high", "low"], "gb": ["scale", "bias", "tanh"], "ga": ["scale", "bias", "tanh"],
            "bb": ["gate"], "glu": ["tanh", "gate", "silu", "high", "low"], "ba": ["gate", "add", "high", "low"],
            "wo": ["add", "square", "sum"]}[kind]


T_STAGES = ["coscos", "sinsin", "cos", "cossin", "sincos", "sin"]
SS_BASE = ["input", "turn", "turned", "scan", "back", "state", "output"]


def s_stages(st):
    return (SS_BASE + (["skip", "gelu"] if st % 4 == 3 else []) + (["highs", "lows"] if st == ST - 1 else []))


E2 = Count([(o, e2_stages(o)) for t in S_TILES for o in outputs_of(t)])
T = Count([(st, T_STAGES) for st in range(ST)])
SS = Count([(st, s_stages(st)) for st in range(ST)])
S_OUT = [o for t in S_TILES for o in outputs_of(t)]
S_OUT_AT = {o: n for n, o in enumerate(S_OUT)}


def second_order():
    out = [("split", 0, None)]
    first, last = S_AT["za", 0], S_AT["glu", 0]
    s = [("T", 0, t) for t in T_STAGES]
    for st in range(ST):
        tables = [("T", st + 1, t) for t in T_STAGES] if st + 1 < ST else []
        mine = [("S", st, t) for t in s_stages(st)]
        for i, m in enumerate(mine):
            s.append(m)
            s += tables[len(tables) * i // len(mine):len(tables) * (i + 1) // len(mine)]
    behind = []
    for j, t in enumerate(S_TILES):
        if j + 1 < len(S_TILES):
            out.append(("split", j + 1, None))
        if t in (("ba", 0), ("wo", 0), ("pw", 0), ("bb", 0)):
            out.extend(behind)
            behind = []
        outs = outputs_of(t)
        each = PARTS // len(outs)
        i = j - first
        beside = s[len(s) * i // (last - first):len(s) * (i + 1) // (last - first)] if first <= j < last else []
        for p in range(PARTS):
            out.append(("mm", j, p))
            half = each // 2 if each > 1 else 1
            q = p % each
            if q < half:
                out.extend(behind[len(behind) * q // half:len(behind) * (q + 1) // half])
            if q == each - 1:
                behind = [("E", outs[p // each], e) for e in e2_stages(outs[p // each])]
            a = PARTS // 2 - 1 if j == first else 0
            if p >= a:
                out.extend(beside[len(beside) * (p - a) // (PARTS - a):len(beside) * (p + 1 - a) // (PARTS - a)])
    out.extend(behind)
    return out


S_ORDER = second_order()
RAW, SPLIT = 3, 2


def build(nc, xT, pos, consts, params, w1, w2, params2, smallb, smallc, outT):
    with ExitStack() as ctx:
        def sb(name, shape, dt=F32):
            return ctx.enter_context(nc.sbuf_tensor(name, shape, dt))

        def sem(name):
            return ctx.enter_context(nc.semaphore(name))

        def at(base, off, name, shape, dt=F32):
            return nc.alloc_sbuf_tensor_at(name, shape, dt, offset=base + off)

        TILE = SEQ * 4
        x = sb("x", [P, KT, SEQ])
        hH, hL = sb("hH", [P, KT, SEQ], F32R), sb("hL", [P, KT, SEQ], F32R)
        cst = sb("cst", [P, NCONST])
        par_at = (nc.sbuf_base + 31) // 32 * 32
        par = sb("par", [P, NPARAM])
        rope_at = (nc.sbuf_base + 31) // 32 * 32
        ropeC, ropeS = sb("ropeC", [P, SEQ]), sb("ropeS", [P, SEQ])
        raw = sb("raw", [P, RAW, KT, P])
        wH, wL = sb("wH", [P, SPLIT, KT, P], F32R), sb("wL", [P, SPLIT, KT, P], F32R)
        rstd, rstdp = sb("rstd", [P, SEQ]), sb("rstdp", [P, SEQ])
        sq_at = (nc.sbuf_base + 31) // 32 * 32
        sq = sb("sq", [P, 2, SEQ])
        tmp = sb("tmp", [P, SEQ])
        small = sb("small", [P, 512])
        turn_small = sb("turn_small", [P, 2, ST, TBL])
        base_o = (nc.sbuf_base + 31) // 32 * 32
        OH, OL = sb("OH", [P, KT, SEQ], F32R), sb("OL", [P, KT, SEQ], F32R)
        base_s = (nc.sbuf_base + 31) // 32 * 32
        SH, SL = sb("SH", [P, KT, SEQ], F32R), sb("SL", [P, KT, SEQ], F32R)
        base_a = (nc.sbuf_base + 31) // 32 * 32
        acc = sb("acc", [P, KT, SEQ])
        base_r = (nc.sbuf_base + 31) // 32 * 32
        room = sb("room", [P, 11, SEQ])

        def spread(where, name):
            return [at(b, i * TILE, f"{name}{n}", [P, SEQ]) for n, (b, i) in enumerate(where)]

        qs = spread([(base_r, 0), (base_s, 8)], "qs")
        vs = spread([(base_r, 1), (base_s, 9)], "vs")
        ks = spread([(base_r, 2), (base_s, 11), (base_s, 13), (base_s, 0)], "ks")
        zs = spread([(base_s, 10), (base_s, 12), (base_s, 14), (base_s, 1)], "zs")
        kbeta = at(base_s, 15 * TILE, "kbeta", [P, SEQ])
        XT = at(base_s, 2 * TILE, "XT", [P, 3, CH, P])
        AT = at(base_s, 5 * TILE, "AT", [P, 3, CH, P])
        qd = at(base_a, 0, "qd", [P, 3, CH, P])
        kd = at(base_a, 3 * TILE, "kd", [P, 3, CH, P])
        LTm = at(base_a, 6 * TILE, "LTm", [P, 2, CH, P])
        vb = at(base_r, 3 * TILE, "vb", [P, 3, CH, P])
        Xi = at(base_r, 6 * TILE, "Xi", [P, CH, P])
        Pm = at(base_r, 7 * TILE, "Pm", [P, CH, P])
        DT = at(base_r, 8 * TILE, "DT", [P, CH, P])
        osq = at(base_r, 9 * TILE, "osq", [P, SEQ])
        S = at(base_r, 10 * TILE, "S", [P, P])
        rr = at(base_r, 10 * TILE + 512, "rr", [P, P])
        vn = at(base_r, 10 * TILE + 1024, "vn", [P, P])
        ab = at(base_r, 9 * TILE, "ab", [P, SEQ])
        rna = rstdp
        kc, kr = at(base_o, 7 * TILE, "kc", [P, SEQ])[:, :], at(base_o, 15 * TILE, "kr", [P, SEQ])[:, :]
        qraw = at(base_s, 8 * TILE, "qraw", [P, SWQ, SEQ])
        kk = at(base_r, 0, "kk", [P, 2, SEQ])
        vtok = at(base_r, 2 * TILE, "vtok", [P, CH, P])
        gate = at(base_r, 3 * TILE, "gate", [P, SEQ])
        gated = at(base_r, 4 * TILE, "gated", [P, SEQ])
        qrs = [rstdp, tmp]
        probs = [at(base_r, (5 + 2 * e) * TILE, f"prob{e}", [P, CH, 2 * P]) for e in range(2)]
        probTs = [at(sq_at, 0, "probT0", [P, 2 * CH, P]), at(base_r, 9 * TILE, "probT1", [P, 2 * CH, P])]
        def col(i, n=CH * HEADS):
            return small[:, i:i + n]
        abt, th, beta, hbeta = col(0, 64), col(64), col(96), col(128)
        at_, mx, ea, gg, gcl = col(160), col(192), col(224, 8), col(232), col(264, 64)
        kdec, egl, eg, nbeg = col(328), col(360), col(392), col(424)
        wcol = [[col(456 + 16 * e + 4 * i, 4) for i in range(4)] for e in range(2)]
        scal = sb("scal", [P, 3, 8, CH])
        srow = sb("srow", [P, 4, CH])

        ps = ctx.enter_context(nc.psum_tensor("ps", [P, 8, 512], F32))
        psD, psB, psA = ps[:, 2:4, :], ps[:, 4:6, :], ps[:, 6:8, :]

        def k_(name):
            return cst[:, CONST[name][0]:CONST[name][1]]

        def p_(name, i=None, n=1):
            a, b = PARAM[name]
            return par[:, a:b] if i is None else par[:, a + i:a + i + n]

        def head_tile(kind, h):
            return {"q": qs[h % 2], "k": ks[h % 4], "v": vs[h % 2], "z": zs[h % 4]}[kind][:, :]

        def conv(kind, head, tap):
            return p_("conv", ("qkv".index(kind) * HEADS + head) * CONV + tap)

        def chunks(m):
            return m.rearrange("p (c n) -> p c n", c=CH)

        def by_head(m, h):
            return m.rearrange("p (c n) -> p c n", c=CH)[:, :, h]

        def second_half(m, s):
            return m.rearrange("p (b n) -> p b n", n=2 * s)[:, :, s:]

        def over_chunks(m):
            return m.unsqueeze(1).to_broadcast([P, CH, P])

        names = ("loaded0", "loaded1", "loaded2", "high_done", "low_done", "tile_done", "tile_stage",
                 "gate_stage", "gram_stage", "inverse_stage", "scan_stage", "window_even", "window_odd", "x_ready", "sq_done", "h_high", "h_low",
                 "ssq_done", "root_done", "rstd_ready", "params_in", "x_part", "sum_in", "sum_done", "post_root",
                 "post_ready", "input_in", "out_done", "setup", "out_ready", "table_stage", "state_stage")
        sems = {n: sem(n) for n in names}
        nums = [s.num for s in sems.values()]
        assert nums == list(range(nums[0], nums[0] + len(nums)))
        loaded = [sems[f"loaded{i}"] for i in range(RAW)]
        (high_done, low_done, tile_done, tile_stage, gate_stage, gram_stage, inverse_stage, scan_stage, window_even, window_odd, x_ready,
         sq_done, h_high, h_low, ssq_done, root_done, rstd_ready, params_in, x_part, sum_in, sum_done, post_root,
         post_ready, input_in, out_done, setup, out_ready, table_stage, state_stage) = [sems[n] for n in names[RAW:]]

        window_stage = (window_even, window_odd)

        def clear_all():
            with nc.Block() as block:
                @block.sync
                def _(sp):
                    sp.sem_clear(range(nums[0], nums[0] + len(nums)))

        with nc.Block() as block:
            @block.sync
            def _(sp):
                sp.dma_start(x[:, :, :], xT).then_inc(input_in, 16)
                sp.dma_start(cst[:, :], consts).then_inc(input_in, 16)
                sp.dma_start(sq[:, 0, :].bitcast(I32), pos.to_broadcast([P, SEQ])).then_inc(input_in, 16)

            @block.vector
            def _(v):
                step = [0]

                def link(ins):
                    step[0] += 1
                    ins.then_inc(setup, 1)
                    v.wait_ge(setup, step[0])

                v.wait_ge(input_in, 48)
                link(v.tensor_copy(tmp[:, :], sq[:, 0, :].bitcast(I32)))
                link(v.tensor_scalar(tmp[:, :], tmp[:, :], k_("invfreq"), None, ALU.mult))
                range_reduce(v, link, rstd[:, :], tmp[:, :], sq[:, 0, :], 0.0)
                range_reduce(v, link, rstdp[:, :], tmp[:, :], sq[:, 0, :], 0.25)
                v.wait_ge(x_part, 2)
                link(v.tensor_scalar(ropeS[:, :], ropeS[:, :], k_("isrot"), None, ALU.mult))
                link(v.tensor_scalar(ropeC[:, :], ropeC[:, :], k_("isrot"), k_("notrot"), ALU.mult, ALU.add))

            @block.scalar
            def _(act):
                act.wait_ge(setup, 2 + 2 * RANGE_STEPS)
                act.activation(ropeS[:, :], rstd[:, :], ACT.Sin).then_inc(x_part, 1)
                act.activation(ropeC[:, :], rstdp[:, :], ACT.Sin, bias=k_("halfpi")).then_inc(x_part, 1)
        clear_all()

        def splitting(block, tiles, weights, params_of):
            @block.sync
            def _(sp):
                if params_of is not None:
                    sp.dma_start(par[:, :], params_of).then_inc(params_in, 16)
                for j in range(len(tiles)):
                    if j >= RAW:
                        sp.wait_ge(low_done, j - RAW + 1)
                    sp.dma_start(raw[:, j % RAW, :, :].rearrange("p t n -> p (t n)"), weights(j)).then_inc(loaded[j % RAW], 16)

        def split_high(act, j):
            act.wait_ge(loaded[j % RAW], 16 * (j // RAW + 1))
            if j >= SPLIT:
                act.wait_ge(tile_done, j - SPLIT + 1)
            act.activation(wH[:, j % SPLIT, :, :], raw[:, j % RAW, :, :], ACT.Copy).then_inc(high_done, 1)

        def split_low(pool, j):
            pool.wait_ge(high_done, j + 1)
            pool.tensor_tensor(wL[:, j % SPLIT, :, :], raw[:, j % RAW, :, :], wH[:, j % SPLIT, :, :].bitcast(F32),
                               ALU.subtract).then_inc(low_done, 1)

        def products(pe, j, p, out, rH, rL, depth, col0=0, width=P, kt0=0, parts=PARTS, before=None):
            s = j % SPLIT
            t = -1
            for t in range(depth * p // parts, depth * (p + 1) // parts):
                if before is not None:
                    before(t)
                wh = wH[:, s, kt0 + t, col0:col0 + width]
                wl = wL[:, s, kt0 + t, col0:col0 + width]
                pe.matmul(out, wh, rH[:, t, :], start=(t == 0), stop=False)
                pe.matmul(out, wh, rL[:, t, :], start=False, stop=False)
                mm = pe.matmul(out, wl, rH[:, t, :], start=False, stop=(t == depth - 1))
            if (t + 1) == depth:
                mm.then_inc(tile_done, 1)

        tmp2 = [room[:, 9, :], room[:, 10, :]]

        def x_add(v, t, gain, n):
            v.scalar_tensor_tensor(out=tmp2[t % 2], in0=acc[:, t, :], scalar=gain(t), in1=rstdp[:, :],
                                   op0=ALU.mult, op1=ALU.mult).then_inc(x_part, 1)
            v.wait_ge(x_part, n + t + 1)
            v.tensor_tensor(x[:, t, :], x[:, t, :], tmp2[t % 2], ALU.add).then_inc(x_ready, 1)

        def x_low(v, t, gain, n):
            v.wait_ge(h_high, n + t + 1)
            v.scalar_tensor_tensor(out=hL[:, t, :], in0=x[:, t, :], scalar=gain(t), in1=hH[:, t, :].bitcast(F32),
                                   op0=ALU.mult, op1=ALU.subtract).then_inc(h_low, 1)

        def x_high(act, gain, n, ready):
            for t in range(KT):
                if ready is not None:
                    act.wait_ge(x_ready, ready + t + 1)
                act.activation(hH[:, t, :], x[:, t, :], ACT.Copy, scale=gain(t)).then_inc(h_high, 1)
                if t >= 2:
                    act.wait_ge(ssq_done, n + t - 1)
                act.activation(sq[:, t % 2, :], x[:, t, :], ACT.Square).then_inc(sq_done, 1)

        def x_sum(pe, base, t):
            pe.wait_ge(sq_done, base + t + 1)
            pe.matmul(ps[:, 7, :], k_("ones"), sq[:, t % 2, :], start=(t == 0), stop=(t == KT - 1)).then_inc(ssq_done, 1)

        def root_scalar(act, done, n, out, src, scale, eps, ready):
            act.wait_ge(done, n)
            act.activation(out, src, ACT.Sqrt, bias=k_(eps), scale=scale).then_inc(ready, 1)

        with nc.Fori(0, DEPTH) as layer:
            with nc.Block() as block:
                splitting(block, LT_TILES, lambda j: w1[layer, j], params[layer])

                @block.gpsimd
                def _(pool):
                    for kind, j, s in L_ORDER:
                        if kind == "split":
                            split_low(pool, j)
                        elif kind == "D" and s in ("qdec", "mask"):
                            pool.wait_ge(gram_stage, D.before(j, s))
                            if s == "qdec":
                                if j >= 3:
                                    pool.wait_ge(scan_stage, B.end(j - 3))
                                pool.tensor_tensor(qd[:, j % 3, :, :], chunks(qs[j % 2][:, :]), chunks(rna[:, :]),
                                                   ALU.mult).then_inc(gram_stage, 1)
                            else:
                                pool.tensor_tensor(DT[:, :, :], DT[:, :, :], over_chunks(k_("upper")),
                                                   ALU.mult).then_inc(gram_stage, 1)
                        elif kind == "B" and s == "low":
                            pool.wait_ge(scan_stage, B.before(j, s))
                            pool.tensor_tensor(OL[:, j, :], osq[:, :], OH[:, j, :].bitcast(F32),
                                               ALU.subtract).then_inc(scan_stage, 1)
                        elif kind == "E" and s == "low":
                            pool.wait_ge(tile_stage, E.before(j, s))
                            if j[0] == "f1":
                                c, t = j[1] // 8, j[1] % 8
                                pool.tensor_tensor((OL, SL)[c % 2][:, t, :], tmp[:, :],
                                                   (OH, SH)[c % 2][:, t, :].bitcast(F32),
                                                   ALU.subtract).then_inc(tile_stage, 1)
                            else:
                                pool.tensor_tensor(OL[:, j[1], :], gated[:, :], OH[:, j[1], :].bitcast(F32),
                                                   ALU.subtract).then_inc(tile_stage, 1)

                @block.scalar
                def _(act):
                    act.wait_ge(params_in, 16)
                    split_high(act, 0)
                    x_high(act, lambda t: p_("pre_mix", t), 0, None)
                    root_scalar(act, ssq_done, KT, rstd[:, :], ps[:, 7, :], 1.0 / D_MODEL, "eps", root_done)
                    for kind, j, s in L_ORDER[1:]:
                        if kind == "split":
                            split_high(act, j)
                        elif kind == "G" and s in ("tanh", "abs", "expn", "ln", "expa", "exps"):
                            act.wait_ge(gate_stage, G.before(0, s))
                            a3 = abt.rearrange("p (c n) -> p c n", c=CH)
                            if s == "tanh":
                                act.activation(th.rearrange("p (c n) -> p c n", c=CH), a3[:, :, 0:HEADS], ACT.Tanh, scale=0.5).then_inc(gate_stage, 1)
                            if s == "abs":
                                act.activation(at_, at_, ACT.Abs).then_inc(gate_stage, 1)
                            if s == "expn":
                                act.activation(at_, at_, ACT.Exp, scale=-1.0).then_inc(gate_stage, 1)
                            if s == "ln":
                                act.activation(at_, at_, ACT.Ln).then_inc(gate_stage, 1)
                            if s == "expa":
                                act.activation(ea, p_("a_log"), ACT.Exp).then_inc(gate_stage, 1)
                            if s == "exps":
                                act.activation(kdec, kdec, ACT.Exp)
                                act.activation(egl, gcl[:, 32:64], ACT.Exp)
                                act.activation(eg, gcl[:, 0:32], ACT.Exp).then_inc(gate_stage, 1)
                        elif kind == "D" and s in ("square", "root", "exps", "copykv"):
                            act.wait_ge(gram_stage, D.before(j, s))
                            w = scal[:, j % 3]
                            if s == "square":
                                act.wait_ge(tile_stage, E.end(("z", j)))
                                act.activation(sq[:, 0, :], ks[j % 4][:, :], ACT.Square)
                                ins = act.activation(sq[:, 1, :], qs[j % 2][:, :], ACT.Square)
                            elif s == "root":
                                if j >= 3:
                                    act.wait_ge(scan_stage, B.end(j - 3))
                                ins = act.activation(w[:, 0:2, :], psD[:, 0, 0:2 * CH].rearrange("p (a c) -> p a c", a=2),
                                                     ACT.Sqrt, bias=k_("eps4"))
                            elif s == "exps":
                                act.activation(rna[:, :], psD[:, 0, :], ACT.Exp)
                                ins = act.activation(DT[:, :, :], DT[:, :, :], ACT.Exp)
                            else:
                                for c in range(CH):
                                    i = c * HEADS + j
                                    act.activation(kd[:, j % 3, c, :], psD[:, 0, c * P:(c + 1) * P], ACT.Copy, scale=w[:, 4, c:c + 1])
                                    ins = act.activation(vb[:, j % 3, c, :], psD[:, 1, c * P:(c + 1) * P], ACT.Copy, scale=hbeta[:, i:i + 1])
                            ins.then_inc(gram_stage, 1)
                        elif kind == "A" and s.startswith("copy"):
                            act.wait_ge(inverse_stage, A.before(j, s))
                            act.activation(Xi[:, :, :], chunks(psA[:, 0, :]), ACT.Copy).then_inc(inverse_stage, 1)
                        elif kind == "B" and (s.startswith("copyv") or s in ("square", "root", "high")):
                            act.wait_ge(scan_stage, B.before(j, s))
                            if s == "square":
                                act.activation(osq[:, :], psB[:, 1, :], ACT.Square).then_inc(scan_stage, 1)
                            elif s == "root":
                                act.activation(srow[:, 1], srow[:, 0], ACT.Sqrt, bias=k_("eps4")).then_inc(scan_stage, 1)
                            elif s == "high":
                                if j == HEADS - 1:
                                    act.wait_ge(tile_stage, E.end(("swk", 0)))
                                act.activation(OH[:, j, :], osq[:, :], ACT.Copy).then_inc(scan_stage, 1)
                            else:
                                act.activation(vn[:, :], psB[:, 0, 0:P], ACT.Copy).then_inc(scan_stage, 1)
                        elif kind == "C" and (s[:-1] in ("exp", "copy") or s == "high"):
                            o = j % 2
                            act.wait_ge(window_stage[o], C[o].before(j, s))
                            prob, (m4, nm4, den, es) = probs[o], wcol[o]
                            if s[:-1] == "exp":
                                e = int(s[-1])
                                for n in range(CH):
                                    a = P if n == 0 else 0
                                    act.activation(prob[:, n, a:], prob[:, n, a:], ACT.Exp, bias=nm4[:, n:n + 1],
                                                   accum_out=den[:, n:n + 1])
                                ins = act.activation(es, nm4, ACT.Exp, bias=p_("sinks", 2 * j + e))
                            elif s[:-1] == "copy":
                                pT = ps[:, 2 + 2 * o:4 + 2 * o, :].rearrange("p b (c n) -> p (b c) n", n=P)
                                ins = act.activation(probTs[o][:, 0:2 * CH - 1, :], pT[:, 0:2 * CH - 1, :], ACT.Copy)
                            else:
                                ins = act.activation(SH[:, j, :], ps[:, 6 + o, :], ACT.Copy)
                            ins.then_inc(window_stage[o], 1)
                        elif kind == "E" and s in ("tap3", "tanh", "copyk", "copyv", "high", "square"):
                            act.wait_ge(tile_stage, E.before(j, s))
                            kd_, i = j
                            dst = head_tile(kd_, i) if kd_ in "qkvz" else None
                            if s == "tap3":
                                if kd_ == "q" and i >= 2:
                                    act.wait_ge(gram_stage, D.end(i - 2))
                                if kd_ == "q" and i >= 4:
                                    act.wait_ge(scan_stage, B.end(i - 4))
                                act.activation(dst, tmp[:, :], ACT.Copy, scale=conv(kd_, i, 3)).then_inc(tile_stage, 1)
                            elif s == "tanh" and kd_ in "qkv":
                                act.activation(tmp[:, :], dst, ACT.Tanh, scale=0.5).then_inc(tile_stage, 1)
                            elif s == "tanh" and kd_ == "z":
                                act.activation(dst, tmp[:, :], ACT.Tanh, scale=0.5).then_inc(tile_stage, 1)
                            elif s == "tanh":
                                act.activation(gate[:, :], gate[:, :], ACT.Tanh, scale=0.5).then_inc(tile_stage, 1)
                            elif s == "copyk":
                                act.activation(kk[:, 0, :], psD[:, 0, :], ACT.Copy)
                                act.activation(kk[:, 1, :], psD[:, 1, :], ACT.Copy).then_inc(tile_stage, 1)
                            elif s == "copyv":
                                act.activation(vtok[:, :, :], chunks(psD[:, 0, :]), ACT.Copy).then_inc(tile_stage, 1)
                            elif s == "high" and kd_ == "f1":
                                act.activation((OH, SH)[i // 8 % 2][:, i % 8, :], tmp[:, :], ACT.Copy).then_inc(tile_stage, 1)
                            elif s == "high":
                                act.activation(OH[:, i, :], gated[:, :], ACT.Copy).then_inc(tile_stage, 1)
                            else:
                                act.activation(sq[:, 0, :], acc[:, i % 8, :], ACT.Square).then_inc(tile_stage, 1)
                            if j == ("wo", KT - 1) and s == "square":
                                root_scalar(act, sum_done, 1, rstdp[:, :], ps[:, 7, :], 1.0 / D_MODEL, "eps", post_root)
                                x_high(act, lambda t: p_("pre_mlp", t), KT, 0)
                                root_scalar(act, ssq_done, 2 * KT, rstd[:, :], ps[:, 7, :], 1.0 / D_MODEL, "eps", root_done)
                    root_scalar(act, sum_done, 2, rstdp[:, :], ps[:, 7, :], 1.0 / D_MODEL, "eps", post_root)

                @block.vector
                def _(v):
                    def rstd_vector(n):
                        v.wait_ge(root_done, n)
                        v.reciprocal(rstd[:, :], rstd[:, :]).then_inc(rstd_ready, 1)
                        v.wait_ge(rstd_ready, n)

                    def post_vector(n):
                        v.wait_ge(post_root, n)
                        v.reciprocal(rstdp[:, :], rstdp[:, :]).then_inc(post_ready, 1)

                    v.wait_ge(params_in, 16)
                    for t in range(KT):
                        x_low(v, t, lambda t: p_("pre_mix", t), 0)
                    rstd_vector(1)
                    for kind, j, s in L_ORDER[1:]:
                        if kind == "G":
                            if s not in ("copy", "beta", "hbeta", "addb", "max", "plus1", "sp", "g", "copyc", "diff", "nbeg"):
                                continue
                            v.wait_ge(gate_stage, G.before(0, s))
                            c8 = lambda ap: ap.rearrange("p (c n) -> p c n", c=CH)
                            if s == "copy":
                                ins = v.tensor_copy(abt, psD[:, 0, 0:64])
                            elif s == "beta":
                                ins = v.tensor_scalar(beta, th, 0.5, 0.5, ALU.mult, ALU.add)
                            elif s == "hbeta":
                                ins = v.tensor_scalar(hbeta, beta, 0.5, None, ALU.mult)
                            elif s == "addb":
                                ins = v.tensor_tensor(c8(at_), c8(abt)[:, :, HEADS:2 * HEADS],
                                                      p_("dt_bias").unsqueeze(1).to_broadcast([P, CH, HEADS]), ALU.add)
                            elif s == "max":
                                ins = v.tensor_scalar(mx, at_, 0.0, None, ALU.max)
                            elif s == "plus1":
                                ins = v.tensor_scalar(at_, at_, 1.0, None, ALU.add)
                            elif s == "sp":
                                ins = v.tensor_tensor(at_, at_, mx, ALU.add)
                            elif s == "g":
                                ins = v.scalar_tensor_tensor(out=c8(gg), in0=c8(at_), scalar=-1.0,
                                                             in1=ea.unsqueeze(1).to_broadcast([P, CH, HEADS]),
                                                             op0=ALU.mult, op1=ALU.mult)
                            elif s == "copyc":
                                ins = v.tensor_copy(gcl, psD[:, 0, 0:64])
                            elif s == "diff":
                                ins = v.tensor_tensor(kdec, gcl[:, 32:64], gcl[:, 0:32], ALU.subtract)
                            else:
                                ins = v.scalar_tensor_tensor(out=nbeg, in0=beta, scalar=-1.0, in1=eg,
                                                             op0=ALU.mult, op1=ALU.mult)
                            ins.then_inc(gate_stage, 1)
                        elif kind == "D" and s in ("recip", "scales", "kbeta", "diff", "masked", "first", "minus"):
                            h = j
                            w = scal[:, h % 3]
                            v.wait_ge(gram_stage, D.before(h, s))
                            a0, a1 = (chunks(psD[:, i, :]) for i in range(2))
                            xt, lt = XT[:, h % 3, :, :], LTm[:, h % 2, :, :]
                            if s == "recip":
                                ins = v.reciprocal(w[:, 0:2, :], w[:, 0:2, :])
                            elif s == "scales":
                                v.tensor_tensor(w[:, 2, :], w[:, 0, :], by_head(beta, h), ALU.mult)
                                v.tensor_tensor(w[:, 3, :], w[:, 0, :], by_head(nbeg, h), ALU.mult)
                                v.tensor_tensor(w[:, 4, :], w[:, 0, :], by_head(kdec, h), ALU.mult)
                                v.tensor_scalar(w[:, 5, :], w[:, 1, :], float(P) ** -0.5, None, ALU.mult)
                                ins = v.scalar_tensor_tensor(out=w[:, 6, :], in0=w[:, 1, :], scalar=4.0 / P ** 2,
                                                             in1=w[:, 1, :], op0=ALU.mult, op1=ALU.mult)
                            elif s == "kbeta":
                                ins = v.tensor_tensor(kbeta[:, :], ks[h % 4][:, :], psD[:, 1, :], ALU.mult)
                            elif s == "diff":
                                for c in range(CH):
                                    i = c * HEADS + h
                                    ins = v.tensor_scalar(DT[:, c, :], a0[:, c, :], gcl[:, i:i + 1], 0.0,
                                                          ALU.subtract, ALU.min)
                            elif s == "masked":
                                if h >= 3:
                                    v.wait_ge(scan_stage, B.end(h - 3))
                                if h >= 2:
                                    v.wait_ge(inverse_stage, A.end(h - 2))
                                for c in range(CH):
                                    r = w[:, 0, c:c + 1]
                                    v.scalar_tensor_tensor(out=AT[:, h % 3, c, :], in0=a1[:, c, :], scalar=r, in1=DT[:, c, :],
                                                           op0=ALU.mult, op1=ALU.mult)
                                    ins = v.scalar_tensor_tensor(out=lt[:, c, :], in0=a0[:, c, :], scalar=r, in1=DT[:, c, :],
                                                                 op0=ALU.mult, op1=ALU.mult)
                            elif s == "first":
                                ins = v.tensor_tensor(xt, lt, over_chunks(k_("first")), ALU.mult)
                            else:
                                ins = v.tensor_tensor(xt, over_chunks(k_("ident")), xt, ALU.subtract)
                            ins.then_inc(gram_stage, 1)
                        elif kind == "A" and (s.startswith("pmask") or s.startswith("update")):
                            v.wait_ge(inverse_stage, A.before(j, s))
                            lev = int(s[-1])
                            if s.startswith("pmask"):
                                m = k_("levels")[:, lev * P:(lev + 1) * P]
                                ins = v.tensor_tensor(Pm[:, :, :], chunks(psA[:, 0, :]), over_chunks(m), ALU.mult)
                            else:
                                xt = second_half(XT[:, j % 3, :, :].rearrange("p c n -> p (c n)"), LEVELS[lev])
                                ins = v.tensor_tensor(xt, xt, second_half(psA[:, 1, :], LEVELS[lev]), ALU.subtract)
                            ins.then_inc(inverse_stage, 1)
                        elif kind == "B":
                            h = j
                            if not (s[:-1] in ("rr", "state") or s in ("mean", "recip", "factor", "norm")):
                                continue
                            w = scal[:, h % 3]
                            v.wait_ge(scan_stage, B.before(h, s))
                            if s == "state0":
                                ins = v.tensor_copy(S[:, :], psB[:, 0, P:2 * P])
                            elif s.startswith("state"):
                                i = int(s[-1]) * HEADS + h
                                ins = v.scalar_tensor_tensor(out=S[:, :], in0=S[:, :], scalar=egl[:, i:i + 1],
                                                             in1=psB[:, 0, P:2 * P], op0=ALU.mult, op1=ALU.add)
                            elif s.startswith("rr"):
                                c = int(s[-1])
                                ins = v.scalar_tensor_tensor(out=rr[:, :], in0=psB[:, 0, 2 * P:3 * P],
                                                             scalar=w[:, 3, c:c + 1], in1=vb[:, h % 3, c, :],
                                                             op0=ALU.mult, op1=ALU.add)
                            elif s == "mean":
                                v.tensor_tensor(srow[:, 0], psB[:, 0, 0:CH], w[:, 6, :], ALU.mult)
                                ins = v.scalar_tensor_tensor(out=osq[:, :], in0=psB[:, 1, :], scalar=p_("norm"),
                                                             in1=zs[h % 4][:, :], op0=ALU.mult, op1=ALU.mult)
                            elif s == "recip":
                                ins = v.reciprocal(srow[:, 2], srow[:, 1])
                            elif s == "factor":
                                ins = v.tensor_tensor(srow[:, 3], srow[:, 2], w[:, 5, :], ALU.mult)
                            else:
                                ins = v.tensor_tensor(osq[:, :], osq[:, :], psB[:, 0, :], ALU.mult)
                            ins.then_inc(scan_stage, 1)
                        elif kind == "C":
                            t, o = j, j % 2
                            e = int(s[-1]) if s[-1].isdigit() else 0
                            w = s.rstrip("01")
                            if w not in ("cos", "sin", "addq", "mask", "max", "maxs", "neg", "den", "recip", "prob", "low"):
                                continue
                            v.wait_ge(window_stage[o], C[o].before(t, s))
                            prob, qr, (m4, nm4, den, es) = probs[o], qrs[o], wcol[o]
                            qc = probTs[o][:, 0:CH, :].rearrange("p c n -> p (c n)")
                            if w == "cos":
                                ins = v.tensor_tensor(qc, qraw[:, t, :], ropeC[:, :], ALU.mult)
                            elif w == "sin":
                                if t < 2:
                                    v.memset(prob[:, 0, 0:P], NEG)
                                ins = v.tensor_tensor(qr[:, :], ps[:, 6 + o, :], ropeS[:, :], ALU.mult)
                            elif w == "addq":
                                ins = v.tensor_tensor(qr[:, :], qr[:, :], qc, ALU.add)
                            elif w == "mask":
                                sc = ps[:, 2 + 2 * o:4 + 2 * o, :].rearrange("p b (n k) -> p (b n) k", k=2 * P)
                                v.scalar_tensor_tensor(out=prob[:, 0, P:], in0=sc[:, 0, P:], scalar=float(HD) ** -0.5,
                                                       in1=k_("window")[:, P:], op0=ALU.mult, op1=ALU.add)
                                ins = v.scalar_tensor_tensor(out=prob[:, 1:, :], in0=sc[:, 1:, :], scalar=float(HD) ** -0.5,
                                                             in1=k_("window").unsqueeze(1).to_broadcast([P, CH - 1, 2 * P]),
                                                             op0=ALU.mult, op1=ALU.add)
                            elif w == "max":
                                ins = v.tensor_reduce(m4, prob[:, :, :], AX.X, ALU.max)
                            elif w == "maxs":
                                ins = v.tensor_scalar(m4, m4, p_("sinks", 2 * t + e), None, ALU.max)
                            elif w == "neg":
                                ins = v.tensor_scalar(nm4, m4, -1.0, None, ALU.mult)
                            elif w == "den":
                                ins = v.tensor_tensor(den, den, es, ALU.add)
                            elif w == "recip":
                                ins = v.reciprocal(den, den)
                            elif w == "prob":
                                v.tensor_scalar(prob[:, 0, P:], prob[:, 0, P:], den[:, 0:1], None, ALU.mult)
                                ins = v.tensor_tensor(prob[:, 1:, :], prob[:, 1:, :],
                                                      den[:, 1:].unsqueeze(2).to_broadcast([P, CH - 1, 2 * P]), ALU.mult)
                            else:
                                ins = v.tensor_tensor(SL[:, t, :], ps[:, 6 + o, :], SH[:, t, :].bitcast(F32), ALU.subtract)
                            ins.then_inc(window_stage[o], 1)
                        elif kind == "E":
                            kd_, i = j
                            n = L_AT[j]
                            b = ps[:, n % 2, :]
                            if s in ("tanh", "tap3", "rotk", "dupk", "copyk", "turnv", "copyv", "high", "low", "square"):
                                continue
                            v.wait_ge(tile_stage, E.before(j, s))
                            if s == e_stages(j)[0]:
                                v.wait_ge(tile_done, n + 1)
                                if j == ("f1", 0):
                                    rstd_vector(2)
                            dst = head_tile(kd_, i) if kd_ in "qkvz" else None
                            if s == "scale":
                                out = {"ab": ab[0:16, :], "ga": gate[:, :], "gb": gate[:, :], "swq": None}.get(kd_, tmp[:, :])
                                if kd_ == "swq":
                                    out = qraw[:, i, :]
                                m = 16 if kd_ == "ab" else P
                                if j == ("swq", 0):
                                    v.wait_ge(scan_stage, B.end(HEADS - 3))
                                    v.wait_ge(gram_stage, D.end(HEADS - 1))
                                if j == ("swq", SWQ // 2):
                                    v.wait_ge(scan_stage, B.end(HEADS - 2))
                                if j == ("ga", 0):
                                    v.wait_ge(scan_stage, B.end(HEADS - 1))
                                ins = v.tensor_tensor(out, b[0:m, :], rstd[0:m, :], ALU.mult)
                            elif s in ("tap2", "tap1", "tap0"):
                                d = 3 - int(s[-1])
                                ins = v.scalar_tensor_tensor(out=dst[:, d:], in0=tmp[:, 0:SEQ - d], scalar=conv(kd_, i, 3 - d),
                                                             in1=dst[:, d:], op0=ALU.mult, op1=ALU.add)
                            elif s == "silu" and kd_ != "z":
                                ins = v.scalar_tensor_tensor(out=dst, in0=tmp[:, :], scalar=1.0, in1=dst, op0=ALU.add, op1=ALU.mult)
                            elif s == "silu":
                                ins = v.scalar_tensor_tensor(out=dst, in0=dst, scalar=1.0, in1=tmp[:, :], op0=ALU.add, op1=ALU.mult)
                            elif s == "cosk":
                                ins = v.tensor_tensor(kc, tmp[:, :], ropeC[:, :], ALU.mult)
                            elif s == "sink":
                                ins = v.tensor_tensor(kr, psD[:, 0, :], ropeS[:, :], ALU.mult)
                            elif s == "addk":
                                ins = v.tensor_tensor(kr, kr, kc, ALU.add)
                            elif s == "gate" and kd_ == "ya":
                                ins = v.scalar_tensor_tensor(out=acc[:, i, :], in0=gate[:, :], scalar=1.0, in1=b, op0=ALU.add, op1=ALU.mult)
                            elif s == "gate":
                                ins = v.scalar_tensor_tensor(out=gated[:, :], in0=gate[:, :], scalar=1.0, in1=b, op0=ALU.add, op1=ALU.mult)
                            elif s == "add" and kd_ == "yb":
                                ins = v.tensor_tensor(gated[:, :], gated[:, :], acc[:, i, :], ALU.add)
                            elif s == "relu2":
                                ins = v.scalar_tensor_tensor(out=tmp[:, :], in0=tmp[:, :], scalar=0.0, in1=tmp[:, :], op0=ALU.max, op1=ALU.mult)
                            elif s == "copy" and kd_ == "wo":
                                ins = v.tensor_scalar(acc[:, i, :], b, 0.5, None, ALU.mult)
                            elif s == "copy":
                                ins = v.tensor_copy(acc[:, i % 8, :], b)
                            elif s == "add":
                                ins = v.tensor_tensor(acc[:, i % 8, :], acc[:, i % 8, :], b, ALU.add)
                            elif s == "sum":
                                if i % 8 == 0:
                                    ins = v.tensor_copy(sq[:, 1, :], sq[:, 0, :])
                                else:
                                    ins = v.tensor_tensor(sq[:, 1, :], sq[:, 1, :], sq[:, 0, :], ALU.add)
                            ins.then_inc(tile_stage, 1)
                            if j == ("wo", KT - 1) and s == "sum":
                                post_vector(1)
                                v.wait_ge(post_ready, 1)
                                for t in range(KT + 1):
                                    if t < KT:
                                        x_add(v, t, lambda t: p_("post_mix", t), 0)
                                    if t:
                                        x_low(v, t - 1, lambda t: p_("pre_mlp", t), KT)
                    post_vector(2)
                    v.wait_ge(post_ready, 2)
                    for t in range(KT):
                        x_add(v, t, lambda t: p_("post_mlp", t), KT)

                @block.tensor
                def _(pe):
                    ident = k_("ident")
                    for kind, j, s in L_ORDER:
                        if kind == "mm":
                            tile = LT_TILES[j]
                            kd_, i = tile
                            rH, rL = hH, hL
                            before = None
                            if s == 0:
                                pe.wait_ge(low_done, j + 1)
                                if j >= 2:
                                    pe.wait_ge(tile_stage, E.before(LT_TILES[j - 2], e_stages(LT_TILES[j - 2])[0]) + 1)
                                if tile == ("ya", 0):
                                    pe.wait_ge(scan_stage, B.end(HEADS - 1))
                                if tile == ("yb", 0):
                                    for o in range(2):
                                        pe.wait_ge(window_stage[o], C[o].end(SWQ - 2 + o))
                                if tile == ("wo", 0):
                                    pe.wait_ge(tile_stage, E.end(("yb", KT - 1)))
                                if kd_ == "f2" and i % 8 == 0:
                                    pe.wait_ge(tile_stage, E.end(("f1", i + 7)))
                                if tile == ("f1", 0):
                                    pe.wait_ge(tile_stage, E.end(("wo", KT - 1)))
                                    pe.matmul(ps[:, 7, :], k_("ones"), sq[:, 1, :], start=True, stop=True).then_inc(sum_done, 1)
                            if kd_ in ("ya", "wo"):
                                rH, rL = OH, OL
                            elif kd_ == "yb":
                                rH, rL = SH, SL
                            elif kd_ == "f2":
                                rH, rL = (OH, OL) if i // 8 % 2 == 0 else (SH, SL)
                            if tile in (("ab", 0), ("f1", 0)):
                                base = 0 if kd_ == "ab" else KT

                                def before(t, base=base):
                                    if t == 0 and base:
                                        pe.wait_ge(post_root, 1)
                                    pe.wait_ge(h_low, base + t + 1)
                                    x_sum(pe, base, t)
                            m = 16 if kd_ == "ab" else P
                            products(pe, j, s, ps[0:m, j % 2, :], rH, rL, KT, width=m, before=before)
                        elif kind == "G" and s in ("turn", "cumsum"):
                            pe.wait_ge(gate_stage, G.before(0, s))
                            if s == "turn":
                                pe.wait_ge(tile_stage, E.end(("ab", 0)))
                                for c in range(CH):
                                    ins = pe.transpose(psD[:, 0, c * 16:(c + 1) * 16], ab[0:16, c * P:(c + 1) * P], ident[0:16, 0:16])
                            else:
                                pe.matmul(psD[:, 0, 0:32], k_("upper"), gg, start=True, stop=True)
                                ins = pe.matmul(psD[:, 0, 32:64], k_("ones"), gg, start=True, stop=True)
                            ins.then_inc(gate_stage, 1)
                        elif kind == "D" and s in ("sums", "rows", "gram", "turnkv"):
                            h = j
                            pe.wait_ge(gram_stage, D.before(h, s))
                            q, k, vv, w = qs[h % 2][:, :], ks[h % 4][:, :], vs[h % 2][:, :], scal[:, h % 3]
                            if s == "rows" and h == 0:
                                pe.wait_ge(gate_stage, G.end(0))
                            for c in range(CH):
                                i, cc = c * HEADS + h, slice(c * P, (c + 1) * P)
                                if s == "sums":
                                    pe.matmul(psD[:, 0, c:c + 1], sq[:, 0, cc], k_("ones")[:, 0:1], start=True, stop=True)
                                    ins = pe.matmul(psD[:, 0, CH + c:CH + c + 1], sq[:, 1, cc], k_("ones")[:, 0:1], start=True, stop=True)
                                elif s == "rows":
                                    pe.matmul(psD[:, 0, cc], gg[:, i:i + 1].to_broadcast([P, P]), k_("upper"), start=True, stop=True)
                                    ins = pe.matmul(psD[:, 1, cc], w[:, 2, c:c + 1].to_broadcast([P, P]), ident, start=True, stop=True)
                                elif s == "gram":
                                    pe.matmul(psD[:, 0, cc], k[:, cc], kbeta[:, cc], start=True, stop=True)
                                    ins = pe.matmul(psD[:, 1, cc], k[:, cc], q[:, cc], start=True, stop=True)
                                else:
                                    pe.transpose(psD[:, 0, cc], k[:, cc], ident)
                                    ins = pe.transpose(psD[:, 1, cc], vv[:, cc], ident)
                            ins.then_inc(gram_stage, 1)
                        elif kind == "A" and s[:-1] in ("p", "q", "turn"):
                            h = j
                            pe.wait_ge(inverse_stage, A.before(h, s))
                            if s == "turni":
                                pe.wait_ge(gram_stage, D.end(h))
                            for c in range(CH):
                                cc = slice(c * P, (c + 1) * P)
                                if s.startswith("turn"):
                                    ins = pe.transpose(psA[:, 0, cc], XT[:, h % 3, c, :], ident)
                                elif s[0] == "p":
                                    ins = pe.matmul(psA[:, 0, cc], LTm[:, h % 2, c, :], Xi[:, c, :], start=True, stop=True)
                                else:
                                    b = LEVELS[int(s[-1])]
                                    ins = pe.matmul(second_half(psA[:, 1, cc], b), Pm[:, c, :], second_half(XT[:, h % 3, c, :], b),
                                                    start=True, stop=True)
                            ins.then_inc(inverse_stage, 1)
                        elif kind == "B" and (s[:-1] in ("v", "o", "r") or s in ("sums", "row")):
                            h = j
                            pe.wait_ge(scan_stage, B.before(h, s))
                            k = ks[h % 4][:, :]
                            c = int(s[-1]) if s[-1].isdigit() else 0
                            cc = slice(c * P, (c + 1) * P)
                            if s == "v0":
                                pe.wait_ge(inverse_stage, A.end(h))
                            if s in ("sums", "row"):
                                for c in range(CH):
                                    if s == "sums":
                                        ins = pe.matmul(psB[:, 0, c:c + 1], osq[:, c * P:(c + 1) * P], k_("ones")[:, 0:1], start=True, stop=True)
                                    else:
                                        ins = pe.matmul(psB[:, 0, c * P:(c + 1) * P], srow[:, 3, c:c + 1].to_broadcast([P, P]), ident,
                                                        start=True, stop=True)
                            elif s[0] == "r":
                                ins = pe.matmul(psB[:, 0, 2 * P:3 * P], k[:, cc], S[:, :], start=True, stop=True)
                            elif s[0] == "v":
                                ins = pe.matmul(psB[:, 0, 0:P], XT[:, h % 3, c, :], vb[:, h % 3, 0, :] if c == 0 else rr[:, :],
                                                start=True, stop=True)
                            else:
                                if c:
                                    pe.matmul(psB[:, 1, cc], S[:, :], qd[:, h % 3, c, :], start=True, stop=False)
                                ins = pe.matmul(psB[:, 1, cc], vn[:, :], AT[:, h % 3, c, :], start=(c == 0), stop=True)
                                if c < CH - 1:
                                    ins = pe.matmul(psB[:, 0, P:2 * P], kd[:, h % 3, c, :], vn[:, :], start=True, stop=True)
                            ins.then_inc(scan_stage, 1)
                        elif kind == "C":
                            t, o = j, j % 2
                            e = int(s[-1]) if s[-1].isdigit() else 0
                            rows = slice(HD * e, HD * (e + 1))
                            kv = t // (SWQ // 2)
                            w = s.rstrip("01")
                            if w not in ("rot", "score", "turn", "pv"):
                                continue
                            pe.wait_ge(window_stage[o], C[o].before(t, s))
                            prob, probT, qr, sc = probs[o], probTs[o], qrs[o], ps[:, 2 + 2 * o:4 + 2 * o, :]
                            if w == "rot":
                                if t < 2:
                                    pe.wait_ge(tile_stage, E.end(("swq", SWQ - 1)))
                                    pe.wait_ge(scan_stage, B.end(HEADS - 1))
                                ins = pe.matmul(ps[:, 6 + o, :], k_("rot"), qraw[:, t, :], start=True, stop=True)
                            elif w == "score":
                                for n in range(CH):
                                    qn = qr[rows, n * P:(n + 1) * P]
                                    bank, a = n // 2, (n % 2) * 2 * P
                                    if n == 0:
                                        ins = pe.matmul(sc[:, 0, P:2 * P], qn, kk[rows, kv, 0:P], start=True, stop=True)
                                    else:
                                        ins = pe.matmul(sc[:, bank, a:a + 2 * P], qn, kk[rows, kv, (n - 1) * P:(n + 1) * P],
                                                        start=True, stop=True)
                            elif w == "turn":
                                pT = sc.rearrange("p b (c n) -> p (b c) n", n=P)
                                for i in range(2 * CH - 1):
                                    n, half = (i + 1) // 2, (i + 1) % 2
                                    ins = pe.transpose(pT[:, i, :], prob[:, n, half * P:(half + 1) * P], ident)
                            else:
                                for n in range(CH):
                                    out = ps[rows, 6 + o, n * P:(n + 1) * P]
                                    for half in ((0, 1) if n else (1,)):
                                        i = 2 * n + half - 1
                                        ins = pe.matmul(out, vtok[:, n - 1 + half, HD * kv:HD * (kv + 1)], probT[:, i, :],
                                                        start=(half == 0 or n == 0), stop=(half == 1))
                            ins.then_inc(window_stage[o], 1)
                        elif kind == "E" and s in ("rotk", "dupk", "turnv"):
                            pe.wait_ge(tile_stage, E.before(j, s))
                            if s == "rotk":
                                pe.wait_ge(gram_stage, D.end(HEADS - 1))
                                ins = pe.matmul(psD[:, 0, :], k_("rot"), tmp[:, :], start=True, stop=True)
                            elif s == "dupk":
                                pe.matmul(psD[:, 0, :], k_("dup0"), kr, start=True, stop=True)
                                ins = pe.matmul(psD[:, 1, :], k_("dup1"), kr, start=True, stop=True)
                            else:
                                for c in range(CH):
                                    ins = pe.transpose(psD[:, 0, c * P:(c + 1) * P], tmp[:, c * P:(c + 1) * P], ident)
                            ins.then_inc(tile_stage, 1)
                    pe.wait_ge(tile_stage, E.end(LT_TILES[-1]))
                    pe.matmul(ps[:, 7, :], k_("ones"), sq[:, 1, :], start=True, stop=True).then_inc(sum_done, 1)
            clear_all()

        par2 = at(par_at, 0, "par2", [P, NPARAM2])
        bmat = at(rope_at, 0, "bmat", [P, 2, SG, P])
        u = at(base_o, 0, "u", [P, SG, SEQ])
        za = at(base_o, 4 * TILE, "za", [P, SG, SEQ])
        turn_c = at(base_o, 8 * TILE, "turn_c", [P, 2, SEQ])
        turn_s = at(base_o, 10 * TILE, "turn_s", [P, 2, SEQ])
        turn_t = at(base_o, 12 * TILE, "turn_t", [P, SEQ])
        cmat = at(base_o, 13 * TILE, "cmat", [P, 2, ST, 32])
        big = at(base_o, 15 * TILE, "big", [P, 2, ST, TBH])
        craw = at(base_a, 0, "craw", [P, 2, ST, 32])
        ctmp = at(base_a, 2 * TILE, "ctmp", [P, 4, ST, 32])
        cols = at(base_a, 6 * TILE, "cols", [P, 20, ST])
        zb = at(base_r, 0, "zb", [P, SG, SEQ])
        t1, t2, zr, zi, sr, si = (at(base_r, (4 + i) * TILE, n, [P, SEQ]) for i, n in
                                  enumerate(("t1", "t2", "zr", "zi", "sr", "si")))
        mixed = at(base_r, 10 * TILE, "mixed", [P, SEQ])
        yaH, yaL = at(base_r, 0, "yaH", [P, SG, SEQ], F32R), at(base_r, 4 * TILE, "yaL", [P, SG, SEQ], F32R)
        sga_a, sga_b = at(base_s, 4 * TILE, "sga_a", [P, SG, SEQ]), at(base_s, 12 * TILE, "sga_b", [P, SG, SEQ])

        def sga(f):
            return (sga_a if f < SG else sga_b)[:, f % SG, :]

        def p2(name, i=None, n=1):
            a, b = PARAM2[name]
            return par2[:, a:b] if i is None else par2[:, a + i:a + i + n]

        mag = small[:, 0:ST]
        half_glu = small[:, ST:ST + SG]

        with nc.Block() as block:
            @block.sync
            def _(sp):
                sp.dma_start(par2[:, :], params2).then_inc(input_in, 16)
                sp.dma_start(bmat[:, :, :, :].rearrange("p a b c -> p (a b c)"), smallb).then_inc(input_in, 16)
                sp.dma_start(craw[:, :, :, :].rearrange("p a b c -> p (a b c)"), smallc).then_inc(input_in, 16)

            dt, ang, lr, ws, wc, k0, cr, ci, nr, ni, den2, q1, q2, q3, q4, cfr, cfi = (cols[:, i, :] for i in range(17))

            @block.scalar
            def _(act):
                act.wait_ge(input_in, 48)
                act.activation(dt, p2("log_dt"), ACT.Exp).then_inc(x_part, 1)
                act.wait_ge(setup, 2)
                act.activation(mag, lr, ACT.Exp).then_inc(x_part, 1)
                act.wait_ge(setup, 2 + 2 * RANGE_STEPS)
                act.activation(ci, ws, ACT.Sin).then_inc(x_part, 1)
                act.activation(cr, wc, ACT.Sin, bias=k_("halfpi")).then_inc(x_part, 1)

            @block.vector
            def _(v):
                step = [0]

                def link(ins):
                    step[0] += 1
                    ins.then_inc(setup, 1)
                    v.wait_ge(setup, step[0])

                def mul(o, a, b):
                    link(v.tensor_tensor(o, a, b, ALU.mult))

                v.wait_ge(x_part, 1)
                link(v.tensor_tensor(ang, p2("lam_im"), dt, ALU.mult))
                link(v.tensor_tensor(lr, p2("lam_re"), dt, ALU.mult))
                range_reduce(v, link, ws, ang, k0, 0.0)
                range_reduce(v, link, wc, ang, k0, 0.25)
                v.wait_ge(x_part, 4)
                link(v.tensor_scalar(half_glu, p2("b_glu"), 0.5, None, ALU.mult))
                mul(nr, mag, cr)
                link(v.tensor_scalar(nr, nr, 1.0, None, ALU.subtract))
                mul(ni, mag, ci)
                mul(q1, p2("lam_re"), p2("lam_re"))
                mul(q2, p2("lam_im"), p2("lam_im"))
                link(v.tensor_tensor(den2, q1, q2, ALU.add))
                link(v.reciprocal(den2, den2))
                mul(q1, nr, p2("lam_re"))
                mul(q2, ni, p2("lam_im"))
                link(v.tensor_tensor(cfr, q1, q2, ALU.add))
                mul(cfr, cfr, den2)
                mul(q1, ni, p2("lam_re"))
                mul(q2, nr, p2("lam_im"))
                link(v.tensor_tensor(cfi, q1, q2, ALU.subtract))
                mul(cfi, cfi, den2)
                wide = lambda a: a.unsqueeze(2).to_broadcast([P, ST, 32])
                mul(ctmp[:, 0], craw[:, 0], wide(cfr))
                mul(ctmp[:, 1], craw[:, 1], wide(cfi))
                mul(ctmp[:, 2], craw[:, 1], wide(cfr))
                mul(ctmp[:, 3], craw[:, 0], wide(cfi))
                link(v.tensor_tensor(cmat[:, 0], ctmp[:, 0], ctmp[:, 1], ALU.subtract))
                link(v.scalar_tensor_tensor(out=cmat[:, 1], in0=ctmp[:, 2], scalar=-1.0, in1=ctmp[:, 3],
                                            op0=ALU.mult, op1=ALU.subtract))
                for table, n in ((turn_small, TBL), (big, TBH)):
                    link(v.memset(table[:, 0, :, 0:1], 1.0))
                    link(v.memset(table[:, 1, :, 0:1], 0.0))
                    k = 1
                    while k < n:
                        a, b = table[:, 0, :, 0:k], table[:, 1, :, 0:k]
                        c = cr.unsqueeze(2).to_broadcast([P, ST, k])
                        d = ci.unsqueeze(2).to_broadcast([P, ST, k])
                        w = [ctmp[:, i, :, 0:k] for i in range(4)]
                        mul(w[0], a, c)
                        mul(w[1], b, d)
                        mul(w[2], a, d)
                        mul(w[3], b, c)
                        link(v.tensor_tensor(table[:, 0, :, k:2 * k], w[0], w[1], ALU.subtract))
                        link(v.tensor_tensor(table[:, 1, :, k:2 * k], w[2], w[3], ALU.add))
                        mul(q1, cr, cr)
                        mul(q2, ci, ci)
                        mul(q3, cr, ci)
                        link(v.tensor_tensor(cr, q1, q2, ALU.subtract))
                        link(v.tensor_scalar(ci, q3, 2.0, None, ALU.mult))
                        k *= 2
        clear_all()

        with nc.Block() as block:
            @block.sync
            def _(sp):
                for j in range(len(S_TILES)):
                    if j >= RAW:
                        sp.wait_ge(low_done, j - RAW + 1)
                    sp.dma_start(raw[:, j % RAW, :, :].rearrange("p t n -> p (t n)"), w2[j]).then_inc(loaded[j % RAW], 16)

            @block.gpsimd
            def _(pool):
                for kind, j, s in S_ORDER:
                    if kind == "split":
                        split_low(pool, j)
                    elif kind == "T":
                        pool.wait_ge(table_stage, T.before(j, s))
                        if s == "coscos" and j >= 2:
                            pool.wait_ge(state_stage, SS.before(j - 2, "state") + 1)
                        cc, ss, tt = turn_c[:, j % 2, :], turn_s[:, j % 2, :], turn_t[:, :]
                        grid = lambda ap: ap.rearrange("p (a b) -> p a b", b=TBL)
                        hi = lambda i: big[:, i, j, :].unsqueeze(2).to_broadcast([P, TBH, TBL])
                        lo = lambda i: turn_small[:, i, j, :].unsqueeze(1).to_broadcast([P, TBH, TBL])
                        if s == "coscos":
                            ins = pool.tensor_tensor(grid(cc), hi(0), lo(0), ALU.mult)
                        elif s == "sinsin":
                            ins = pool.tensor_tensor(grid(tt), hi(1), lo(1), ALU.mult)
                        elif s == "cos":
                            ins = pool.tensor_tensor(cc, cc, tt, ALU.subtract)
                        elif s == "cossin":
                            ins = pool.tensor_tensor(grid(ss), hi(0), lo(1), ALU.mult)
                        elif s == "sincos":
                            ins = pool.tensor_tensor(grid(tt), hi(1), lo(0), ALU.mult)
                        else:
                            ins = pool.tensor_tensor(ss, ss, tt, ALU.add)
                        ins.then_inc(table_stage, 1)
                    elif kind == "E" and j[0] == "ub" and s == "low":
                        pool.wait_ge(tile_stage, E2.before(j, s))
                        i = j[1]
                        pool.tensor_tensor(SL[:, SG + i, :], mixed[:, :], SH[:, SG + i, :].bitcast(F32),
                                           ALU.subtract).then_inc(tile_stage, 1)

            @block.scalar
            def _(act):
                def high(j):
                    act.wait_ge(loaded[j % RAW], 16 * (j // RAW + 1))
                    if j >= SPLIT:
                        act.wait_ge(tile_done, S_OUT_AT[outputs_of(S_TILES[j - SPLIT])[-1]] + 1)
                    act.activation(wH[:, j % SPLIT, :, :], raw[:, j % RAW, :, :], ACT.Copy).then_inc(high_done, 1)

                high(0)
                x_high(act, lambda t: p2("norm", t), 0, None)
                root_scalar(act, ssq_done, KT, rstd[:, :], ps[:, 7, :], 1.0 / D_MODEL, "eps", root_done)
                for kind, j, s in S_ORDER[1:]:
                    if kind == "split":
                        high(j)
                    elif kind == "S" and s in ("gelu", "highs"):
                        act.wait_ge(state_stage, SS.before(j, s))
                        if s == "gelu":
                            act.activation(u[:, j // 4, :], u[:, j // 4, :], ACT.Gelu_apprx_tanh).then_inc(state_stage, 1)
                        else:
                            act.wait_ge(tile_stage, E2.end(("bb", KT - 1)))
                            act.activation(SH[:, 0:SG, :], u[:, :, :], ACT.Copy).then_inc(state_stage, 1)
                    elif kind == "E" and s in ("tanh", "high", "square"):
                        kd_, i = j
                        act.wait_ge(tile_stage, E2.before(j, s))
                        if kd_ == "glu" and s == "tanh":
                            n = S_OUT_AT[j]
                            act.wait_ge(tile_done, n + 1)
                            ins = act.activation(tmp[:, :], ps[:, n % 2, :], ACT.Tanh, scale=0.5, bias=half_glu[:, i:i + 1])
                        elif s == "tanh" and kd_ in ("za", "zb"):
                            ins = act.activation(tmp[:, :], (za if kd_ == "za" else zb)[:, i, :], ACT.Tanh, scale=0.5)
                        elif s == "tanh":
                            g = acc[:, i, :] if kd_ == "gb" else sga(i)
                            ins = act.activation(g, g, ACT.Tanh, scale=0.5)
                        elif s == "high":
                            dst, f = {"ub": (SH[:, (SG + i) % KT, :], 1.0), "pw": (SH[:, i, :], 0.5),
                                      "glu": (yaH[:, i % SG, :], 0.25), "ba": (OH[:, i, :], 0.5)}[kd_]
                            ins = act.activation(dst, mixed[:, :], ACT.Copy, scale=f)
                        else:
                            ins = act.activation(sq[:, 0, :], x[:, i, :], ACT.Square)
                        ins.then_inc(tile_stage, 1)
                root_scalar(act, sum_done, 1, rstdp[:, :], ps[:, 7, :], 1.0 / D_MODEL, "eps", post_root)

            @block.vector
            def _(v):
                for t in range(KT):
                    x_low(v, t, lambda t: p2("norm", t), 0)
                v.wait_ge(root_done, 1)
                v.reciprocal(rstd[:, :], rstd[:, :]).then_inc(rstd_ready, 1)
                v.wait_ge(rstd_ready, 1)
                for kind, j, s in S_ORDER[1:]:
                    if kind == "S" and s not in ("input", "output", "gelu", "highs"):
                        v.wait_ge(state_stage, SS.before(j, s))
                        cc, ss = turn_c[:, j % 2, :], turn_s[:, j % 2, :]
                        mul = lambda o, a, b: v.tensor_tensor(o[:, :], a, b, ALU.mult)
                        if s == "turn":
                            v.wait_ge(table_stage, T.end(j))
                            mul(t1, cc, psA[:, 0, :])
                            mul(t2, ss, psA[:, 1, :])
                            mul(sr, cc, psA[:, 1, :])
                            ins = mul(si, ss, psA[:, 0, :])
                        elif s == "turned":
                            v.tensor_tensor(zr[:, :], t1[:, :], t2[:, :], ALU.add)
                            ins = v.tensor_tensor(zi[:, :], sr[:, :], si[:, :], ALU.subtract)
                        elif s == "scan":
                            decay = mag[:, j:j + 1].to_broadcast([P, SEQ])
                            v.tensor_tensor_scan(t1[:, :], decay, zr[:, :], 0.0, ALU.mult, ALU.add)
                            ins = v.tensor_tensor_scan(t2[:, :], decay, zi[:, :], 0.0, ALU.mult, ALU.add)
                        elif s == "back":
                            mul(zr, cc, t1[:, :])
                            mul(zi, ss, t2[:, :])
                            mul(sr, cc, t2[:, :])
                            ins = mul(si, ss, t1[:, :])
                        elif s == "state":
                            v.tensor_tensor(zr[:, :], zr[:, :], zi[:, :], ALU.subtract)
                            ins = v.tensor_tensor(sr[:, :], sr[:, :], si[:, :], ALU.add)
                        elif s == "skip":
                            c = j // 4
                            ins = v.scalar_tensor_tensor(out=u[:, c, :], in0=u[:, c, :], scalar=p2("d", c),
                                                         in1=ps[:, 4, :], op0=ALU.mult, op1=ALU.add)
                        else:
                            ins = v.tensor_tensor(SL[:, 0:SG, :], u[:, :, :], SH[:, 0:SG, :].bitcast(F32), ALU.subtract)
                        ins.then_inc(state_stage, 1)
                    elif kind == "E":
                        kd_, i = j
                        n = S_OUT_AT[j]
                        b = ps[:, n % 2, :]
                        if s in ("tanh", "high", "square") or (kd_ == "ub" and s == "low"):
                            continue
                        v.wait_ge(tile_stage, E2.before(j, s))
                        if s == e2_stages(j)[0]:
                            v.wait_ge(tile_done, n + 1)
                        if s in ("scale", "bias") and kd_ != "pw":
                            dst = {"ua": lambda: u[:, i, :], "za": lambda: za[:, i, :], "ub": lambda: tmp[:, :],
                                   "zb": lambda: zb[:, i, :], "gb": lambda: acc[:, i, :], "ga": lambda: sga(i)}[kd_]()
                            if s == "scale":
                                ins = v.tensor_tensor(dst, b, rstd[:, :], ALU.mult)
                            else:
                                ins = v.tensor_scalar(dst, dst, p2("b_in", IN2[kd_] + i), None, ALU.add)
                        elif s == "silu" and kd_ != "glu":
                            z = (za if kd_ == "za" else zb)[:, i, :]
                            ins = v.scalar_tensor_tensor(out=z, in0=tmp[:, :], scalar=1.0, in1=z, op0=ALU.add, op1=ALU.mult)
                        elif s.startswith("sum") and kd_ == "ub":
                            m = int(s[-1])
                            d = 2 ** m
                            src = tmp if m == 0 else sq[:, (m - 1) % 2, :]
                            dst = sq[:, m % 2, :]
                            v.tensor_copy(dst[:, 0:d], src[:, 0:d])
                            ins = v.tensor_tensor(dst[:, d:], src[:, d:SEQ], src[:, 0:SEQ - d], ALU.add)
                        elif s == "mean":
                            win = 2 ** (i + 1)
                            src = sq[:, i % 2, :]
                            v.scalar_tensor_tensor(out=mixed[:, :], in0=src, scalar=1.0 / win, in1=tmp[:, :],
                                                   op0=ALU.mult, op1=ALU.subtract)
                            ins = v.tensor_tensor(small[:, 32:32 + win], src[:, 0:win], k_("invcount")[:, 0:win], ALU.mult)
                        elif s == "early":
                            win = 2 ** (i + 1)
                            ins = v.tensor_tensor(mixed[:, 0:win], small[:, 32:32 + win], tmp[:, 0:win], ALU.subtract)
                        elif kd_ == "pw" and s == "scale":
                            ins = v.scalar_tensor_tensor(out=mixed[:, :], in0=b, scalar=p2("pool_scale", i), in1=zb[:, i, :],
                                                         op0=ALU.mult, op1=ALU.mult)
                        elif s == "low":
                            f, hi_, dst = {"pw": (0.5, SH[:, i, :], SL[:, i, :]), "glu": (0.25, yaH[:, i % SG, :], yaL[:, i % SG, :]),
                                           "ba": (0.5, OH[:, i, :], OL[:, i, :])}[kd_]
                            ins = v.scalar_tensor_tensor(out=dst, in0=mixed[:, :], scalar=f, in1=hi_.bitcast(F32),
                                                         op0=ALU.mult, op1=ALU.subtract)
                        elif s == "gate" and kd_ == "bb":
                            ins = v.scalar_tensor_tensor(out=acc[:, i, :], in0=acc[:, i, :], scalar=1.0, in1=b, op0=ALU.add, op1=ALU.mult)
                        elif s == "gate" and kd_ == "glu":
                            ins = v.scalar_tensor_tensor(out=tmp[:, :], in0=tmp[:, :], scalar=1.0, in1=u[:, i, :], op0=ALU.add, op1=ALU.mult)
                        elif s == "silu":
                            ins = v.tensor_tensor(mixed[:, :], tmp[:, :], za[:, i, :], ALU.mult)
                        elif s == "gate":
                            ins = v.scalar_tensor_tensor(out=mixed[:, :], in0=sga(i), scalar=1.0, in1=b, op0=ALU.add, op1=ALU.mult)
                        elif s == "add" and kd_ == "ba":
                            ins = v.tensor_tensor(mixed[:, :], mixed[:, :], acc[:, i, :], ALU.add)
                        elif s == "add":
                            ins = v.tensor_tensor(x[:, i, :], x[:, i, :], b, ALU.add)
                        elif s == "sum" and i == 0:
                            ins = v.tensor_copy(sq[:, 1, :], sq[:, 0, :])
                        else:
                            ins = v.tensor_tensor(sq[:, 1, :], sq[:, 1, :], sq[:, 0, :], ALU.add)
                        ins.then_inc(tile_stage, 1)
                v.wait_ge(post_root, 1)
                v.reciprocal(rstdp[:, :], rstdp[:, :]).then_inc(post_ready, 1)
                v.wait_ge(post_ready, 1)
                for t in range(KT):
                    v.scalar_tensor_tensor(out=acc[:, t, :], in0=x[:, t, :], scalar=p2("final", t), in1=rstdp[:, :],
                                           op0=ALU.mult, op1=ALU.mult).then_inc(x_ready, 1)

            @block.tensor
            def _(pe):
                for kind, j, s in S_ORDER:
                    if kind == "mm":
                        tile = S_TILES[j]
                        kd_, i = tile
                        outs = outputs_of(tile)
                        each = PARTS // len(outs)
                        o, part = outs[s // each], s % each
                        n = S_OUT_AT[o]
                        depth = S_DEPTH.get(kd_, KT)
                        if s == 0:
                            pe.wait_ge(low_done, j + 1)
                        if part == 0 and n >= 2:
                            pe.wait_ge(tile_stage, E2.before(S_OUT[n - 2], e2_stages(S_OUT[n - 2])[0]) + 1)
                        if s == 0:
                            if kd_ == "pw":
                                pe.wait_ge(tile_stage, E2.end(("ub", SG - 1)))
                            if tile == ("bb", 0):
                                pe.wait_ge(tile_stage, E2.end(("pw", SG - 1)))
                            if tile == ("glu", 0):
                                pe.wait_ge(state_stage, SS.end(ST - 1))
                            if tile == ("ba", 0):
                                pe.wait_ge(tile_stage, E2.end(("glu", SG - 1)))
                            if tile == ("wo", 0):
                                pe.wait_ge(tile_stage, E2.end(("ba", KT - 1)))
                        rH, rL = {"pw": lambda: (SH[:, SG + o[1]:, :], SL[:, SG + o[1]:, :]), "bb": lambda: (SH, SL),
                                  "glu": lambda: (SH, SL), "ba": lambda: (yaH, yaL),
                                  "wo": lambda: (OH, OL)}.get(kd_, lambda: (hH, hL))()
                        before = None
                        if tile == ("ua", 0):
                            def before(t):
                                pe.wait_ge(h_low, t + 1)
                                x_sum(pe, 0, t)
                        products(pe, j, part, ps[:, n % 2, :], rH, rL, depth, kt0=(s // each) * depth, parts=each,
                                 before=before)
                    elif kind == "S" and s in ("input", "output"):
                        pe.wait_ge(state_stage, SS.before(j, s))
                        c, r = j // 4, slice(32 * (j % 4), 32 * (j % 4 + 1))
                        if s == "input":
                            if j % 4 == 0:
                                pe.wait_ge(tile_stage, E2.end(("ua", c)))
                            pe.matmul(psA[:, 0, :], bmat[r, 0, c, :], u[r, c, :], start=True, stop=True)
                            ins = pe.matmul(psA[:, 1, :], bmat[r, 1, c, :], u[r, c, :], start=True, stop=True)
                        else:
                            pe.matmul(ps[r, 4, :], cmat[:, 0, j, :], zr[:, :], start=True, stop=False)
                            ins = pe.matmul(ps[r, 4, :], cmat[:, 1, j, :], sr[:, :], start=False, stop=True)
                        ins.then_inc(state_stage, 1)
                pe.wait_ge(tile_stage, E2.end(("wo", KT - 1)))
                pe.matmul(ps[:, 7, :], k_("ones"), sq[:, 1, :], start=True, stop=True).then_inc(sum_done, 1)
        with nc.Block() as block:
            @block.sync
            def _(sp):
                sp.dma_start(outT, acc[:, :, :]).then_inc(out_done, 16)
                sp.wait_ge(out_done, 16)


RANGE_STEPS = 6


def range_reduce(v, link, out, ang, k, quarter):
    two_pi = 2 * np.pi
    p1 = 6.28125
    p2 = float(np.float32(0.00193500518798828125))
    p3 = float(np.float32(two_pi - p1 - p2))
    magic = 1.5 * 2.0 ** 23
    link(v.tensor_scalar(k, ang, 1.0 / two_pi, quarter, ALU.mult, ALU.add))
    link(v.tensor_scalar(k, k, magic, None, ALU.add))
    link(v.tensor_scalar(k, k, magic, None, ALU.subtract))
    link(v.scalar_tensor_tensor(out=out, in0=k, scalar=-p1, in1=ang, op0=ALU.mult, op1=ALU.add))
    link(v.scalar_tensor_tensor(out=out, in0=k, scalar=-p2, in1=out, op0=ALU.mult, op1=ALU.add))
    link(v.scalar_tensor_tensor(out=out, in0=k, scalar=-p3, in1=out, op0=ALU.mult, op1=ALU.add))


def kernel(**inputs):
    import concourse.bacc as bacc
    from concourse.bass_utils import run_bass_kernel_spmd

    a = {n: np.asarray(v) for n, v in inputs.items()}

    def tiles(w, depth=KT):
        n = w.shape[-1] // P
        return w.reshape(depth, P, n, P).transpose(2, 1, 0, 3).reshape(n, P, depth * P)

    def columns(g):
        return g.reshape(-1, P).T

    def every(g):
        return np.broadcast_to(g[None, :], (P, g.size))

    w1, params = [], []
    for l in range(DEPTH):
        wi = a["w_in"][l]
        o = np.cumsum([0, 1024, 1024, 1024, 1024, 16, 1024, 128, 128, 1024, 1024])
        t = {n: tiles(wi[:, o[i]:o[i + 1]]) for i, n in enumerate(("q", "k", "v", "z", None, "swq", "swk", "swv", "ga", "gb")) if n}
        ab = np.zeros((P, KT, P), np.float32)
        ab[:, :, 0:16] = wi[:, o[4]:o[5]].reshape(KT, P, 16).transpose(1, 0, 2)
        t["ab"] = ab.reshape(1, P, D_MODEL)
        t["ya"], t["yb"], t["wo"] = (tiles(a[n][l]) for n in ("w_up_dn", "w_up_sw", "w_o"))
        t["f1"] = tiles(a["w_ff1"][l])
        t["f2"] = np.concatenate([tiles(a["w_ff2"][l][c * D_MODEL:(c + 1) * D_MODEL]) for c in range(FFC)])
        w1.append(np.stack([t[k][i] for k, i in LT_TILES]))
        conv = a["dn_conv_w"][l].reshape(CONV, 3 * HEADS, P).transpose(2, 1, 0).reshape(P, -1)
        params.append(np.concatenate([columns(a[n][l]) for n in ("pre_mix_g", "post_mix_g", "pre_mlp_g", "post_mlp_g")]
                                     + [conv, a["dn_norm_g"][l][:, None], every(a["dn_a_log"][l]),
                                        every(a["dn_dt_bias"][l]), every(a["sw_sinks"][l])], axis=1))
    w = a["w_in_2"][0]
    t = {k: tiles(w[:, P * i:P * (i + n)]) for k, i, n in (("ua", IN2["ua"], SG), ("za", IN2["za"], SG), ("ub", IN2["ub"], SG),
                                                           ("zb", IN2["zb"], SG), ("ga", IN2["ga"], KT), ("gb", IN2["gb"], KT))}

    def pairs(w):
        h = tiles(w, SG)
        return h.reshape(-1, 2, P, SG * P).transpose(0, 2, 1, 3).reshape(-1, P, 2 * SG * P)

    t["bb"], t["ba"], t["glu"] = pairs(a["w_branch_b_2"][0]), pairs(a["w_branch_a_2"][0]), pairs(a["ssm_w_glu_2"][0])
    t["pw"] = np.zeros((1, P, D_MODEL), np.float32)
    t["pw"][0, :, 0:SG * P] = a["pool_w_2"][0].transpose(1, 0, 2).reshape(P, SG * P)
    t["wo"] = tiles(a["w_out_2"][0])
    states = lambda v: v.reshape(ST, P).T
    log_dt = np.broadcast_to(a["ssm_log_dt_2"][0][:, None], (2 * ST, P // 2))
    params2 = np.concatenate([columns(a[n][0]) for n in ("norm_g_2",)] + [columns(a["final_norm_g_2"])]
                             + [columns(a[n][0]) for n in ("b_in_2", "ssm_d_2", "ssm_b_glu_2", "pool_scale_2")]
                             + [states(a["ssm_lam_re_2"][0]), states(a["ssm_lam_im_2"][0]), states(log_dt)], axis=1)
    smallb = np.zeros((2, P, SG, P), np.float32)
    smallc = np.zeros((2, P, ST, 32), np.float32)
    for i, (nb, ncm) in enumerate((("ssm_b_re_2", "ssm_c_re_2"), ("ssm_b_im_2", "ssm_c_im_2"))):
        for g in range(2 * ST):
            st, e = g // 2, g % 2
            row, col = 32 * (st % 4) + 16 * e, 64 * e
            smallb[i, row:row + 16, st // 4, col:col + 64] = a[nb][0, g].T
            smallc[i, col:col + 64, st, 16 * e:16 * e + 16] = a[ncm][0, g].T
    data = {
        "w2": np.stack([t[k][i] for k, i in S_TILES]),
        "params2": params2,
        "smallb": smallb.transpose(1, 0, 2, 3).reshape(P, -1),
        "smallc": smallc.transpose(1, 0, 2, 3).reshape(P, -1),
        "xT": a["x"][0].T.reshape(KT, P, SEQ).transpose(1, 0, 2),
        "pos": a["positions"].reshape(1, SEQ),
        "consts": constants(),
        "params": np.stack(params),
        "w1": np.stack(w1),
    }
    nc = bacc.Bacc("TRN2", target_bir_lowering=False, num_devices=1)
    data = {n: np.ascontiguousarray(v) for n, v in data.items()}
    aps = {n: nc.dram_tensor(n, v.shape, mybir.dt.from_np(v.dtype), kind="ExternalInput").ap() for n, v in data.items()}
    outT = nc.dram_tensor("outT", (P, KT, SEQ), F32, kind="ExternalOutput").ap()
    build(nc, aps["xT"], aps["pos"], aps["consts"], aps["params"], aps["w1"], aps["w2"], aps["params2"],
          aps["smallb"], aps["smallc"], outT)
    r = run_bass_kernel_spmd(nc, [data], core_ids=[0])
    got = r.results[0]["outT"]
    return got.transpose(1, 0, 2).reshape(1, D_MODEL, SEQ).transpose(0, 2, 1)
```

```python
from contextlib import ExitStack

import numpy as np
import concourse.bass as bass
from concourse import mybir

F32 = mybir.dt.float32
F32R = mybir.dt.float32r
I32 = mybir.dt.int32
ALU = mybir.AluOpType
ACT = mybir.ActivationFunctionType
AX = mybir.AxisListType

P = 128
SEQ, D_MODEL, DEPTH, D_FF = 512, 1024, 2, 4096
KT = D_MODEL // P
HEADS, CONV = 8, 4
CH = SEQ // P
SWQ = 8
HD = 64
FFC = D_FF // D_MODEL
EPS = 1e-6
NEG = -1e30
LEVELS = (2, 4, 8, 16, 32, 64)
SG = 4
ST = 16
TBL = 32
TBH = SEQ // TBL
RAW, SPLIT = 3, 2
PARTS = 8

def layer_tiles():
    out = [("ab", 0)]
    for h in range(HEADS):
        out += [("q", h), ("k", h), ("v", h), ("z", h)]
    out += [("swk", 0), ("swv", 0)] + [("swq", t) for t in range(SWQ)]
    for f in range(KT):
        out += [("ga", f), ("ya", f)]
    for f in range(KT):
        out += [("gb", f), ("yb", f)]
    out += [("wo", f) for f in range(KT)]
    up = lambda c: [("f1", 8 * c + j) for j in range(8)]
    down = lambda c: [("f2", 8 * c + j) for j in range(8)]
    out += up(0)
    for c in range(1, FFC):
        out += up(c) + down(c - 1)
    return out + down(FFC - 1)


def second_tiles():
    out = [("ua", i) for i in range(SG)] + [("za", i) for i in range(SG)]
    out += [("ub", i) for i in range(SG)] + [("zb", i) for i in range(SG)] + [("pw", 0)]
    out += [("gb", f) for f in range(KT)] + [("bb", i) for i in range(KT // 2)]
    out += [("ga", f) for f in range(KT - 1)] + [("glu", i) for i in range(SG // 2)] + [("ga", KT - 1)]
    return out + [("ba", i) for i in range(KT // 2)] + [("wo", f) for f in range(KT)]


OUTS = {"pw": SG, "bb": 2, "glu": 2, "ba": 2}
S_DEPTH = {"pw": 1, "bb": SG, "glu": SG, "ba": SG}


def outputs_of(tile):
    kind, i = tile
    n = OUTS.get(kind, 1)
    return [(kind, n * i + o) for o in range(n)]


LT_TILES = layer_tiles()
L_AT = {t: i for i, t in enumerate(LT_TILES)}
S_TILES = second_tiles()
S_AT = {t: i for i, t in enumerate(S_TILES)}

CONST = {}
_at = 0
for _name, _n in [("ident", P), ("ones", P), ("upper", P), ("first", P), ("levels", P * len(LEVELS)), ("rot", P),
                  ("dup0", P), ("dup1", P), ("window", 2 * P), ("invfreq", 1), ("isrot", 1), ("notrot", 1),
                  ("eps", 1), ("eps4", 1), ("halfpi", 1), ("invcount", 16)]:
    CONST[_name] = (_at, _at + _n)
    _at += _n
NCONST = _at

PARAM = {}
_at = 0
for _name, _n in [("pre_mix", KT), ("post_mix", KT), ("pre_mlp", KT), ("post_mlp", KT), ("next", KT), ("conv", CONV * 3 * HEADS),
                  ("norm", 1), ("a_log", HEADS), ("dt_bias", HEADS), ("sinks", 2 * SWQ)]:
    PARAM[_name] = (_at, _at + _n)
    _at += _n
NPARAM = _at


PARAM2 = {}
_at = 0
for _name, _n in [("final", KT), ("b_in", D_MODEL * 4 // P), ("d", SG), ("b_glu", SG), ("pool_scale", SG),
                  ("lam_re", ST), ("lam_im", ST), ("log_dt", ST)]:
    PARAM2[_name] = (_at, _at + _n)
    _at += _n
NPARAM2 = _at
IN2 = {"ua": 0, "za": SG, "ub": 2 * SG, "zb": 3 * SG, "ga": 4 * SG, "gb": 4 * SG + KT}


def constants():
    c = np.zeros((P, NCONST), np.float32)
    i, j = np.arange(P)[:, None], np.arange(P)[None, :]

    def put(name, v):
        c[:, CONST[name][0]:CONST[name][1]] = v

    put("ident", i == j)
    put("ones", 1.0)
    put("upper", i <= j)
    put("first", (i % 2 == 0) & (j == i + 1))
    put("levels", np.concatenate([(i // (2 * s) == j // (2 * s)) & (i % (2 * s) >= s) & (j % (2 * s) < s)
                                  for s in LEVELS], axis=1))
    r = i % HD
    half = HD // 8
    rj = j % HD
    put("rot", -1.0 * ((rj < half) & (i == j + half)) + 1.0 * ((rj >= half) & (rj < 2 * half) & (i == j - half)))
    put("dup0", i == j % HD)
    put("dup1", i == j % HD + HD)
    q, k = np.arange(P)[:, None] + P, np.arange(2 * P)[None, :]
    put("window", np.where((q - k >= 0) & (q - k < P), 0.0, NEG))
    p = np.arange(P)[:, None]
    inv = np.float32(500000.0) ** (-(p % half).astype(np.float32) * np.float32(2.0 / (2 * half)))
    put("invfreq", np.where(p % HD < 2 * half, inv, 0.0))
    put("isrot", p % HD < 2 * half)
    put("notrot", p % HD >= 2 * half)
    put("eps", EPS)
    put("eps4", 4 * EPS)
    put("halfpi", np.pi / 2)
    put("invcount", 1.0 / np.arange(1, 17)[None, :])
    return c


class Count:

    def __init__(self, rounds):
        self.value = {}
        n = 0
        for key, stages in rounds:
            for s in stages:
                self.value[key, s] = n
                n += 1
            self.value[key, "end"] = n

    def before(self, key, stage):
        return self.value[key, stage]

    def end(self, key):
        return self.value[key, "end"]


E_STAGES = {
    "ab": ["scale"],
    "q": ["scale", "tap3", "tap2", "tap1", "tap0", "tanh", "silu"],
    "z": ["scale", "tanh", "silu"],
    "swk": ["scale", "cosk", "rotk", "sink", "addk", "dupk", "copyk"],
    "swv": ["scale", "turnv", "copyv"],
    "swq": ["scale"],
    "ga": ["scale", "tanh"],
    "ya": ["gate"],
    "yb": ["gate", "add", "high", "low"],
    "wo": ["copy", "square", "gain", "sum"],
    "f1": ["scale", "relu2", "high", "low"],
}
E_STAGES["k"] = E_STAGES["v"] = E_STAGES["q"]
E_STAGES["gb"] = E_STAGES["ga"]


def e_stages(tile):
    kind, i = tile
    if kind == "f2":
        return (["copy"] if i < 8 else ["add"]) + (["square", "gain", "sum"] if i >= 8 * (FFC - 1) else [])
    return E_STAGES[kind]


G_STAGES = ["turn", "copy", "tanh", "beta", "hbeta", "addb", "max", "abs", "expn", "plus1", "ln", "sp", "expa", "g",
            "cumsum", "copyc", "diff", "exps", "nbeg"]
D_STAGES = ["square", "sums", "root", "recip", "scales", "rows", "kbeta", "diff", "exps", "qdec", "mask", "gram",
            "masked", "first", "minus", "turnkv", "copykv"]
A_STAGES = ["turni", "copyi"] + [f"{s}{v}" for v in range(len(LEVELS))
                                 for s in (["p", "pmask", "q", "update"] + (["turn", "copy"] if v < len(LEVELS) - 1 else []))]
B_STAGES = (["v0", "copyv0", "o0", "state0"]
            + [f"{s}{c}" for c in range(1, CH)
               for s in (["r", "rr", "v", "copyv", "o"] + (["state"] if c < CH - 1 else []))]
            + ["square", "sums", "mean", "root", "recip", "factor", "row", "norm", "high", "low"])
C_STAGES = (["rot", "cos", "sin", "addq"]
            + [f"{s}{e}" for e in range(2)
               for s in ("score", "mask", "max", "maxs", "neg", "exp", "den", "recip", "prob", "turn", "copy", "pv")]
            + ["high", "low"])

TBL_STEPS, TBH_STEPS = TBL.bit_length() - 1, TBH.bit_length() - 1
Z_STAGES = (["dt", "angles", "mag", "reduce", "sines", "input", "maps0", "maps1"]
            + [f"double{m}" for m in range(TBL_STEPS + TBH_STEPS)])
T_STAGES = ["coscos", "sinsin", "cos", "cossin", "sincos", "sin"]

E = Count([(t, e_stages(t)) for t in LT_TILES])
G = Count([(0, G_STAGES)])
A = Count([(h, A_STAGES) for h in range(HEADS)])
B = Count([(h, B_STAGES) for h in range(HEADS)])
D = Count([(h, D_STAGES) for h in range(HEADS)])
C = [Count([(t, C_STAGES) for t in range(e, SWQ, 2)]) for e in range(2)]


def ordered(chains, needs, engine_of, micros, hop):
    heads = [0] * len(chains)
    ended = {}
    free = {}
    out = []
    left = sum(len(c) for c in chains)
    while left:
        best = None
        for n, chain in enumerate(chains):
            if heads[n] == len(chain):
                continue
            e = chain[heads[n]]
            before = needs(e) + ([chain[heads[n] - 1]] if heads[n] else [])
            if any(b not in ended for b in before):
                continue
            start = max([free.get(engine_of(e), 0.0)] + [ended[b] + hop for b in before])
            if best is None or start < best[0] - 1e-9:
                best = (start, n, e)
        start, n, e = best
        free[engine_of(e)] = ended[e] = start + micros(e)
        heads[n] += 1
        left -= 1
        out.append(e)
    return out


LENGTH = {"pe": 0.85, "act": 0.65, "vector": 0.72, "pool": 1.15}


def engine_of(e):
    kind, j, s = e
    if kind == "mm":
        return "pe"
    if kind in ("split_high", "split_low"):
        return {"split_high": "act", "split_low": "pool"}[kind]
    return LAYER_ENGINES.get((kind, s)) or LAYER_ENGINES.get((kind, s.rstrip("0123456789")), "vector")


LAYER_ENGINES = {}
for _engine, _kind, _stages in [
        ("pe", "G", "turn cumsum"), ("act", "G", "tanh abs expn ln expa exps"),
        ("pe", "D", "sums rows gram turnkv"), ("act", "D", "square root exps copykv"), ("pool", "D", "qdec mask"),
        ("pe", "A", "turni p q turn"), ("act", "A", "copyi copy"),
        ("pe", "B", "v o r sums row"), ("act", "B", "copyv square root high"), ("pool", "B", "low"),
        ("pe", "C", "rot score turn pv"), ("act", "C", "exp copy high"),
        ("pe", "E", "rotk dupk turnv"), ("act", "E", "tap3 tanh copyk copyv high square gain"), ("pool", "E", "low"),
        ("act", "Z", "dt mag sines"), ("pool", "T", " ".join(T_STAGES)), ("pe", "S", "input output"), ("act", "S", "gelu highs")]:
    for _s in _stages.split():
        LAYER_ENGINES[_kind, _s] = _engine


def micros(e):
    kind, j, s = e
    if kind == "mm":
        return 5.12 / PARTS
    if kind == "split_high":
        return 1.1
    if kind == "split_low":
        return 2.2
    name = s.rstrip("0123456789") if s else s
    if kind == "G":
        return 0.25
    special = {("A", "q"): 0.45, ("A", "update"): 0.45, ("A", "turn"): 0.6, ("B", "v"): 0.25, ("B", "r"): 0.25,
               ("B", "o"): 0.65, ("B", "copyv"): 0.25, ("B", "rr"): 0.25, ("B", "state"): 0.25, ("B", "root"): 1.4,
               ("B", "factor"): 0.1, ("B", "recip"): 0.1, ("B", "mean"): 0.85, ("B", "sums"): 0.2,
               ("D", "square"): 1.25, ("D", "sums"): 0.3, ("D", "root"): 1.4, ("D", "recip"): 0.1, ("D", "scales"): 0.4,
               ("D", "rows"): 1.7, ("D", "gram"): 1.7, ("D", "turnkv"): 1.2, ("D", "masked"): 1.5, ("D", "copykv"): 1.9,
               ("D", "exps"): 1.25, ("C", "score"): 1.5, ("C", "mask"): 1.3, ("C", "max"): 1.0, ("C", "maxs"): 0.1,
               ("C", "neg"): 0.1, ("C", "den"): 0.1, ("C", "recip"): 0.1, ("C", "exp"): 1.5, ("C", "prob"): 1.1,
               ("C", "turn"): 1.2, ("C", "copy"): 1.1, ("C", "pv"): 1.5, ("E", "dupk"): 1.7, ("E", "copyk"): 1.25,
               ("Z", "double"): 2.0, ("Z", "reduce"): 2.0, ("Z", "input"): 1.5, ("Z", "maps"): 2.2,
               ("S", "input"): 1.7, ("S", "turn"): 2.8, ("S", "turned"): 1.4, ("S", "scan"): 1.6, ("S", "back"): 2.8,
               ("S", "state"): 1.4, ("S", "output"): 1.7, ("S", "highs"): 2.2, ("S", "lows"): 2.8}
    return special.get((kind, name), LENGTH[engine_of(e)])


def slack1(e):
    kind, j, s = e
    if engine_of(e) == "pe" or kind in ("split_high", "split_low", "Z"):
        f = 1.0
    elif kind == "C":
        f = 1.2
    else:
        last_heads = j[0].startswith("sw") if kind == "E" else j >= HEADS - 2
        f = 0.9 if last_heads else 1.25
    return micros(e) * f


def slack2(e):
    return micros2(e) * (1.0 if engine2_of(e) == "pe" else 0.9)


def pieces(tiles):
    return [("mm", j, p) for j in range(len(tiles)) for p in range(PARTS)]


def layer_order():
    def e_first(t):
        return ("E", t, e_stages(t)[0])

    def e_last(t):
        return ("E", t, e_stages(t)[-1])

    def last(kind, h):
        return (kind, h, {"A": A_STAGES, "B": B_STAGES, "C": C_STAGES, "D": D_STAGES, "G": G_STAGES}[kind][-1])

    def needs(e):
        kind, j, s = e
        out = []
        if kind == "split_high" and j >= SPLIT:
            out = [("mm", j - SPLIT, PARTS - 1)]
        if kind == "split_low":
            out = [("split_high", j, None)]
        if kind == "mm" and s == 0:
            t = LT_TILES[j]
            out = [("split_low", j, None)] if j else []
            if j >= 2:
                out.append(e_first(LT_TILES[j - 2]))
            if t == ("ya", 0):
                out.append(last("B", HEADS - 1))
            if t == ("yb", 0):
                out += [last("C", SWQ - 1), last("C", SWQ - 2)]
            if t == ("wo", 0):
                out.append(e_last(("yb", KT - 1)))
            if t == ("f1", 0):
                out.append(e_last(("wo", KT - 1)))
            if t[0] == "f2" and t[1] % 8 == 0:
                out.append(e_last(("f1", t[1] + 7)))
        if kind == "E":
            if s == e_stages(j)[0]:
                out.append(("mm", L_AT[j], PARTS - 1))
            k, i = j
            if k == "q" and s == "tap3" and i >= 2:
                out.append(last("D", i - 2))
                if i >= 4:
                    out.append(last("B", i - 4))
            if s == "scale":
                if j == ("swq", 0):
                    out += [last("B", HEADS - 3), last("D", HEADS - 1)]
                if j == ("swq", SWQ // 2):
                    out.append(last("B", HEADS - 2))
                if j == ("ga", 0):
                    out.append(last("B", HEADS - 1))
            if s == "rotk":
                out.append(last("D", HEADS - 1))
        if kind == "Z" and s == "dt":
            out.append(e_last(("f1", 7)))
        if kind == "G" and s == "turn":
            out.append(e_last(("ab", 0)))
        if kind == "D":
            if s == "square":
                out.append(e_last(("z", j)))
            if s in ("qdec", "root") and j >= 3:
                out.append(last("B", j - 3))
            if s == "rows" and j == 0:
                out.append(last("G", 0))
            if s == "masked" and j >= 2:
                out.append(last("A", j - 2))
                if j >= 3:
                    out.append(last("B", j - 3))
        if kind == "A" and s == "turni":
            out.append(last("D", j))
        if kind == "B" and s == "v0":
            out.append(last("A", j))
        if kind == "B" and s == "high" and j == HEADS - 1:
            out.append(e_last(("swk", 0)))
        if kind == "C" and s == "rot" and j < 2:
            out += [e_last(("swq", SWQ - 1)), last("B", HEADS - 1)]
        return out

    chains = [[(k, j, None) for j in range(1, len(LT_TILES))] for k in ("split_high", "split_low")]
    chains += [[(k, h, s) for h in range(n) for s in stages] for k, n, stages in
               (("G", 1, G_STAGES), ("B", HEADS, B_STAGES), ("A", HEADS, A_STAGES), ("D", HEADS, D_STAGES))]
    chains += [[("C", t, s) for t in range(o, SWQ, 2) for s in C_STAGES] for o in range(2)]
    chains += [[("E", t, s) for t in LT_TILES for s in e_stages(t)], pieces(LT_TILES), [("Z", 0, s) for s in Z_STAGES]]
    return ordered(chains, needs, engine_of, slack1, .2)


NEXT_SLOT, NEXT_LOADS = len(LT_TILES) % RAW, len(LT_TILES) // RAW + (len(LT_TILES) % RAW > 0)
L_ORDER = layer_order()

def e2_stages(out):
    kind, i = out
    if kind == "ub":
        return (["scale", "bias"] + [f"sum{m}" for m in range(i + 1)] + ["mean", "early", "high", "low"])
    return {"ua": ["scale", "bias"], "za": ["scale", "bias", "tanh", "silu"], "zb": ["scale", "bias", "tanh", "silu"],
            "pw": ["scale", "high", "low"], "gb": ["scale", "bias", "tanh"], "ga": ["scale", "bias", "tanh"],
            "bb": ["gate"], "glu": ["tanh", "gate", "silu", "high", "low"], "ba": ["gate", "add", "high", "low"],
            "wo": ["add", "square", "sum"]}[kind]


SS_BASE = ["input", "turn", "turned", "scan", "back", "state", "output"]


def s_stages(st):
    return (SS_BASE + (["skip", "gelu"] if st % 4 == 3 else []) + (["highs", "lows"] if st == ST - 1 else []))


E2 = Count([(o, e2_stages(o)) for t in S_TILES for o in outputs_of(t)])
Z = Count([(0, Z_STAGES)])
T = Count([(st, T_STAGES) for st in range(ST)])
SS = Count([(st, s_stages(st)) for st in range(ST)])
S_OUT = [o for t in S_TILES for o in outputs_of(t)]
S_OUT_AT = {o: n for n, o in enumerate(S_OUT)}


def second_order():
    def e_first(o):
        return ("E", o, e2_stages(o)[0])

    def e_last(o):
        return ("E", o, e2_stages(o)[-1])

    def part_end(o):
        t = next(t for t in S_TILES if o in outputs_of(t))
        outs = outputs_of(t)
        return ("mm", S_AT[t], (outs.index(o) + 1) * PARTS // len(outs) - 1)

    def needs(e):
        kind, j, s = e
        out = []
        if kind == "split_high" and j >= SPLIT:
            out = [("mm", j - SPLIT, PARTS - 1)]
        if kind == "split_low":
            out = [("split_high", j, None)]
        if kind == "mm":
            t = S_TILES[j]
            outs = outputs_of(t)
            each = PARTS // len(outs)
            if s == 0 and j:
                out = [("split_low", j, None)]
            if s % each == 0:
                n = S_OUT_AT[outs[s // each]]
                if n >= 2:
                    out.append(e_first(S_OUT[n - 2]))
            if s == 0:
                out += {("pw", 0): [e_last(("ub", SG - 1))], ("bb", 0): [e_last(("pw", SG - 1))],
                        ("glu", 0): [("S", ST - 1, "lows")], ("ba", 0): [e_last(("glu", SG - 1))],
                        ("wo", 0): [e_last(("ba", KT - 1))]}.get(t, [])
        if kind == "E" and s == e2_stages(j)[0]:
            out.append(part_end(j))
        if kind == "S":
            if s == "input" and j % 4 == 0:
                out.append(e_last(("ua", j // 4)))
            if s == "turn":
                out.append(("T", j, T_STAGES[-1]))
            if s == "highs":
                out.append(e_last(("bb", KT - 1)))
        if kind == "T" and s == "coscos" and j >= 2:
            out.append(("S", j - 2, "state"))
        return out

    chains = [[(k, j, None) for j in range(1, len(S_TILES))] for k in ("split_high", "split_low")]
    chains += [[("S", st, s) for st in range(ST) for s in s_stages(st)], [("E", o, s) for o in S_OUT for s in e2_stages(o)],
              [("T", st, s) for st in range(ST) for s in T_STAGES], pieces(S_TILES)]
    return ordered(chains, needs, engine2_of, slack2, .15)


def engine2_of(e):
    kind, j, s = e
    if kind == "E" and s == "low":
        return "pool" if j[0] == "ub" else "vector"
    return engine_of(e)


def micros2(e):
    if e[0] == "mm":
        t = S_TILES[e[1]]
        return 5.12 / PARTS * len(outputs_of(t)) * S_DEPTH.get(t[0], KT) / KT
    return LENGTH["vector"] if e[0] == "E" and engine2_of(e) == "vector" else micros(e)


S_ORDER = second_order()


def build(nc, xT, pos, consts, gain0, params, w0, w1, w2, params2, smallb, smallc, outT):
    with ExitStack() as ctx:
        def sb(name, shape, dt=F32):
            return ctx.enter_context(nc.sbuf_tensor(name, shape, dt))

        def sem(name):
            return ctx.enter_context(nc.semaphore(name))

        def at(base, off, name, shape, dt=F32):
            return nc.alloc_sbuf_tensor_at(name, shape, dt, offset=base + off)

        TILE = SEQ * 4
        x = sb("x", [P, KT, SEQ])
        hH, hL = sb("hH", [P, KT, SEQ], F32R), sb("hL", [P, KT, SEQ], F32R)
        cst = sb("cst", [P, NCONST])
        par = sb("par", [P, NPARAM])
        rope_at = (nc.sbuf_base + 31) // 32 * 32
        ropeC, ropeS = sb("ropeC", [P, SEQ]), sb("ropeS", [P, SEQ])
        raw = sb("raw", [P, RAW, KT, P])
        wH, wL = sb("wH", [P, SPLIT, KT, P], F32R), sb("wL", [P, SPLIT, KT, P], F32R)
        par2 = sb("par2", [P, NPARAM2])
        spare = sb("spare", [P, 1])
        first_gain = sb("first_gain", [P, KT])
        rstd, rstdp = sb("rstd", [P, SEQ]), sb("rstdp", [P, SEQ])
        sq_at = (nc.sbuf_base + 31) // 32 * 32
        sq = sb("sq", [P, 2, SEQ])
        tmp = sb("tmp", [P, SEQ])
        small = sb("small", [P, 512])
        turn_small = sb("turn_small", [P, 2, ST, TBL])
        base_o = (nc.sbuf_base + 31) // 32 * 32
        OH, OL = sb("OH", [P, KT, SEQ], F32R), sb("OL", [P, KT, SEQ], F32R)
        base_s = (nc.sbuf_base + 31) // 32 * 32
        SH, SL = sb("SH", [P, KT, SEQ], F32R), sb("SL", [P, KT, SEQ], F32R)
        base_a = (nc.sbuf_base + 31) // 32 * 32
        acc = sb("acc", [P, KT, SEQ])
        base_r = (nc.sbuf_base + 31) // 32 * 32
        room = sb("room", [P, 11, SEQ])

        sq2 = room[:, 0, :]
        def spread(where, name):
            return [at(b, i * TILE, f"{name}{n}", [P, SEQ]) for n, (b, i) in enumerate(where)]

        qs = spread([(base_r, 0), (base_s, 8)], "qs")
        vs = spread([(base_r, 1), (base_s, 9)], "vs")
        ks = spread([(base_r, 2), (base_s, 11), (base_s, 13), (base_s, 0)], "ks")
        zs = spread([(base_s, 10), (base_s, 12), (base_s, 14), (base_s, 1)], "zs")
        kbeta = at(base_s, 15 * TILE, "kbeta", [P, SEQ])
        XT = at(base_s, 2 * TILE, "XT", [P, 3, CH, P])
        AT = at(base_s, 5 * TILE, "AT", [P, 3, CH, P])
        qd = at(base_a, 0, "qd", [P, 3, CH, P])
        kd = at(base_a, 3 * TILE, "kd", [P, 3, CH, P])
        LTm = at(base_a, 6 * TILE, "LTm", [P, 2, CH, P])
        vb = at(base_r, 3 * TILE, "vb", [P, 3, CH, P])
        Xi = at(base_r, 6 * TILE, "Xi", [P, CH, P])
        Pm = at(base_r, 7 * TILE, "Pm", [P, CH, P])
        DT = at(base_r, 8 * TILE, "DT", [P, CH, P])
        osq = at(base_r, 9 * TILE, "osq", [P, SEQ])
        S = at(base_r, 10 * TILE, "S", [P, P])
        rr = at(base_r, 10 * TILE + 512, "rr", [P, P])
        vn = at(base_r, 10 * TILE + 1024, "vn", [P, P])
        ab = at(base_r, 9 * TILE, "ab", [P, SEQ])
        rna = rstdp
        kc, kr = at(base_o, 7 * TILE, "kc", [P, SEQ])[:, :], at(base_o, 15 * TILE, "kr", [P, SEQ])[:, :]
        qraw = at(base_s, 8 * TILE, "qraw", [P, SWQ, SEQ])
        kk = at(base_r, 0, "kk", [P, 2, SEQ])
        vtok = at(base_r, 2 * TILE, "vtok", [P, CH, P])
        gate = at(base_r, 3 * TILE, "gate", [P, SEQ])
        gated = at(base_r, 4 * TILE, "gated", [P, SEQ])
        qrs = [rstdp, tmp]
        probs = [at(base_r, (5 + 2 * e) * TILE, f"prob{e}", [P, CH, 2 * P]) for e in range(2)]
        probTs = [at(sq_at, 0, "probT0", [P, 2 * CH, P]), at(base_r, 9 * TILE, "probT1", [P, 2 * CH, P])]
        def col(i, n=CH * HEADS):
            return small[:, i:i + n]
        abt, th, beta, hbeta = col(0, 64), col(64), col(96), col(128)
        alpha, mx, ea, gg, gcl = col(160), col(192), col(224, 8), col(232), col(264, 64)
        kdec, egl, eg, nbeg = col(328), col(360), col(392), col(424)
        wcol = [[col(456 + 16 * e + 4 * i, 4) for i in range(4)] for e in range(2)]
        scal = sb("scal", [P, 3, 8, CH])
        srow = sb("srow", [P, 4, CH])

        ps = ctx.enter_context(nc.psum_tensor("ps", [P, 8, 512], F32))
        psD, psB, psA = ps[:, 2:4, :], ps[:, 4:6, :], ps[:, 6:8, :]

        def k_(name):
            return cst[:, CONST[name][0]:CONST[name][1]]

        def p_(name, i=None, n=1):
            a, b = PARAM[name]
            return par[:, a:b] if i is None else par[:, a + i:a + i + n]

        def head_tile(kind, h):
            return {"q": qs[h % 2], "k": ks[h % 4], "v": vs[h % 2], "z": zs[h % 4]}[kind][:, :]

        def conv(kind, head, tap):
            return p_("conv", ("qkv".index(kind) * HEADS + head) * CONV + tap)

        def chunks(m):
            return m.rearrange("p (c n) -> p c n", c=CH)

        def by_head(m, h):
            return m.rearrange("p (c n) -> p c n", c=CH)[:, :, h]

        def second_half(m, s):
            return m.rearrange("p (b n) -> p b n", n=2 * s)[:, :, s:]

        def over_chunks(m):
            return m.unsqueeze(1).to_broadcast([P, CH, P])

        names = ("loaded0", "loaded1", "loaded2", "high_done", "low_done", "tile_done", "tile_stage",
                 "gate_stage", "gram_stage", "inverse_stage", "scan_stage", "window_even", "window_odd", "coef_stage", "x_even", "sq_done", "h_high", "h_low",
                 "ssq_done", "root_done", "rstd_ready", "params_in", "x_part", "even_part", "odd_part", "x_odd", "coef_in", "sum_done", "post_root",
                 "post_ready", "input_in", "out_done", "setup", "out_ready", "table_stage", "state_stage")
        sems = {n: sem(n) for n in names}
        nums = [s.num for s in sems.values()]
        assert nums == list(range(nums[0], nums[0] + len(nums)))
        loaded = [sems[f"loaded{i}"] for i in range(RAW)]
        loaded_x = [sem(f"loaded_x{t}") for t in range(KT)]
        (high_done, low_done, tile_done, tile_stage, gate_stage, gram_stage, inverse_stage, scan_stage, window_even, window_odd, coef_stage, x_even,
         sq_done, h_high, h_low, ssq_done, root_done, rstd_ready, params_in, x_part, even_part, odd_part, x_odd, coef_in, sum_done, post_root,
         post_ready, input_in, out_done, setup, out_ready, table_stage, state_stage) = [sems[n] for n in names[RAW:]]

        window_stage = (window_even, window_odd)

        def clear_all():
            with nc.Block() as block:
                @block.sync
                def _(sp):
                    sp.sem_clear(range(nums[0], nums[0] + len(nums)))

        def raw_tile(slot):
            return raw[:, slot, :, :].rearrange("p t n -> p (t n)")

        def load_weights(sp, weights, j):
            if j > RAW:
                sp.wait_ge(low_done, j - RAW)
            sp.dma_start(raw_tile(j % RAW), weights(j - 1)).then_inc(loaded[j % RAW], 16)

        def split_high(act, j, outputs_done):
            act.wait_ge(loaded[j % RAW], 16 * (j // RAW + (j % RAW > 0)))
            if j >= SPLIT:
                act.wait_ge(tile_done, outputs_done)
            act.activation(wH[:, j % SPLIT, :, :], raw[:, j % RAW, :, :], ACT.Copy).then_inc(high_done, 1)

        def split_low(pool, j):
            pool.wait_ge(high_done, j)
            pool.tensor_tensor(wL[:, j % SPLIT, :, :], raw[:, j % RAW, :, :], wH[:, j % SPLIT, :, :].bitcast(F32),
                               ALU.subtract).then_inc(low_done, 1)

        def next_high(act, slot):
            act.activation(wH[:, 0, :, :], raw[:, slot, :, :], ACT.Copy).then_inc(high_done, 1)

        def next_low(pool, slot, n):
            pool.wait_ge(high_done, n)
            pool.tensor_tensor(wL[:, 0, :, :], raw[:, slot, :, :], wH[:, 0, :, :].bitcast(F32), ALU.subtract)

        def products(pe, j, p, out, rH, rL, depth, col0=0, width=P, kt0=0, parts=PARTS, before=None):
            s = j % SPLIT
            t = -1
            for t in range(depth * p // parts, depth * (p + 1) // parts):
                if before is not None:
                    before(t)
                wh = wH[:, s, kt0 + t, col0:col0 + width]
                wl = wL[:, s, kt0 + t, col0:col0 + width]
                pe.matmul(out, wh, rH[:, t, :], start=(t == 0), stop=False)
                pe.matmul(out, wh, rL[:, t, :], start=False, stop=False)
                mm = pe.matmul(out, wl, rH[:, t, :], start=False, stop=(t == depth - 1))
            if (t + 1) == depth:
                mm.then_inc(tile_done, 1)

        def x_add(eng, t, n):
            part, ready = ((even_part, x_even), (odd_part, x_odd))[t % 2]
            eng.tensor_tensor(acc[:, t, :], acc[:, t, :], rstdp[:, :], ALU.mult).then_inc(part, 1)
            eng.wait_ge(part, n * KT // 2 + t // 2 + 1)
            eng.tensor_tensor(x[:, t, :], x[:, t, :], acc[:, t, :], ALU.add).then_inc(ready, 1)

        def x_added(eng, t, n):
            eng.wait_ge((x_even, x_odd)[t % 2], n * KT // 2 + t // 2 + 1)

        def odd_adds(pool, n):
            pool.wait_ge(post_ready, n + 1)
            for t in range(1, KT, 2):
                x_add(pool, t, n)

        def x_low(v, t, gain, n):
            v.wait_ge(h_high, n + t + 1)
            v.scalar_tensor_tensor(out=hL[:, t, :], in0=x[:, t, :], scalar=gain(t), in1=hH[:, t, :].bitcast(F32),
                                   op0=ALU.mult, op1=ALU.subtract).then_inc(h_low, 1)

        def x_high(act, gain, n, added):
            for t in range(KT):
                if added is None:
                    act.wait_ge(loaded_x[t], 16)
                else:
                    x_added(act, t, added)
                act.activation(hH[:, t, :], x[:, t, :], ACT.Copy, scale=gain(t)).then_inc(h_high, 1)
                if t >= 2:
                    act.wait_ge(ssq_done, n + t - 1)
                act.activation(sq[:, t % 2, :], x[:, t, :], ACT.Square).then_inc(sq_done, 1)

        def adds_and_lows(v, gain, n, lows):
            v.wait_ge(post_ready, n + 1)
            low = 0
            for t in range(0, KT, 2):
                x_add(v, t, n)
                while low < t - 1:
                    x_low(v, low, gain, lows)
                    low += 1
            for low in range(low, KT):
                x_low(v, low, gain, lows)

        def x_sum(pe, base, t):
            pe.wait_ge(sq_done, base + t + 1)
            pe.matmul(ps[:, 7, :], k_("ones"), sq[:, t % 2, :], start=(t == 0), stop=(t == KT - 1)).then_inc(ssq_done, 1)

        def root_scalar(act, done, n, out, src, scale, eps, ready):
            act.activation(spare[:, 0:1], k_("eps"), ACT.Sqrt)
            act.wait_ge(done, n)
            act.activation(out, src, ACT.Sqrt, bias=k_(eps), scale=scale).then_inc(ready, 1)

        bmat = at(rope_at, 0, "bmat", [P, 2, SG, P])
        u = at(base_o, 0, "u", [P, SG, SEQ])
        za = at(base_o, 4 * TILE, "za", [P, SG, SEQ])
        turn_c = at(base_o, 8 * TILE, "turn_c", [P, 2, SEQ])
        turn_s = at(base_o, 10 * TILE, "turn_s", [P, 2, SEQ])
        turn_t = at(base_o, 12 * TILE, "turn_t", [P, SEQ])
        cmat = at(base_r, 0, "cmat", [P, 2, ST, 32])
        big = at(base_r, 2 * TILE, "big", [P, 2, ST, TBH])
        craw = at(base_r, 3 * TILE, "craw", [P, 2, ST, 32])
        ctmp = at(base_r, 5 * TILE, "ctmp", [P, 4, ST, 32])
        cols = small[:, 64:64 + 17 * ST].rearrange("p (i n) -> p i n", n=ST)
        zb = spread([(base_o, 13), (base_o, 14), (base_o, 15), (base_r, 3)], "zb")
        t1, t2, zr, zi, sr, si = (at(base_r, (4 + i) * TILE, n, [P, SEQ]) for i, n in
                                  enumerate(("t1", "t2", "zr", "zi", "sr", "si")))
        mixed = at(base_r, 10 * TILE, "mixed", [P, SEQ])
        yaH, yaL = at(base_r, 0, "yaH", [P, SG, SEQ], F32R), at(base_r, 4 * TILE, "yaL", [P, SG, SEQ], F32R)
        sga_a, sga_b = at(base_s, 4 * TILE, "sga_a", [P, SG, SEQ]), at(base_s, 12 * TILE, "sga_b", [P, SG, SEQ])

        def sga(f):
            return (sga_a if f < SG else sga_b)[:, f % SG, :]

        def p2(name, i=None, n=1):
            a, b = PARAM2[name]
            return par2[:, a:b] if i is None else par2[:, a + i:a + i + n]

        mag = small[:, 0:ST]
        half_glu = small[:, ST:ST + SG]

        dt, ang, lr, ws, wc, k0, cr, ci, nr, ni, den2, q1, q2, q3, q4, cfr, cfi = (cols[:, i, :] for i in range(17))

        steps = [0]

        def coefficients(v, s):
            def link(ins):
                steps[0] += 1
                ins.then_inc(setup, 1)
                v.wait_ge(setup, steps[0])

            def mul(o, a, b):
                return v.tensor_tensor(o, a, b, ALU.mult)

            if s == "angles":
                v.tensor_scalar(half_glu, p2("b_glu"), 0.5, None, ALU.mult)
                mul(ang, p2("lam_im"), dt)
                ins = mul(lr, p2("lam_re"), dt)
            elif s == "reduce":
                range_reduce(v, link, ws, ang, k0, 0.0)
                range_reduce(v, link, wc, ang, k0, 0.25)
                ins = mul(q1, p2("lam_re"), p2("lam_re"))
            elif s == "input":
                mul(q2, p2("lam_im"), p2("lam_im"))
                mul(nr, mag, cr)
                link(mul(ni, mag, ci))
                v.tensor_scalar(nr, nr, 1.0, None, ALU.subtract)
                link(v.tensor_tensor(den2, q1, q2, ALU.add))
                v.reciprocal(den2, den2)
                mul(q1, nr, p2("lam_re"))
                mul(q2, ni, p2("lam_im"))
                mul(q3, ni, p2("lam_re"))
                link(mul(q4, nr, p2("lam_im")))
                v.tensor_tensor(cfr, q1, q2, ALU.add)
                link(v.tensor_tensor(cfi, q3, q4, ALU.subtract))
                mul(cfr, cfr, den2)
                ins = mul(cfi, cfi, den2)
            elif s in ("maps0", "maps1"):
                wide = lambda a: a.unsqueeze(2).to_broadcast([P, ST, 32])
                v.wait_ge(coef_in, 16)
                if s == "maps0":
                    mul(ctmp[:, 0], craw[:, 0], wide(cfr))
                    link(mul(ctmp[:, 1], craw[:, 1], wide(cfi)))
                    ins = v.tensor_tensor(cmat[:, 0], ctmp[:, 0], ctmp[:, 1], ALU.subtract)
                else:
                    mul(ctmp[:, 2], craw[:, 1], wide(cfr))
                    link(mul(ctmp[:, 3], craw[:, 0], wide(cfi)))
                    ins = v.scalar_tensor_tensor(out=cmat[:, 1], in0=ctmp[:, 2], scalar=-1.0, in1=ctmp[:, 3],
                                                 op0=ALU.mult, op1=ALU.subtract)
            else:
                m = int(s[6:])
                small_steps = m < TBL_STEPS
                table, k = (turn_small, 2 ** m) if small_steps else (big, 2 ** (m - TBL_STEPS))
                if k == 1:
                    v.memset(table[:, 0, :, 0:1], 1.0)
                    link(v.memset(table[:, 1, :, 0:1], 0.0))
                a, b = table[:, 0, :, 0:k], table[:, 1, :, 0:k]
                c = cr.unsqueeze(2).to_broadcast([P, ST, k])
                d = ci.unsqueeze(2).to_broadcast([P, ST, k])
                w = [ctmp[:, i, :, 0:k] for i in range(4)]
                mul(w[0], a, c)
                mul(w[1], b, d)
                mul(w[2], a, d)
                mul(w[3], b, c)
                mul(q1, cr, cr)
                mul(q2, ci, ci)
                link(mul(q3, cr, ci))
                v.tensor_tensor(table[:, 0, :, k:2 * k], w[0], w[1], ALU.subtract)
                v.tensor_tensor(table[:, 1, :, k:2 * k], w[2], w[3], ALU.add)
                v.tensor_tensor(cr, q1, q2, ALU.subtract)
                ins = v.tensor_scalar(ci, q3, 2.0, None, ALU.mult)
            ins.then_inc(coef_stage, 1)

        with nc.Block() as block:
            @block.sync
            def _(sp):
                sp.dma_start(sq2[:, :].bitcast(I32), pos.to_broadcast([P, SEQ])).then_inc(input_in, 16)
                sp.dma_start(cst[:, :], consts).then_inc(input_in, 16)
                sp.dma_start(first_gain[:, :], gain0).then_inc(params_in, 16)
                for t in range(KT):
                    sp.dma_start(x[:, t, :], xT[:, t, :]).then_inc(loaded_x[t], 16)
                    if t == 2:
                        sp.dma_start(raw_tile(0), w0).then_inc(loaded[0], 16)
                sp.dma_start(par2[:, :], params2).then_inc(coef_in, 16)
                sp.wait_ge(coef_in, 16)

            @block.vector
            def _(v):
                step = [0]

                def link(ins):
                    step[0] += 1
                    ins.then_inc(setup, 1)
                    v.wait_ge(setup, step[0])

                v.wait_ge(input_in, 32)
                v.wait_ge(params_in, 16)
                link(v.tensor_copy(tmp[:, :], sq2[:, :].bitcast(I32)))
                link(v.tensor_scalar(tmp[:, :], tmp[:, :], k_("invfreq"), None, ALU.mult))
                range_reduce(v, link, rstd[:, :], tmp[:, :], sq2[:, :], 0.0)
                range_reduce(v, link, rstdp[:, :], tmp[:, :], sq2[:, :], 0.25)
                for t in range(KT):
                    x_low(v, t, lambda t: first_gain[:, t:t + 1], 0)
                v.wait_ge(x_part, 2)
                v.tensor_scalar(ropeS[:, :], ropeS[:, :], k_("isrot"), None, ALU.mult)
                v.tensor_scalar(ropeC[:, :], ropeC[:, :], k_("isrot"), k_("notrot"), ALU.mult, ALU.add)

            @block.scalar
            def _(act):
                act.wait_ge(params_in, 16)
                x_high(act, lambda t: first_gain[:, t:t + 1], 0, None)
                act.wait_ge(loaded[0], 16)
                next_high(act, 0)
                act.wait_ge(setup, 2 + 2 * RANGE_STEPS)
                act.activation(ropeS[:, :], rstd[:, :], ACT.Sin).then_inc(x_part, 1)
                act.activation(ropeC[:, :], rstdp[:, :], ACT.Sin, bias=k_("halfpi")).then_inc(x_part, 1)

            @block.gpsimd
            def _(pool):
                next_low(pool, 0, 1)

            @block.tensor
            def _(pe):
                pe.wait_ge(input_in, 32)
                for t in range(KT):
                    x_sum(pe, 0, t)
        clear_all()

        with nc.Fori(0, DEPTH) as layer:
            with nc.Block() as block:
                @block.sync
                def _(sp):
                    sp.dma_start(par[:, :], params[layer]).then_inc(params_in, 16)
                    for j in range(1, len(LT_TILES) + 1):
                        load_weights(sp, lambda i: w1[layer, i], j)
                        if j == L_AT["f1", 4]:
                            sp.wait_ge(tile_stage, E.end(("wo", 0)))
                            sp.dma_start(craw[:, :, :, :].rearrange("p a b c -> p (a b c)"), smallc).then_inc(coef_in, 16)

                @block.gpsimd
                def _(pool):
                    for kind, j, s in L_ORDER:
                        if kind == "split_low":
                            split_low(pool, j)
                            if j == L_AT["f1", 0]:
                                odd_adds(pool, 0)
                        elif kind == "D" and s in ("qdec", "mask"):
                            pool.wait_ge(gram_stage, D.before(j, s))
                            if s == "qdec":
                                if j >= 3:
                                    pool.wait_ge(scan_stage, B.end(j - 3))
                                pool.tensor_tensor(qd[:, j % 3, :, :], chunks(qs[j % 2][:, :]), chunks(rna[:, :]),
                                                   ALU.mult).then_inc(gram_stage, 1)
                            else:
                                pool.tensor_tensor(DT[:, :, :], DT[:, :, :], over_chunks(k_("upper")),
                                                   ALU.mult).then_inc(gram_stage, 1)
                        elif kind == "B" and s == "low":
                            pool.wait_ge(scan_stage, B.before(j, s))
                            pool.tensor_tensor(OL[:, j, :], osq[:, :], OH[:, j, :].bitcast(F32),
                                               ALU.subtract).then_inc(scan_stage, 1)
                        elif kind == "E" and s == "low":
                            pool.wait_ge(tile_stage, E.before(j, s))
                            if j[0] == "f1":
                                c, t = j[1] // 8, j[1] % 8
                                pool.tensor_tensor((OL, SL)[c % 2][:, t, :], tmp[:, :],
                                                   (OH, SH)[c % 2][:, t, :].bitcast(F32),
                                                   ALU.subtract).then_inc(tile_stage, 1)
                            else:
                                pool.tensor_tensor(OL[:, j[1], :], gated[:, :], OH[:, j[1], :].bitcast(F32),
                                                   ALU.subtract).then_inc(tile_stage, 1)
                    next_low(pool, NEXT_SLOT, len(LT_TILES))
                    odd_adds(pool, 1)

                @block.scalar
                def _(act):
                    act.wait_ge(params_in, 16)
                    act.activation(rstd[:, :], ps[:, 7, :], ACT.Sqrt, bias=k_("eps"), scale=1.0 / D_MODEL).then_inc(root_done, 1)
                    for kind, j, s in L_ORDER:
                        if kind == "split_high":
                            split_high(act, j, j - SPLIT + 1)
                        elif kind == "Z" and s in ("dt", "mag", "sines"):
                            act.wait_ge(coef_stage, Z.before(0, s))
                            if s == "dt":
                                act.activation(dt, p2("log_dt"), ACT.Exp).then_inc(coef_stage, 1)
                            elif s == "mag":
                                act.activation(mag, lr, ACT.Exp).then_inc(coef_stage, 1)
                            else:
                                act.activation(ci, ws, ACT.Sin)
                                act.activation(cr, wc, ACT.Sin, bias=k_("halfpi")).then_inc(coef_stage, 1)
                        elif kind == "G" and s in ("tanh", "abs", "expn", "ln", "expa", "exps"):
                            act.wait_ge(gate_stage, G.before(0, s))
                            a3 = abt.rearrange("p (c n) -> p c n", c=CH)
                            if s == "tanh":
                                act.activation(th.rearrange("p (c n) -> p c n", c=CH), a3[:, :, 0:HEADS], ACT.Tanh, scale=0.5).then_inc(gate_stage, 1)
                            if s == "abs":
                                act.activation(alpha, alpha, ACT.Abs).then_inc(gate_stage, 1)
                            if s == "expn":
                                act.activation(alpha, alpha, ACT.Exp, scale=-1.0).then_inc(gate_stage, 1)
                            if s == "ln":
                                act.activation(alpha, alpha, ACT.Ln).then_inc(gate_stage, 1)
                            if s == "expa":
                                act.activation(ea, p_("a_log"), ACT.Exp).then_inc(gate_stage, 1)
                            if s == "exps":
                                act.activation(kdec, kdec, ACT.Exp)
                                act.activation(egl, gcl[:, 32:64], ACT.Exp)
                                act.activation(eg, gcl[:, 0:32], ACT.Exp).then_inc(gate_stage, 1)
                        elif kind == "D" and s in ("square", "root", "exps", "copykv"):
                            act.wait_ge(gram_stage, D.before(j, s))
                            w = scal[:, j % 3]
                            if s == "square":
                                act.wait_ge(tile_stage, E.end(("z", j)))
                                act.activation(sq[:, 0, :], ks[j % 4][:, :], ACT.Square)
                                ins = act.activation(sq[:, 1, :], qs[j % 2][:, :], ACT.Square)
                            elif s == "root":
                                if j >= 3:
                                    act.wait_ge(scan_stage, B.end(j - 3))
                                ins = act.activation(w[:, 0:2, :], psD[:, 0, 0:2 * CH].rearrange("p (a c) -> p a c", a=2),
                                                     ACT.Sqrt, bias=k_("eps4"))
                            elif s == "exps":
                                act.activation(rna[:, :], psD[:, 0, :], ACT.Exp)
                                ins = act.activation(DT[:, :, :], DT[:, :, :], ACT.Exp)
                            else:
                                for c in range(CH):
                                    i = c * HEADS + j
                                    act.activation(kd[:, j % 3, c, :], psD[:, 0, c * P:(c + 1) * P], ACT.Copy, scale=w[:, 4, c:c + 1])
                                    ins = act.activation(vb[:, j % 3, c, :], psD[:, 1, c * P:(c + 1) * P], ACT.Copy, scale=hbeta[:, i:i + 1])
                            ins.then_inc(gram_stage, 1)
                        elif kind == "A" and s.startswith("copy"):
                            act.wait_ge(inverse_stage, A.before(j, s))
                            act.activation(Xi[:, :, :], chunks(psA[:, 0, :]), ACT.Copy).then_inc(inverse_stage, 1)
                        elif kind == "B" and (s.startswith("copyv") or s in ("square", "root", "high")):
                            act.wait_ge(scan_stage, B.before(j, s))
                            if s == "square":
                                act.activation(osq[:, :], psB[:, 1, :], ACT.Square).then_inc(scan_stage, 1)
                            elif s == "root":
                                act.activation(srow[:, 1], srow[:, 0], ACT.Sqrt, bias=k_("eps4")).then_inc(scan_stage, 1)
                            elif s == "high":
                                if j == HEADS - 1:
                                    act.wait_ge(tile_stage, E.end(("swk", 0)))
                                act.activation(OH[:, j, :], osq[:, :], ACT.Copy).then_inc(scan_stage, 1)
                            else:
                                act.activation(vn[:, :], psB[:, 0, 0:P], ACT.Copy).then_inc(scan_stage, 1)
                        elif kind == "C" and (s[:-1] in ("exp", "copy") or s == "high"):
                            o = j % 2
                            act.wait_ge(window_stage[o], C[o].before(j, s))
                            prob, (m4, nm4, den, es) = probs[o], wcol[o]
                            if s[:-1] == "exp":
                                e = int(s[-1])
                                for n in range(CH):
                                    a = P if n == 0 else 0
                                    act.activation(prob[:, n, a:], prob[:, n, a:], ACT.Exp, bias=nm4[:, n:n + 1],
                                                   accum_out=den[:, n:n + 1])
                                ins = act.activation(es, nm4, ACT.Exp, bias=p_("sinks", 2 * j + e))
                            elif s[:-1] == "copy":
                                pT = ps[:, 2 + 2 * o:4 + 2 * o, :].rearrange("p b (c n) -> p (b c) n", n=P)
                                ins = act.activation(probTs[o][:, 0:2 * CH - 1, :], pT[:, 0:2 * CH - 1, :], ACT.Copy)
                            else:
                                ins = act.activation(SH[:, j, :], ps[:, 6 + o, :], ACT.Copy)
                            ins.then_inc(window_stage[o], 1)
                        elif kind == "E" and s in ("tap3", "tanh", "copyk", "copyv", "high", "square", "gain"):
                            act.wait_ge(tile_stage, E.before(j, s))
                            kd_, i = j
                            dst = head_tile(kd_, i) if kd_ in "qkvz" else None
                            if s == "tap3":
                                if kd_ == "q" and i >= 2:
                                    act.wait_ge(gram_stage, D.end(i - 2))
                                if kd_ == "q" and i >= 4:
                                    act.wait_ge(scan_stage, B.end(i - 4))
                                act.activation(dst, tmp[:, :], ACT.Copy, scale=conv(kd_, i, 3)).then_inc(tile_stage, 1)
                            elif s == "tanh" and kd_ in "qkv":
                                act.activation(tmp[:, :], dst, ACT.Tanh, scale=0.5).then_inc(tile_stage, 1)
                            elif s == "tanh" and kd_ == "z":
                                act.activation(dst, tmp[:, :], ACT.Tanh, scale=0.5).then_inc(tile_stage, 1)
                            elif s == "tanh":
                                act.activation(gate[:, :], gate[:, :], ACT.Tanh, scale=0.5).then_inc(tile_stage, 1)
                            elif s == "copyk":
                                act.activation(kk[:, 0, :], psD[:, 0, :], ACT.Copy)
                                act.activation(kk[:, 1, :], psD[:, 1, :], ACT.Copy).then_inc(tile_stage, 1)
                            elif s == "copyv":
                                act.activation(vtok[:, :, :], chunks(psD[:, 0, :]), ACT.Copy).then_inc(tile_stage, 1)
                            elif s == "high" and kd_ == "f1":
                                act.activation((OH, SH)[i // 8 % 2][:, i % 8, :], tmp[:, :], ACT.Copy).then_inc(tile_stage, 1)
                            elif s == "high":
                                act.activation(OH[:, i, :], gated[:, :], ACT.Copy).then_inc(tile_stage, 1)
                            elif s == "square":
                                act.activation(sq[:, 0, :], acc[:, i % 8, :], ACT.Square).then_inc(tile_stage, 1)
                            else:
                                g = p_("post_mix" if kd_ == "wo" else "post_mlp", i % 8)
                                act.activation(acc[:, i % 8, :], acc[:, i % 8, :], ACT.Copy, scale=g).then_inc(tile_stage, 1)
                            if j == ("wo", KT - 1) and s == "gain":
                                root_scalar(act, sum_done, 1, rstdp[:, :], ps[:, 7, :], 1.0 / D_MODEL, "eps", post_root)
                                x_high(act, lambda t: p_("pre_mlp", t), 0, 0)
                                root_scalar(act, ssq_done, KT, rstd[:, :], ps[:, 7, :], 1.0 / D_MODEL, "eps", root_done)
                    act.wait_ge(loaded[NEXT_SLOT], 16 * NEXT_LOADS)
                    act.wait_ge(tile_done, len(LT_TILES))
                    next_high(act, NEXT_SLOT)
                    root_scalar(act, sum_done, 2, rstdp[:, :], ps[:, 7, :], 1.0 / D_MODEL, "eps", post_root)
                    x_high(act, lambda t: p_("next", t), KT, 1)

                @block.vector
                def _(v):
                    def rstd_vector(n):
                        v.wait_ge(root_done, n)
                        v.reciprocal(rstd[:, :], rstd[:, :]).then_inc(rstd_ready, 1)
                        v.wait_ge(rstd_ready, n)

                    def post_vector(n):
                        v.wait_ge(post_root, n)
                        v.reciprocal(rstdp[:, :], rstdp[:, :]).then_inc(post_ready, 1)

                    v.wait_ge(params_in, 16)
                    rstd_vector(1)
                    for kind, j, s in L_ORDER:
                        if kind == "Z" and s not in ("dt", "mag", "sines"):
                            v.wait_ge(coef_stage, Z.before(0, s))
                            coefficients(v, s)
                        elif kind == "G":
                            if s not in ("copy", "beta", "hbeta", "addb", "max", "plus1", "sp", "g", "copyc", "diff", "nbeg"):
                                continue
                            v.wait_ge(gate_stage, G.before(0, s))
                            c8 = lambda ap: ap.rearrange("p (c n) -> p c n", c=CH)
                            if s == "copy":
                                ins = v.tensor_copy(abt, psD[:, 0, 0:64])
                            elif s == "beta":
                                ins = v.tensor_scalar(beta, th, 0.5, 0.5, ALU.mult, ALU.add)
                            elif s == "hbeta":
                                ins = v.tensor_scalar(hbeta, beta, 0.5, None, ALU.mult)
                            elif s == "addb":
                                ins = v.tensor_tensor(c8(alpha), c8(abt)[:, :, HEADS:2 * HEADS],
                                                      p_("dt_bias").unsqueeze(1).to_broadcast([P, CH, HEADS]), ALU.add)
                            elif s == "max":
                                ins = v.tensor_scalar(mx, alpha, 0.0, None, ALU.max)
                            elif s == "plus1":
                                ins = v.tensor_scalar(alpha, alpha, 1.0, None, ALU.add)
                            elif s == "sp":
                                ins = v.tensor_tensor(alpha, alpha, mx, ALU.add)
                            elif s == "g":
                                ins = v.scalar_tensor_tensor(out=c8(gg), in0=c8(alpha), scalar=-1.0,
                                                             in1=ea.unsqueeze(1).to_broadcast([P, CH, HEADS]),
                                                             op0=ALU.mult, op1=ALU.mult)
                            elif s == "copyc":
                                ins = v.tensor_copy(gcl, psD[:, 0, 0:64])
                            elif s == "diff":
                                ins = v.tensor_tensor(kdec, gcl[:, 32:64], gcl[:, 0:32], ALU.subtract)
                            else:
                                ins = v.scalar_tensor_tensor(out=nbeg, in0=beta, scalar=-1.0, in1=eg,
                                                             op0=ALU.mult, op1=ALU.mult)
                            ins.then_inc(gate_stage, 1)
                        elif kind == "D" and s in ("recip", "scales", "kbeta", "diff", "masked", "first", "minus"):
                            h = j
                            w = scal[:, h % 3]
                            v.wait_ge(gram_stage, D.before(h, s))
                            a0, a1 = (chunks(psD[:, i, :]) for i in range(2))
                            xt, lt = XT[:, h % 3, :, :], LTm[:, h % 2, :, :]
                            if s == "recip":
                                ins = v.reciprocal(w[:, 0:2, :], w[:, 0:2, :])
                            elif s == "scales":
                                v.tensor_tensor(w[:, 2, :], w[:, 0, :], by_head(beta, h), ALU.mult)
                                v.tensor_tensor(w[:, 3, :], w[:, 0, :], by_head(nbeg, h), ALU.mult)
                                v.tensor_tensor(w[:, 4, :], w[:, 0, :], by_head(kdec, h), ALU.mult)
                                v.tensor_scalar(w[:, 5, :], w[:, 1, :], float(P) ** -0.5, None, ALU.mult)
                                ins = v.scalar_tensor_tensor(out=w[:, 6, :], in0=w[:, 1, :], scalar=4.0 / P ** 2,
                                                             in1=w[:, 1, :], op0=ALU.mult, op1=ALU.mult)
                            elif s == "kbeta":
                                ins = v.tensor_tensor(kbeta[:, :], ks[h % 4][:, :], psD[:, 1, :], ALU.mult)
                            elif s == "diff":
                                for c in range(CH):
                                    i = c * HEADS + h
                                    ins = v.tensor_scalar(DT[:, c, :], a0[:, c, :], gcl[:, i:i + 1], 0.0,
                                                          ALU.subtract, ALU.min)
                            elif s == "masked":
                                if h >= 3:
                                    v.wait_ge(scan_stage, B.end(h - 3))
                                if h >= 2:
                                    v.wait_ge(inverse_stage, A.end(h - 2))
                                for c in range(CH):
                                    r = w[:, 0, c:c + 1]
                                    v.scalar_tensor_tensor(out=AT[:, h % 3, c, :], in0=a1[:, c, :], scalar=r, in1=DT[:, c, :],
                                                           op0=ALU.mult, op1=ALU.mult)
                                    ins = v.scalar_tensor_tensor(out=lt[:, c, :], in0=a0[:, c, :], scalar=r, in1=DT[:, c, :],
                                                                 op0=ALU.mult, op1=ALU.mult)
                            elif s == "first":
                                ins = v.tensor_tensor(xt, lt, over_chunks(k_("first")), ALU.mult)
                            else:
                                ins = v.tensor_tensor(xt, over_chunks(k_("ident")), xt, ALU.subtract)
                            ins.then_inc(gram_stage, 1)
                        elif kind == "A" and (s.startswith("pmask") or s.startswith("update")):
                            v.wait_ge(inverse_stage, A.before(j, s))
                            lev = int(s[-1])
                            if s.startswith("pmask"):
                                m = k_("levels")[:, lev * P:(lev + 1) * P]
                                ins = v.tensor_tensor(Pm[:, :, :], chunks(psA[:, 0, :]), over_chunks(m), ALU.mult)
                            else:
                                xt = second_half(XT[:, j % 3, :, :].rearrange("p c n -> p (c n)"), LEVELS[lev])
                                ins = v.tensor_tensor(xt, xt, second_half(psA[:, 1, :], LEVELS[lev]), ALU.subtract)
                            ins.then_inc(inverse_stage, 1)
                        elif kind == "B":
                            h = j
                            if not (s[:-1] in ("rr", "state") or s in ("mean", "recip", "factor", "norm")):
                                continue
                            w = scal[:, h % 3]
                            v.wait_ge(scan_stage, B.before(h, s))
                            if s == "state0":
                                ins = v.tensor_copy(S[:, :], psB[:, 0, P:2 * P])
                            elif s.startswith("state"):
                                i = int(s[-1]) * HEADS + h
                                ins = v.scalar_tensor_tensor(out=S[:, :], in0=S[:, :], scalar=egl[:, i:i + 1],
                                                             in1=psB[:, 0, P:2 * P], op0=ALU.mult, op1=ALU.add)
                            elif s.startswith("rr"):
                                c = int(s[-1])
                                ins = v.scalar_tensor_tensor(out=rr[:, :], in0=psB[:, 0, 2 * P:3 * P],
                                                             scalar=w[:, 3, c:c + 1], in1=vb[:, h % 3, c, :],
                                                             op0=ALU.mult, op1=ALU.add)
                            elif s == "mean":
                                v.tensor_tensor(srow[:, 0], psB[:, 0, 0:CH], w[:, 6, :], ALU.mult)
                                ins = v.scalar_tensor_tensor(out=osq[:, :], in0=psB[:, 1, :], scalar=p_("norm"),
                                                             in1=zs[h % 4][:, :], op0=ALU.mult, op1=ALU.mult)
                            elif s == "recip":
                                ins = v.reciprocal(srow[:, 2], srow[:, 1])
                            elif s == "factor":
                                ins = v.tensor_tensor(srow[:, 3], srow[:, 2], w[:, 5, :], ALU.mult)
                            else:
                                ins = v.tensor_tensor(osq[:, :], osq[:, :], psB[:, 0, :], ALU.mult)
                            ins.then_inc(scan_stage, 1)
                        elif kind == "C":
                            t, o = j, j % 2
                            e = int(s[-1]) if s[-1].isdigit() else 0
                            w = s.rstrip("01")
                            if w not in ("cos", "sin", "addq", "mask", "max", "maxs", "neg", "den", "recip", "prob", "low"):
                                continue
                            v.wait_ge(window_stage[o], C[o].before(t, s))
                            prob, qr, (m4, nm4, den, es) = probs[o], qrs[o], wcol[o]
                            qc = probTs[o][:, 0:CH, :].rearrange("p c n -> p (c n)")
                            if w == "cos":
                                ins = v.tensor_tensor(qc, qraw[:, t, :], ropeC[:, :], ALU.mult)
                            elif w == "sin":
                                if t < 2:
                                    v.memset(prob[:, 0, 0:P], NEG)
                                ins = v.tensor_tensor(qr[:, :], ps[:, 6 + o, :], ropeS[:, :], ALU.mult)
                            elif w == "addq":
                                ins = v.tensor_tensor(qr[:, :], qr[:, :], qc, ALU.add)
                            elif w == "mask":
                                sc = ps[:, 2 + 2 * o:4 + 2 * o, :].rearrange("p b (n k) -> p (b n) k", k=2 * P)
                                v.scalar_tensor_tensor(out=prob[:, 0, P:], in0=sc[:, 0, P:], scalar=float(HD) ** -0.5,
                                                       in1=k_("window")[:, P:], op0=ALU.mult, op1=ALU.add)
                                ins = v.scalar_tensor_tensor(out=prob[:, 1:, :], in0=sc[:, 1:, :], scalar=float(HD) ** -0.5,
                                                             in1=k_("window").unsqueeze(1).to_broadcast([P, CH - 1, 2 * P]),
                                                             op0=ALU.mult, op1=ALU.add)
                            elif w == "max":
                                ins = v.tensor_reduce(m4, prob[:, :, :], AX.X, ALU.max)
                            elif w == "maxs":
                                ins = v.tensor_scalar(m4, m4, p_("sinks", 2 * t + e), None, ALU.max)
                            elif w == "neg":
                                ins = v.tensor_scalar(nm4, m4, -1.0, None, ALU.mult)
                            elif w == "den":
                                ins = v.tensor_tensor(den, den, es, ALU.add)
                            elif w == "recip":
                                ins = v.reciprocal(den, den)
                            elif w == "prob":
                                v.tensor_scalar(prob[:, 0, P:], prob[:, 0, P:], den[:, 0:1], None, ALU.mult)
                                ins = v.tensor_tensor(prob[:, 1:, :], prob[:, 1:, :],
                                                      den[:, 1:].unsqueeze(2).to_broadcast([P, CH - 1, 2 * P]), ALU.mult)
                            else:
                                ins = v.tensor_tensor(SL[:, t, :], ps[:, 6 + o, :], SH[:, t, :].bitcast(F32), ALU.subtract)
                            ins.then_inc(window_stage[o], 1)
                        elif kind == "E":
                            kd_, i = j
                            n = L_AT[j]
                            b = ps[:, n % 2, :]
                            if s in ("tanh", "tap3", "rotk", "dupk", "copyk", "turnv", "copyv", "high", "low", "square", "gain"):
                                continue
                            v.wait_ge(tile_stage, E.before(j, s))
                            if s == e_stages(j)[0]:
                                v.wait_ge(tile_done, n + 1)
                                if j == ("f1", 0):
                                    rstd_vector(2)
                            dst = head_tile(kd_, i) if kd_ in "qkvz" else None
                            if s == "scale":
                                out = {"ab": ab[0:16, :], "ga": gate[:, :], "gb": gate[:, :], "swq": None}.get(kd_, tmp[:, :])
                                if kd_ == "swq":
                                    out = qraw[:, i, :]
                                m = 16 if kd_ == "ab" else P
                                if j == ("swq", 0):
                                    v.wait_ge(scan_stage, B.end(HEADS - 3))
                                    v.wait_ge(gram_stage, D.end(HEADS - 1))
                                if j == ("swq", SWQ // 2):
                                    v.wait_ge(scan_stage, B.end(HEADS - 2))
                                if j == ("ga", 0):
                                    v.wait_ge(scan_stage, B.end(HEADS - 1))
                                ins = v.tensor_tensor(out, b[0:m, :], rstd[0:m, :], ALU.mult)
                            elif s in ("tap2", "tap1", "tap0"):
                                d = 3 - int(s[-1])
                                ins = v.scalar_tensor_tensor(out=dst[:, d:], in0=tmp[:, 0:SEQ - d], scalar=conv(kd_, i, 3 - d),
                                                             in1=dst[:, d:], op0=ALU.mult, op1=ALU.add)
                            elif s == "silu" and kd_ != "z":
                                ins = v.scalar_tensor_tensor(out=dst, in0=tmp[:, :], scalar=1.0, in1=dst, op0=ALU.add, op1=ALU.mult)
                            elif s == "silu":
                                ins = v.scalar_tensor_tensor(out=dst, in0=dst, scalar=1.0, in1=tmp[:, :], op0=ALU.add, op1=ALU.mult)
                            elif s == "cosk":
                                ins = v.tensor_tensor(kc, tmp[:, :], ropeC[:, :], ALU.mult)
                            elif s == "sink":
                                ins = v.tensor_tensor(kr, psD[:, 0, :], ropeS[:, :], ALU.mult)
                            elif s == "addk":
                                ins = v.tensor_tensor(kr, kr, kc, ALU.add)
                            elif s == "gate" and kd_ == "ya":
                                ins = v.scalar_tensor_tensor(out=acc[:, i, :], in0=gate[:, :], scalar=1.0, in1=b, op0=ALU.add, op1=ALU.mult)
                            elif s == "gate":
                                ins = v.scalar_tensor_tensor(out=gated[:, :], in0=gate[:, :], scalar=1.0, in1=b, op0=ALU.add, op1=ALU.mult)
                            elif s == "add" and kd_ == "yb":
                                ins = v.tensor_tensor(gated[:, :], gated[:, :], acc[:, i, :], ALU.add)
                            elif s == "relu2":
                                ins = v.scalar_tensor_tensor(out=tmp[:, :], in0=tmp[:, :], scalar=0.0, in1=tmp[:, :], op0=ALU.max, op1=ALU.mult)
                            elif s == "copy" and kd_ == "wo":
                                ins = v.tensor_scalar(acc[:, i, :], b, 0.5, None, ALU.mult)
                            elif s == "copy":
                                ins = v.tensor_copy(acc[:, i % 8, :], b)
                            elif s == "add":
                                ins = v.tensor_tensor(acc[:, i % 8, :], acc[:, i % 8, :], b, ALU.add)
                            elif s == "sum":
                                if i % 8 == 0:
                                    ins = v.tensor_copy(sq[:, 1, :], sq[:, 0, :])
                                else:
                                    ins = v.tensor_tensor(sq[:, 1, :], sq[:, 1, :], sq[:, 0, :], ALU.add)
                            ins.then_inc(tile_stage, 1)
                            if j == ("wo", KT - 1) and s == "sum":
                                post_vector(1)
                                adds_and_lows(v, lambda t: p_("pre_mlp", t), 0, 0)
                    post_vector(2)
                    adds_and_lows(v, lambda t: p_("next", t), 1, KT)

                @block.tensor
                def _(pe):
                    ident = k_("ident")
                    for kind, j, s in L_ORDER:
                        if kind == "mm":
                            tile = LT_TILES[j]
                            kd_, i = tile
                            rH, rL = hH, hL
                            before = None
                            if s == 0:
                                if j:
                                    pe.wait_ge(low_done, j)
                                if j >= 2:
                                    pe.wait_ge(tile_stage, E.before(LT_TILES[j - 2], e_stages(LT_TILES[j - 2])[0]) + 1)
                                if tile == ("ya", 0):
                                    pe.wait_ge(scan_stage, B.end(HEADS - 1))
                                if tile == ("yb", 0):
                                    for o in range(2):
                                        pe.wait_ge(window_stage[o], C[o].end(SWQ - 2 + o))
                                if tile == ("wo", 0):
                                    pe.wait_ge(tile_stage, E.end(("yb", KT - 1)))
                                if kd_ == "f2" and i % 8 == 0:
                                    pe.wait_ge(tile_stage, E.end(("f1", i + 7)))
                                if tile == ("f1", 0):
                                    pe.wait_ge(tile_stage, E.end(("wo", KT - 1)))
                                    pe.matmul(ps[:, 7, :], k_("ones"), sq[:, 1, :], start=True, stop=True).then_inc(sum_done, 1)
                            if kd_ in ("ya", "wo"):
                                rH, rL = OH, OL
                            elif kd_ == "yb":
                                rH, rL = SH, SL
                            elif kd_ == "f2":
                                rH, rL = (OH, OL) if i // 8 % 2 == 0 else (SH, SL)
                            if tile == ("f1", 0):
                                def before(t):
                                    if t == 0:
                                        pe.wait_ge(post_root, 1)
                                    pe.wait_ge(h_low, t + 1)
                                    x_sum(pe, 0, t)
                            m = 16 if kd_ == "ab" else P
                            products(pe, j, s, ps[0:m, j % 2, :], rH, rL, KT, width=m, before=before)
                        elif kind == "G" and s in ("turn", "cumsum"):
                            pe.wait_ge(gate_stage, G.before(0, s))
                            if s == "turn":
                                pe.wait_ge(tile_stage, E.end(("ab", 0)))
                                for c in range(CH):
                                    ins = pe.transpose(psD[:, 0, c * 16:(c + 1) * 16], ab[0:16, c * P:(c + 1) * P], ident[0:16, 0:16])
                            else:
                                pe.matmul(psD[:, 0, 0:32], k_("upper"), gg, start=True, stop=True)
                                ins = pe.matmul(psD[:, 0, 32:64], k_("ones"), gg, start=True, stop=True)
                            ins.then_inc(gate_stage, 1)
                        elif kind == "D" and s in ("sums", "rows", "gram", "turnkv"):
                            h = j
                            pe.wait_ge(gram_stage, D.before(h, s))
                            q, k, vv, w = qs[h % 2][:, :], ks[h % 4][:, :], vs[h % 2][:, :], scal[:, h % 3]
                            if s == "rows" and h == 0:
                                pe.wait_ge(gate_stage, G.end(0))
                            for c in range(CH):
                                i, cc = c * HEADS + h, slice(c * P, (c + 1) * P)
                                if s == "sums":
                                    pe.matmul(psD[:, 0, c:c + 1], sq[:, 0, cc], k_("ones")[:, 0:1], start=True, stop=True)
                                    ins = pe.matmul(psD[:, 0, CH + c:CH + c + 1], sq[:, 1, cc], k_("ones")[:, 0:1], start=True, stop=True)
                                elif s == "rows":
                                    pe.matmul(psD[:, 0, cc], gg[:, i:i + 1].to_broadcast([P, P]), k_("upper"), start=True, stop=True)
                                    ins = pe.matmul(psD[:, 1, cc], w[:, 2, c:c + 1].to_broadcast([P, P]), ident, start=True, stop=True)
                                elif s == "gram":
                                    pe.matmul(psD[:, 0, cc], k[:, cc], kbeta[:, cc], start=True, stop=True)
                                    ins = pe.matmul(psD[:, 1, cc], k[:, cc], q[:, cc], start=True, stop=True)
                                else:
                                    pe.transpose(psD[:, 0, cc], k[:, cc], ident)
                                    ins = pe.transpose(psD[:, 1, cc], vv[:, cc], ident)
                            ins.then_inc(gram_stage, 1)
                        elif kind == "A" and s[:-1] in ("p", "q", "turn"):
                            h = j
                            pe.wait_ge(inverse_stage, A.before(h, s))
                            if s == "turni":
                                pe.wait_ge(gram_stage, D.end(h))
                            for c in range(CH):
                                cc = slice(c * P, (c + 1) * P)
                                if s.startswith("turn"):
                                    ins = pe.transpose(psA[:, 0, cc], XT[:, h % 3, c, :], ident)
                                elif s[0] == "p":
                                    ins = pe.matmul(psA[:, 0, cc], LTm[:, h % 2, c, :], Xi[:, c, :], start=True, stop=True)
                                else:
                                    b = LEVELS[int(s[-1])]
                                    ins = pe.matmul(second_half(psA[:, 1, cc], b), Pm[:, c, :], second_half(XT[:, h % 3, c, :], b),
                                                    start=True, stop=True)
                            ins.then_inc(inverse_stage, 1)
                        elif kind == "B" and (s[:-1] in ("v", "o", "r") or s in ("sums", "row")):
                            h = j
                            pe.wait_ge(scan_stage, B.before(h, s))
                            k = ks[h % 4][:, :]
                            c = int(s[-1]) if s[-1].isdigit() else 0
                            cc = slice(c * P, (c + 1) * P)
                            if s == "v0":
                                pe.wait_ge(inverse_stage, A.end(h))
                            if s in ("sums", "row"):
                                for c in range(CH):
                                    if s == "sums":
                                        ins = pe.matmul(psB[:, 0, c:c + 1], osq[:, c * P:(c + 1) * P], k_("ones")[:, 0:1], start=True, stop=True)
                                    else:
                                        ins = pe.matmul(psB[:, 0, c * P:(c + 1) * P], srow[:, 3, c:c + 1].to_broadcast([P, P]), ident,
                                                        start=True, stop=True)
                            elif s[0] == "r":
                                ins = pe.matmul(psB[:, 0, 2 * P:3 * P], k[:, cc], S[:, :], start=True, stop=True)
                            elif s[0] == "v":
                                ins = pe.matmul(psB[:, 0, 0:P], XT[:, h % 3, c, :], vb[:, h % 3, 0, :] if c == 0 else rr[:, :],
                                                start=True, stop=True)
                            else:
                                if c:
                                    pe.matmul(psB[:, 1, cc], S[:, :], qd[:, h % 3, c, :], start=True, stop=False)
                                ins = pe.matmul(psB[:, 1, cc], vn[:, :], AT[:, h % 3, c, :], start=(c == 0), stop=True)
                                if c < CH - 1:
                                    ins = pe.matmul(psB[:, 0, P:2 * P], kd[:, h % 3, c, :], vn[:, :], start=True, stop=True)
                            ins.then_inc(scan_stage, 1)
                        elif kind == "C":
                            t, o = j, j % 2
                            e = int(s[-1]) if s[-1].isdigit() else 0
                            rows = slice(HD * e, HD * (e + 1))
                            kv = t // (SWQ // 2)
                            w = s.rstrip("01")
                            if w not in ("rot", "score", "turn", "pv"):
                                continue
                            pe.wait_ge(window_stage[o], C[o].before(t, s))
                            prob, probT, qr, sc = probs[o], probTs[o], qrs[o], ps[:, 2 + 2 * o:4 + 2 * o, :]
                            if w == "rot":
                                if t < 2:
                                    pe.wait_ge(tile_stage, E.end(("swq", SWQ - 1)))
                                    pe.wait_ge(scan_stage, B.end(HEADS - 1))
                                ins = pe.matmul(ps[:, 6 + o, :], k_("rot"), qraw[:, t, :], start=True, stop=True)
                            elif w == "score":
                                for n in range(CH):
                                    qn = qr[rows, n * P:(n + 1) * P]
                                    bank, a = n // 2, (n % 2) * 2 * P
                                    if n == 0:
                                        ins = pe.matmul(sc[:, 0, P:2 * P], qn, kk[rows, kv, 0:P], start=True, stop=True)
                                    else:
                                        ins = pe.matmul(sc[:, bank, a:a + 2 * P], qn, kk[rows, kv, (n - 1) * P:(n + 1) * P],
                                                        start=True, stop=True)
                            elif w == "turn":
                                pT = sc.rearrange("p b (c n) -> p (b c) n", n=P)
                                for i in range(2 * CH - 1):
                                    n, half = (i + 1) // 2, (i + 1) % 2
                                    ins = pe.transpose(pT[:, i, :], prob[:, n, half * P:(half + 1) * P], ident)
                            else:
                                for n in range(CH):
                                    out = ps[rows, 6 + o, n * P:(n + 1) * P]
                                    for half in ((0, 1) if n else (1,)):
                                        i = 2 * n + half - 1
                                        ins = pe.matmul(out, vtok[:, n - 1 + half, HD * kv:HD * (kv + 1)], probT[:, i, :],
                                                        start=(half == 0 or n == 0), stop=(half == 1))
                            ins.then_inc(window_stage[o], 1)
                        elif kind == "E" and s in ("rotk", "dupk", "turnv"):
                            pe.wait_ge(tile_stage, E.before(j, s))
                            if s == "rotk":
                                pe.wait_ge(gram_stage, D.end(HEADS - 1))
                                ins = pe.matmul(psD[:, 0, :], k_("rot"), tmp[:, :], start=True, stop=True)
                            elif s == "dupk":
                                pe.matmul(psD[:, 0, :], k_("dup0"), kr, start=True, stop=True)
                                ins = pe.matmul(psD[:, 1, :], k_("dup1"), kr, start=True, stop=True)
                            else:
                                for c in range(CH):
                                    ins = pe.transpose(psD[:, 0, c * P:(c + 1) * P], tmp[:, c * P:(c + 1) * P], ident)
                            ins.then_inc(tile_stage, 1)
                    pe.wait_ge(tile_stage, E.end(LT_TILES[-1]))
                    pe.matmul(ps[:, 7, :], k_("ones"), sq[:, 1, :], start=True, stop=True).then_inc(sum_done, 1)
                    pe.wait_ge(post_root, 2)
                    for t in range(KT):
                        x_sum(pe, KT, t)
            clear_all()

        with nc.Block() as block:
            @block.sync
            def _(sp):
                load_weights(sp, lambda i: w2[i], 1)
                sp.dma_start(bmat[:, :, :, :].rearrange("p a b c -> p (a b c)"), smallb).then_inc(input_in, 16)
                for j in range(2, len(S_TILES)):
                    load_weights(sp, lambda i: w2[i], j)
                for t in range(KT):
                    sp.wait_ge(out_ready, t + 1)
                    sp.dma_start(outT[:, t, :], acc[:, t, :]).then_inc(out_done, 16)
                sp.wait_ge(out_done, 16 * KT)

            @block.gpsimd
            def _(pool):
                for kind, j, s in S_ORDER:
                    if kind == "split_low":
                        split_low(pool, j)
                    elif kind == "T":
                        pool.wait_ge(table_stage, T.before(j, s))
                        if s == "coscos" and j >= 2:
                            pool.wait_ge(state_stage, SS.before(j - 2, "state") + 1)
                        cc, ss, tt = turn_c[:, j % 2, :], turn_s[:, j % 2, :], turn_t[:, :]
                        grid = lambda ap: ap.rearrange("p (a b) -> p a b", b=TBL)
                        hi = lambda i: big[:, i, j, :].unsqueeze(2).to_broadcast([P, TBH, TBL])
                        lo = lambda i: turn_small[:, i, j, :].unsqueeze(1).to_broadcast([P, TBH, TBL])
                        if s == "coscos":
                            ins = pool.tensor_tensor(grid(cc), hi(0), lo(0), ALU.mult)
                        elif s == "sinsin":
                            ins = pool.tensor_tensor(grid(tt), hi(1), lo(1), ALU.mult)
                        elif s == "cos":
                            ins = pool.tensor_tensor(cc, cc, tt, ALU.subtract)
                        elif s == "cossin":
                            ins = pool.tensor_tensor(grid(ss), hi(0), lo(1), ALU.mult)
                        elif s == "sincos":
                            ins = pool.tensor_tensor(grid(tt), hi(1), lo(0), ALU.mult)
                        else:
                            ins = pool.tensor_tensor(ss, ss, tt, ALU.add)
                        ins.then_inc(table_stage, 1)
                    elif kind == "E" and j[0] == "ub" and s == "low":
                        pool.wait_ge(tile_stage, E2.before(j, s))
                        i = j[1]
                        pool.tensor_tensor(SL[:, SG + i, :], mixed[:, :], SH[:, SG + i, :].bitcast(F32),
                                           ALU.subtract).then_inc(tile_stage, 1)

            @block.scalar
            def _(act):
                act.activation(rstd[:, :], ps[:, 7, :], ACT.Sqrt, bias=k_("eps"), scale=1.0 / D_MODEL).then_inc(root_done, 1)
                for kind, j, s in S_ORDER:
                    if kind == "split_high":
                        split_high(act, j, S_OUT_AT[outputs_of(S_TILES[j - SPLIT])[-1]] + 1 if j >= SPLIT else 0)
                    elif kind == "S" and s in ("gelu", "highs"):
                        act.wait_ge(state_stage, SS.before(j, s))
                        if s == "gelu":
                            act.activation(u[:, j // 4, :], u[:, j // 4, :], ACT.Gelu_apprx_tanh).then_inc(state_stage, 1)
                        else:
                            act.wait_ge(tile_stage, E2.end(("bb", KT - 1)))
                            act.activation(SH[:, 0:SG, :], u[:, :, :], ACT.Copy).then_inc(state_stage, 1)
                    elif kind == "E" and s in ("tanh", "high", "square"):
                        kd_, i = j
                        act.wait_ge(tile_stage, E2.before(j, s))
                        if kd_ == "glu" and s == "tanh":
                            n = S_OUT_AT[j]
                            act.wait_ge(tile_done, n + 1)
                            ins = act.activation(tmp[:, :], ps[:, n % 2, :], ACT.Tanh, scale=0.5, bias=half_glu[:, i:i + 1])
                        elif s == "tanh" and kd_ in ("za", "zb"):
                            ins = act.activation(tmp[:, :], (za[:, i, :] if kd_ == "za" else zb[i][:, :]), ACT.Tanh, scale=0.5)
                        elif s == "tanh":
                            g = acc[:, i, :] if kd_ == "gb" else sga(i)
                            ins = act.activation(g, g, ACT.Tanh, scale=0.5)
                        elif s == "high":
                            dst, f = {"ub": (SH[:, (SG + i) % KT, :], 1.0), "pw": (SH[:, i, :], 0.5),
                                      "glu": (yaH[:, i % SG, :], 0.25), "ba": (OH[:, i, :], 0.5)}[kd_]
                            ins = act.activation(dst, mixed[:, :], ACT.Copy, scale=f)
                        else:
                            ins = act.activation(sq[:, 0, :], x[:, i, :], ACT.Square)
                        ins.then_inc(tile_stage, 1)
                root_scalar(act, sum_done, 1, rstdp[:, :], ps[:, 7, :], 1.0 / D_MODEL, "eps", post_root)

            @block.vector
            def _(v):
                v.wait_ge(root_done, 1)
                v.reciprocal(rstd[:, :], rstd[:, :]).then_inc(rstd_ready, 1)
                v.wait_ge(rstd_ready, 1)
                for kind, j, s in S_ORDER:
                    if kind == "S" and s not in ("input", "output", "gelu", "highs"):
                        v.wait_ge(state_stage, SS.before(j, s))
                        cc, ss = turn_c[:, j % 2, :], turn_s[:, j % 2, :]
                        mul = lambda o, a, b: v.tensor_tensor(o[:, :], a, b, ALU.mult)
                        if s == "turn":
                            v.wait_ge(table_stage, T.end(j))
                            mul(t1, cc, psA[:, 0, :])
                            mul(t2, ss, psA[:, 1, :])
                            mul(sr, cc, psA[:, 1, :])
                            ins = mul(si, ss, psA[:, 0, :])
                        elif s == "turned":
                            v.tensor_tensor(zr[:, :], t1[:, :], t2[:, :], ALU.add)
                            ins = v.tensor_tensor(zi[:, :], sr[:, :], si[:, :], ALU.subtract)
                        elif s == "scan":
                            decay = mag[:, j:j + 1].to_broadcast([P, SEQ])
                            v.tensor_tensor_scan(t1[:, :], decay, zr[:, :], 0.0, ALU.mult, ALU.add)
                            ins = v.tensor_tensor_scan(t2[:, :], decay, zi[:, :], 0.0, ALU.mult, ALU.add)
                        elif s == "back":
                            mul(zr, cc, t1[:, :])
                            mul(zi, ss, t2[:, :])
                            mul(sr, cc, t2[:, :])
                            ins = mul(si, ss, t1[:, :])
                        elif s == "state":
                            v.tensor_tensor(zr[:, :], zr[:, :], zi[:, :], ALU.subtract)
                            ins = v.tensor_tensor(sr[:, :], sr[:, :], si[:, :], ALU.add)
                        elif s == "skip":
                            c = j // 4
                            ins = v.scalar_tensor_tensor(out=u[:, c, :], in0=u[:, c, :], scalar=p2("d", c),
                                                         in1=ps[:, 4, :], op0=ALU.mult, op1=ALU.add)
                        else:
                            ins = v.tensor_tensor(SL[:, 0:SG, :], u[:, :, :], SH[:, 0:SG, :].bitcast(F32), ALU.subtract)
                        ins.then_inc(state_stage, 1)
                    elif kind == "E":
                        kd_, i = j
                        n = S_OUT_AT[j]
                        b = ps[:, n % 2, :]
                        if s in ("tanh", "high", "square") or (kd_ == "ub" and s == "low"):
                            continue
                        v.wait_ge(tile_stage, E2.before(j, s))
                        if s == e2_stages(j)[0]:
                            v.wait_ge(tile_done, n + 1)
                        if s in ("scale", "bias") and kd_ != "pw":
                            dst = {"ua": lambda: u[:, i, :], "za": lambda: za[:, i, :], "ub": lambda: tmp[:, :],
                                   "zb": lambda: zb[i][:, :], "gb": lambda: acc[:, i, :], "ga": lambda: sga(i)}[kd_]()
                            if s == "scale":
                                ins = v.tensor_tensor(dst, b, rstd[:, :], ALU.mult)
                            else:
                                ins = v.tensor_scalar(dst, dst, p2("b_in", IN2[kd_] + i), None, ALU.add)
                        elif s == "silu" and kd_ != "glu":
                            z = (za[:, i, :] if kd_ == "za" else zb[i][:, :])
                            ins = v.scalar_tensor_tensor(out=z, in0=tmp[:, :], scalar=1.0, in1=z, op0=ALU.add, op1=ALU.mult)
                        elif s.startswith("sum") and kd_ == "ub":
                            m = int(s[-1])
                            d = 2 ** m
                            src = tmp if m == 0 else sq[:, (m - 1) % 2, :]
                            dst = sq[:, m % 2, :]
                            v.tensor_copy(dst[:, 0:d], src[:, 0:d])
                            ins = v.tensor_tensor(dst[:, d:], src[:, d:SEQ], src[:, 0:SEQ - d], ALU.add)
                        elif s == "mean":
                            win = 2 ** (i + 1)
                            src = sq[:, i % 2, :]
                            v.scalar_tensor_tensor(out=mixed[:, :], in0=src, scalar=1.0 / win, in1=tmp[:, :],
                                                   op0=ALU.mult, op1=ALU.subtract)
                            ins = v.tensor_tensor(small[:, 32:32 + win], src[:, 0:win], k_("invcount")[:, 0:win], ALU.mult)
                        elif s == "early":
                            win = 2 ** (i + 1)
                            ins = v.tensor_tensor(mixed[:, 0:win], small[:, 32:32 + win], tmp[:, 0:win], ALU.subtract)
                        elif kd_ == "pw" and s == "scale":
                            ins = v.scalar_tensor_tensor(out=mixed[:, :], in0=b, scalar=p2("pool_scale", i), in1=zb[i][:, :],
                                                         op0=ALU.mult, op1=ALU.mult)
                        elif s == "low":
                            f, hi_, dst = {"pw": (0.5, SH[:, i, :], SL[:, i, :]), "glu": (0.25, yaH[:, i % SG, :], yaL[:, i % SG, :]),
                                           "ba": (0.5, OH[:, i, :], OL[:, i, :])}[kd_]
                            ins = v.scalar_tensor_tensor(out=dst, in0=mixed[:, :], scalar=f, in1=hi_.bitcast(F32),
                                                         op0=ALU.mult, op1=ALU.subtract)
                        elif s == "gate" and kd_ == "bb":
                            ins = v.scalar_tensor_tensor(out=acc[:, i, :], in0=acc[:, i, :], scalar=1.0, in1=b, op0=ALU.add, op1=ALU.mult)
                        elif s == "gate" and kd_ == "glu":
                            ins = v.scalar_tensor_tensor(out=tmp[:, :], in0=tmp[:, :], scalar=1.0, in1=u[:, i, :], op0=ALU.add, op1=ALU.mult)
                        elif s == "silu":
                            ins = v.tensor_tensor(mixed[:, :], tmp[:, :], za[:, i, :], ALU.mult)
                        elif s == "gate":
                            ins = v.scalar_tensor_tensor(out=mixed[:, :], in0=sga(i), scalar=1.0, in1=b, op0=ALU.add, op1=ALU.mult)
                        elif s == "add" and kd_ == "ba":
                            ins = v.tensor_tensor(mixed[:, :], mixed[:, :], acc[:, i, :], ALU.add)
                        elif s == "add":
                            ins = v.tensor_tensor(x[:, i, :], x[:, i, :], b, ALU.add)
                        elif s == "sum" and i == 0:
                            ins = v.tensor_copy(sq[:, 1, :], sq[:, 0, :])
                        else:
                            ins = v.tensor_tensor(sq[:, 1, :], sq[:, 1, :], sq[:, 0, :], ALU.add)
                        ins.then_inc(tile_stage, 1)
                v.wait_ge(post_root, 1)
                v.reciprocal(rstdp[:, :], rstdp[:, :]).then_inc(post_ready, 1)
                v.wait_ge(post_ready, 1)
                for t in range(KT):
                    v.scalar_tensor_tensor(out=acc[:, t, :], in0=x[:, t, :], scalar=p2("final", t), in1=rstdp[:, :],
                                           op0=ALU.mult, op1=ALU.mult).then_inc(out_ready, 1)

            @block.tensor
            def _(pe):
                for kind, j, s in S_ORDER:
                    if kind == "mm":
                        tile = S_TILES[j]
                        kd_, i = tile
                        outs = outputs_of(tile)
                        each = PARTS // len(outs)
                        o, part = outs[s // each], s % each
                        n = S_OUT_AT[o]
                        depth = S_DEPTH.get(kd_, KT)
                        if s == 0 and j:
                            pe.wait_ge(low_done, j)
                        if part == 0 and n >= 2:
                            pe.wait_ge(tile_stage, E2.before(S_OUT[n - 2], e2_stages(S_OUT[n - 2])[0]) + 1)
                        if s == 0:
                            if kd_ == "pw":
                                pe.wait_ge(tile_stage, E2.end(("ub", SG - 1)))
                            if tile == ("bb", 0):
                                pe.wait_ge(tile_stage, E2.end(("pw", SG - 1)))
                            if tile == ("glu", 0):
                                pe.wait_ge(state_stage, SS.end(ST - 1))
                            if tile == ("ba", 0):
                                pe.wait_ge(tile_stage, E2.end(("glu", SG - 1)))
                            if tile == ("wo", 0):
                                pe.wait_ge(tile_stage, E2.end(("ba", KT - 1)))
                        rH, rL = {"pw": lambda: (SH[:, SG + o[1]:, :], SL[:, SG + o[1]:, :]), "bb": lambda: (SH, SL),
                                  "glu": lambda: (SH, SL), "ba": lambda: (yaH, yaL),
                                  "wo": lambda: (OH, OL)}.get(kd_, lambda: (hH, hL))()
                        products(pe, j, part, ps[:, n % 2, :], rH, rL, depth, kt0=(s // each) * depth, parts=each)
                    elif kind == "S" and s in ("input", "output"):
                        pe.wait_ge(state_stage, SS.before(j, s))
                        c, r = j // 4, slice(32 * (j % 4), 32 * (j % 4 + 1))
                        if s == "input":
                            if j == 0:
                                pe.wait_ge(input_in, 16)
                                pe.wait_ge(root_done, 1)
                            if j % 4 == 0:
                                pe.wait_ge(tile_stage, E2.end(("ua", c)))
                            pe.matmul(psA[:, 0, :], bmat[r, 0, c, :], u[r, c, :], start=True, stop=True)
                            ins = pe.matmul(psA[:, 1, :], bmat[r, 1, c, :], u[r, c, :], start=True, stop=True)
                        else:
                            pe.matmul(ps[r, 4, :], cmat[:, 0, j, :], zr[:, :], start=True, stop=False)
                            ins = pe.matmul(ps[r, 4, :], cmat[:, 1, j, :], sr[:, :], start=False, stop=True)
                        ins.then_inc(state_stage, 1)
                pe.wait_ge(tile_stage, E2.end(("wo", KT - 1)))
                pe.matmul(ps[:, 7, :], k_("ones"), sq[:, 1, :], start=True, stop=True).then_inc(sum_done, 1)


RANGE_STEPS = 6


def range_reduce(v, link, out, ang, k, quarter):
    two_pi = 2 * np.pi
    p1 = 6.28125
    p2 = float(np.float32(0.00193500518798828125))
    p3 = float(np.float32(two_pi - p1 - p2))
    magic = 1.5 * 2.0 ** 23
    link(v.tensor_scalar(k, ang, 1.0 / two_pi, quarter, ALU.mult, ALU.add))
    link(v.tensor_scalar(k, k, magic, None, ALU.add))
    link(v.tensor_scalar(k, k, magic, None, ALU.subtract))
    link(v.scalar_tensor_tensor(out=out, in0=k, scalar=-p1, in1=ang, op0=ALU.mult, op1=ALU.add))
    link(v.scalar_tensor_tensor(out=out, in0=k, scalar=-p2, in1=out, op0=ALU.mult, op1=ALU.add))
    link(v.scalar_tensor_tensor(out=out, in0=k, scalar=-p3, in1=out, op0=ALU.mult, op1=ALU.add))


def kernel(**inputs):
    import concourse.bacc as bacc
    from concourse.bass_utils import run_bass_kernel_spmd

    a = {n: np.asarray(v) for n, v in inputs.items()}

    def tiles(w, depth=KT):
        n = w.shape[-1] // P
        return w.reshape(depth, P, n, P).transpose(2, 1, 0, 3).reshape(n, P, depth * P)

    def columns(g):
        return g.reshape(-1, P).T

    def every(g):
        return np.broadcast_to(g[None, :], (P, g.size))

    w1, params = [], []
    for l in range(DEPTH):
        wi = a["w_in"][l]
        o = np.cumsum([0, 1024, 1024, 1024, 1024, 16, 1024, 128, 128, 1024, 1024])
        t = {n: tiles(wi[:, o[i]:o[i + 1]]) for i, n in enumerate(("q", "k", "v", "z", None, "swq", "swk", "swv", "ga", "gb")) if n}
        ab = np.zeros((P, KT, P), np.float32)
        ab[:, :, 0:16] = wi[:, o[4]:o[5]].reshape(KT, P, 16).transpose(1, 0, 2)
        t["ab"] = ab.reshape(1, P, D_MODEL)
        t["ya"], t["yb"], t["wo"] = (tiles(a[n][l]) for n in ("w_up_dn", "w_up_sw", "w_o"))
        t["f1"] = tiles(a["w_ff1"][l])
        t["f2"] = np.concatenate([tiles(a["w_ff2"][l][c * D_MODEL:(c + 1) * D_MODEL]) for c in range(FFC)])
        w1 += [t[k][i] for k, i in LT_TILES]
        conv = a["dn_conv_w"][l].reshape(CONV, 3 * HEADS, P).transpose(2, 1, 0).reshape(P, -1)
        params.append(np.concatenate([columns(a[n][l]) for n in ("pre_mix_g", "post_mix_g", "pre_mlp_g", "post_mlp_g")]
                                     + [columns(a["pre_mix_g"][l + 1] if l + 1 < DEPTH else a["norm_g_2"][0])]
                                     + [conv, a["dn_norm_g"][l][:, None], every(a["dn_a_log"][l]),
                                        every(a["dn_dt_bias"][l]), every(a["sw_sinks"][l])], axis=1))
    w = a["w_in_2"][0]
    t = {k: tiles(w[:, P * i:P * (i + n)]) for k, i, n in (("ua", IN2["ua"], SG), ("za", IN2["za"], SG), ("ub", IN2["ub"], SG),
                                                           ("zb", IN2["zb"], SG), ("ga", IN2["ga"], KT), ("gb", IN2["gb"], KT))}

    def pairs(w):
        h = tiles(w, SG)
        return h.reshape(-1, 2, P, SG * P).transpose(0, 2, 1, 3).reshape(-1, P, 2 * SG * P)

    t["bb"], t["ba"], t["glu"] = pairs(a["w_branch_b_2"][0]), pairs(a["w_branch_a_2"][0]), pairs(a["ssm_w_glu_2"][0])
    t["pw"] = np.zeros((1, P, D_MODEL), np.float32)
    t["pw"][0, :, 0:SG * P] = a["pool_w_2"][0].transpose(1, 0, 2).reshape(P, SG * P)
    t["wo"] = tiles(a["w_out_2"][0])
    states = lambda v: v.reshape(ST, P).T
    log_dt = np.broadcast_to(a["ssm_log_dt_2"][0][:, None], (2 * ST, P // 2))
    params2 = np.concatenate([columns(a["final_norm_g_2"])]
                             + [columns(a[n][0]) for n in ("b_in_2", "ssm_d_2", "ssm_b_glu_2", "pool_scale_2")]
                             + [states(a["ssm_lam_re_2"][0]), states(a["ssm_lam_im_2"][0]), states(log_dt)], axis=1)
    smallb = np.zeros((2, P, SG, P), np.float32)
    smallc = np.zeros((2, P, ST, 32), np.float32)
    for i, (nb, ncm) in enumerate((("ssm_b_re_2", "ssm_c_re_2"), ("ssm_b_im_2", "ssm_c_im_2"))):
        for g in range(2 * ST):
            st, e = g // 2, g % 2
            row, col = 32 * (st % 4) + 16 * e, 64 * e
            smallb[i, row:row + 16, st // 4, col:col + 64] = a[nb][0, g].T
            smallc[i, col:col + 64, st, 16 * e:16 * e + 16] = a[ncm][0, g].T
    w2 = [t[k][i] for k, i in S_TILES]
    w1.append(w2[0])
    data = {
        "gain0": columns(a["pre_mix_g"][0]),
        "w0": w1[0],
        "w1": np.stack(w1[1:]).reshape(DEPTH, len(LT_TILES), P, D_MODEL),
        "w2": np.stack(w2[1:]),
        "params2": params2,
        "smallb": smallb.transpose(1, 0, 2, 3).reshape(P, -1),
        "smallc": smallc.transpose(1, 0, 2, 3).reshape(P, -1),
        "xT": a["x"][0].T.reshape(KT, P, SEQ).transpose(1, 0, 2),
        "pos": a["positions"].reshape(1, SEQ),
        "consts": constants(),
        "params": np.stack(params),
    }
    nc = bacc.Bacc("TRN2", target_bir_lowering=False, num_devices=1)
    data = {n: np.ascontiguousarray(v) for n, v in data.items()}
    aps = {n: nc.dram_tensor(n, v.shape, mybir.dt.from_np(v.dtype), kind="ExternalInput").ap() for n, v in data.items()}
    outT = nc.dram_tensor("outT", (P, KT, SEQ), F32, kind="ExternalOutput").ap()
    build(nc, aps["xT"], aps["pos"], aps["consts"], aps["gain0"], aps["params"], aps["w0"], aps["w1"], aps["w2"], aps["params2"],
          aps["smallb"], aps["smallc"], outT)
    r = run_bass_kernel_spmd(nc, [data], core_ids=[0])
    got = r.results[0]["outT"]
    return got.transpose(1, 0, 2).reshape(1, D_MODEL, SEQ).transpose(0, 2, 1)
```
